# Optimizing a Trainium2 kernel written in Bass

```python
import jax, jax.numpy as jnp
from jax import lax
import numpy as np

D_MODEL = 1024
BATCH = 1
SEQ = 1024
DEPTH = 1

ATT_HEADS = 16
ATT_KV_HEADS = 4
ATT_HEAD_DIM = 64
ATT_WINDOW = 128
ATT_BLOCK = 128
ROPE_THETA = 10000.0
MLSTM_HEADS = 4
MLSTM_V_DIM = D_MODEL // MLSTM_HEADS
MLSTM_QK_DIM = MLSTM_V_DIM // 2
MLSTM_CHUNK = 128
MLSTM_CONV = 4
D_FF = 2816
RMS_EPS = 1e-5

ATT_Q_W = ATT_HEADS * ATT_HEAD_DIM
ATT_KV_W = ATT_KV_HEADS * ATT_HEAD_DIM
ML_QK_W = MLSTM_HEADS * MLSTM_QK_DIM
ML_V_W = MLSTM_HEADS * MLSTM_V_DIM
SPLITS = (ATT_Q_W, ATT_KV_W, ATT_KV_W, ML_QK_W, ML_QK_W, ML_V_W, ML_V_W,
          MLSTM_HEADS, MLSTM_HEADS, D_MODEL, D_MODEL)
IN_PROJ_W = sum(SPLITS)

kernel_name = "hybrid_swa_sink_mlstm_macaron"

def rms_norm(x, g):
    xf = x.astype(jnp.float32)
    y = xf * lax.rsqrt(jnp.mean(xf * xf, axis=-1, keepdims=True) + RMS_EPS)
    return (y * g.astype(jnp.float32)).astype(x.dtype)

def swiglu(h, w_gate, w_up, w_down):
    return (jax.nn.silu(h @ w_gate) * (h @ w_up)) @ w_down

def rope(x):
    half = x.shape[-1] // 2
    pos = jnp.arange(x.shape[1], dtype=jnp.float32)
    inv_freq = ROPE_THETA ** (-jnp.arange(half, dtype=jnp.float32) / half)
    ang = pos[:, None] * inv_freq[None, :]
    cos = jnp.cos(ang)[None, :, None, :]
    sin = jnp.sin(ang)[None, :, None, :]
    xf = x.astype(jnp.float32)
    x1, x2 = xf[..., :half], xf[..., half:]
    return jnp.concatenate([x1 * cos - x2 * sin, x2 * cos + x1 * sin], axis=-1).astype(x.dtype)

def sliding_window_attention(q, k, v, sinks):
    B, S = q.shape[0], q.shape[1]
    nb = S // ATT_BLOCK
    G = ATT_HEADS // ATT_KV_HEADS
    qb = q.reshape(B, nb, ATT_BLOCK, ATT_KV_HEADS, G, ATT_HEAD_DIM)

    def with_prev(t):
        tb = t.reshape(B, nb, ATT_BLOCK, ATT_KV_HEADS, ATT_HEAD_DIM)
        prev = jnp.pad(tb[:, :-1], ((0, 0), (1, 0), (0, 0), (0, 0), (0, 0)))
        return jnp.concatenate([prev, tb], axis=2)

    kb, vb = with_prev(k), with_prev(v)
    scores = jnp.einsum('bnqhgd,bnkhd->bnhgqk', qb, kb,
                        preferred_element_type=jnp.float32) * (ATT_HEAD_DIM ** -0.5)
    qi = jnp.arange(ATT_BLOCK)[:, None]
    kj = jnp.arange(2 * ATT_BLOCK)[None, :]
    rel = qi + ATT_BLOCK - kj
    band = (rel >= 0) & (rel < ATT_WINDOW)
    key_pos = jnp.arange(nb)[:, None, None] * ATT_BLOCK + kj[None] - ATT_BLOCK
    mask = band[None] & (key_pos >= 0)
    scores = jnp.where(mask[None, :, None, None], scores, -jnp.inf)
    sink = sinks.astype(jnp.float32).reshape(ATT_KV_HEADS, G)[None, None, :, :, None, None]
    m = jnp.maximum(scores.max(axis=-1, keepdims=True), sink)
    p = jnp.exp(scores - m)
    denom = p.sum(axis=-1, keepdims=True) + jnp.exp(sink - m)
    p = (p / denom).astype(v.dtype)
    out = jnp.einsum('bnhgqk,bnkhd->bnqhgd', p, vb)
    return out.reshape(B, S, ATT_Q_W)

def causal_depthwise_conv(x, w, b):
    K, C = w.shape
    y = lax.conv_general_dilated(x, w[:, None, :].astype(x.dtype), window_strides=(1,),
                                 padding=[(K - 1, 0)],
                                 dimension_numbers=('NWC', 'WIO', 'NWC'),
                                 feature_group_count=C)
    return y + b

def mlstm_chunkwise(q, k, v, i_pre, f_pre):
    B, S, H, Dk = q.shape
    Dv = v.shape[-1]
    L = MLSTM_CHUNK
    nc = S // L
    f32 = jnp.float32

    def chunks(t):
        return jnp.moveaxis(t.astype(f32).reshape(B, nc, L, H, -1), 3, 1)

    qc = chunks(q)
    kc = chunks(k) * (Dk ** -0.5)
    vc = chunks(v)
    ig = jnp.moveaxis(i_pre.astype(f32).reshape(B, nc, L, H), 3, 1)
    logf = jax.nn.log_sigmoid(jnp.moveaxis(f_pre.astype(f32).reshape(B, nc, L, H), 3, 1))
    b = jnp.cumsum(logf, axis=-1)
    b_end = b[..., -1]

    w_end = b_end[..., None] - b + ig
    m_loc = w_end.max(axis=-1)
    a = jnp.exp(w_end - m_loc[..., None])
    dC = jnp.einsum('bhclv,bhcld->bhcvd', a[..., None] * vc, kc)
    dn = jnp.einsum('bhcl,bhcld->bhcd', a, kc)

    def step(carry, inp):
        C, n, m = carry
        dC_c, dn_c, m_loc_c, b_end_c = inp
        m_new = jnp.maximum(b_end_c + m, m_loc_c)
        s_old = jnp.exp(b_end_c + m - m_new)
        s_new = jnp.exp(m_loc_c - m_new)
        C_new = s_old[..., None, None] * C + s_new[..., None, None] * dC_c
        n_new = s_old[..., None] * n + s_new[..., None] * dn_c
        return (C_new, n_new, m_new), (C, n, m)

    init = (jnp.zeros((B, H, Dv, Dk), f32), jnp.zeros((B, H, Dk), f32), jnp.zeros((B, H), f32))
    xs = (jnp.moveaxis(dC, 2, 0), jnp.moveaxis(dn, 2, 0),
          jnp.moveaxis(m_loc, 2, 0), jnp.moveaxis(b_end, 2, 0))
    _, (C_prev, n_prev, m_prev) = lax.scan(step, init, xs)
    C_prev = jnp.moveaxis(C_prev, 0, 2)
    n_prev = jnp.moveaxis(n_prev, 0, 2)
    m_prev = jnp.moveaxis(m_prev, 0, 2)

    causal = jnp.tril(jnp.ones((L, L), dtype=bool))
    log_d = jnp.where(causal, b[..., :, None] - b[..., None, :] + ig[..., None, :], -jnp.inf)
    log_inter = b + m_prev[..., None]
    m_t = jnp.maximum(log_d.max(axis=-1), log_inter)
    s = jnp.einsum('bhcld,bhcsd->bhcls', qc, kc) * jnp.exp(log_d - m_t[..., None])
    inter = jnp.exp(log_inter - m_t)
    num = (jnp.einsum('bhcls,bhcsv->bhclv', s, vc)
           + inter[..., None] * jnp.einsum('bhcld,bhcvd->bhclv', qc, C_prev))
    den = s.sum(axis=-1) + inter * jnp.einsum('bhcld,bhcd->bhcl', qc, n_prev)
    h = num / jnp.maximum(jnp.abs(den), jnp.exp(-m_t))[..., None]
    return jnp.moveaxis(h, 1, 3).reshape(B, S, H * Dv).astype(q.dtype)

def hybrid_mixer(h, w_in, b_i, b_f, attn_sinks, conv_w, conv_b, head_norm,
                 w_att, w_mlstm, w_out):
    B, S, _ = h.shape
    z = h @ w_in
    idx = np.cumsum(SPLITS)[:-1].tolist()
    q_a, k_a, v_a, q_m, k_m, v_m, o_m, i_m, f_m, g_a, g_m = jnp.split(z, idx, axis=-1)

    q_a = rope(q_a.reshape(B, S, ATT_HEADS, ATT_HEAD_DIM))
    k_a = rope(k_a.reshape(B, S, ATT_KV_HEADS, ATT_HEAD_DIM))
    v_a = v_a.reshape(B, S, ATT_KV_HEADS, ATT_HEAD_DIM)
    y_a = sliding_window_attention(q_a, k_a, v_a, attn_sinks) @ w_att

    qk = jax.nn.silu(causal_depthwise_conv(jnp.concatenate([q_m, k_m], axis=-1), conv_w, conv_b))
    q_m, k_m = qk[..., :ML_QK_W], qk[..., ML_QK_W:]
    h_m = mlstm_chunkwise(q_m.reshape(B, S, MLSTM_HEADS, MLSTM_QK_DIM),
                          k_m.reshape(B, S, MLSTM_HEADS, MLSTM_QK_DIM),
                          v_m.reshape(B, S, MLSTM_HEADS, MLSTM_V_DIM),
                          i_m + b_i, f_m + b_f)
    h_m = rms_norm(h_m.reshape(B, S, MLSTM_HEADS, MLSTM_V_DIM),
                   head_norm.reshape(MLSTM_HEADS, MLSTM_V_DIM)).reshape(B, S, ML_V_W)
    y_m = (jax.nn.sigmoid(o_m) * h_m) @ w_mlstm

    y = jax.nn.sigmoid(g_a) * y_a + jax.nn.sigmoid(g_m) * y_m
    return y @ w_out

def setup_inputs(seed: int = 0) -> dict:
    key = jax.random.key(seed)
    ks = jax.random.split(key, 24)
    f32 = jnp.float32

    def nrm(k, shape, scale):
        return jax.random.normal(k, shape, f32) * scale

    def gain(k, shape):
        return 1.0 + 0.02 * jax.random.normal(k, shape, f32)

    L = DEPTH
    return {
        "x": jax.random.normal(ks[0], (BATCH, SEQ, D_MODEL), f32),
        "ffn1_norm": gain(ks[1], (L, D_MODEL)),
        "ffn1_w_gate": nrm(ks[2], (L, D_MODEL, D_FF), D_MODEL ** -0.5),
        "ffn1_w_up": nrm(ks[3], (L, D_MODEL, D_FF), D_MODEL ** -0.5),
        "ffn1_w_down": nrm(ks[4], (L, D_FF, D_MODEL), D_FF ** -0.5),
        "mix_norm": gain(ks[5], (L, D_MODEL)),
        "w_in": nrm(ks[6], (L, D_MODEL, IN_PROJ_W), D_MODEL ** -0.5),
        "b_i": nrm(ks[7], (L, MLSTM_HEADS), 0.1),
        "b_f": jnp.linspace(3.0, 6.0, MLSTM_HEADS, dtype=f32)[None, :] + nrm(ks[8], (L, MLSTM_HEADS), 0.1),
        "attn_sinks": nrm(ks[9], (L, ATT_HEADS), 1.0),
        "conv_w": nrm(ks[10], (L, MLSTM_CONV, 2 * ML_QK_W), MLSTM_CONV ** -0.5),
        "conv_b": nrm(ks[11], (L, 2 * ML_QK_W), 0.01),
        "head_norm": gain(ks[12], (L, ML_V_W)),
        "w_att": nrm(ks[13], (L, ATT_Q_W, D_MODEL), ATT_Q_W ** -0.5),
        "w_mlstm": nrm(ks[14], (L, ML_V_W, D_MODEL), ML_V_W ** -0.5),
        "w_out": nrm(ks[15], (L, D_MODEL, D_MODEL), D_MODEL ** -0.5),
        "ffn2_norm": gain(ks[16], (L, D_MODEL)),
        "ffn2_w_gate": nrm(ks[17], (L, D_MODEL, D_FF), D_MODEL ** -0.5),
        "ffn2_w_up": nrm(ks[18], (L, D_MODEL, D_FF), D_MODEL ** -0.5),
        "ffn2_w_down": nrm(ks[19], (L, D_FF, D_MODEL), D_FF ** -0.5),
        "final_norm": gain(ks[20], (D_MODEL,)),
    }

def reference(x, ffn1_norm, ffn1_w_gate, ffn1_w_up, ffn1_w_down, mix_norm, w_in, b_i, b_f,
              attn_sinks, conv_w, conv_b, head_norm, w_att, w_mlstm, w_out,
              ffn2_norm, ffn2_w_gate, ffn2_w_up, ffn2_w_down, final_norm):
    for l in range(DEPTH):
        x = x + 0.5 * swiglu(rms_norm(x, ffn1_norm[l]), ffn1_w_gate[l], ffn1_w_up[l], ffn1_w_down[l])
        x = x + hybrid_mixer(rms_norm(x, mix_norm[l]), w_in[l], b_i[l], b_f[l], attn_sinks[l],
                             conv_w[l], conv_b[l], head_norm[l], w_att[l], w_mlstm[l], w_out[l])
        x = x + 0.5 * swiglu(rms_norm(x, ffn2_norm[l]), ffn2_w_gate[l], ffn2_w_up[l], ffn2_w_down[l])
    return rms_norm(x, final_norm)


_drawn_inputs = setup_inputs


def setup_inputs(seed=0):
    import zlib

    import numpy as np

    out = dict(_drawn_inputs(seed))
    spreads = {}
    factors = {'ffn1_norm': 5.741,
     'mix_norm': 5.124,
     'b_i': 64.0,
     'attn_sinks': 64.0,
     'conv_b': 64.0,
     'head_norm': 176.139,
     'ffn2_norm': 27.091,
     'final_norm': 25.673}
    for name, (base, spread) in spreads.items():
        noise = np.random.default_rng([zlib.crc32(name.encode()), seed]).standard_normal(out[name].shape)
        drawn = base * np.exp(spread * noise) if base else spread * noise
        out[name] = __import__('jax').numpy.asarray(drawn.astype(out[name].dtype))
    for name, factor in factors.items():
        out[name] = (out[name] * factor).astype(out[name].dtype)
    return out
```

```python
from contextlib import ExitStack

import numpy as np

import concourse.bass as bass
from concourse import mybir
from concourse.alu_op_type import AluOpType as ALU

ACT = mybir.ActivationFunctionType
F32 = mybir.dt.float32
F32R = mybir.dt.float32r

P = 128
D = 1024
S = 1024
KT = D // P
HALF = 512
F = 2816
FT = F // P
PAIRS = FT // 2
EPS = 1e-5

FFN_UNITS = 3 * FT

C_GAIN = 0
C_EPS = 32
C_HN = 33
C_BI, C_BF = 41, 42
C_CONV = 43
N_COLS = C_CONV + 5 * 8

HEADS, KV_HEADS, HD = 16, 4, 64
GROUP = HEADS // KV_HEADS
MH = 4
DV = D // MH
DK = DV // 2
NA = DV + 1
NB = S // P
BIG = 1e30

N_ROPE, N_RAW, N_CONV = 10, 18, 8
Z_TILES = N_ROPE + N_RAW + N_CONV
PROJ_UNITS = 1 + Z_TILES
U_PROJ = FFN_UNITS
U_BLK = U_PROJ + PROJ_UNITS
U_MERGE = U_BLK + 2 * NB
U_FFN2 = U_MERGE + 3 * KT
M_PROJ = 2 * FT
M_BLK = M_PROJ + PROJ_UNITS
M_MERGE = M_BLK + 2 * NB
M_FFN2 = M_MERGE + 3 * KT


class Lin:
    def __init__(self, reg, m=1, a=0):
        self.reg, self.m, self.a = reg, m, a

    def __mul__(self, k):
        return Lin(self.reg, self.m * k, self.a * k)

    def __add__(self, k):
        return Lin(self.reg, self.m, self.a + k)

    __radd__ = __add__

    def __sub__(self, k):
        return self + -k


def val(v):
    return v.reg * v.m + v.a if isinstance(v, Lin) else v


def hybrid_layer(nc, w_stream, x_t, cols, ident_d, sinks, rope_cs, masks, mask_big, sel_head, sel_last,
                 out, zs, gs, att_s, mem_s, x_s):
    with ExitStack() as ctx:
        e = ctx.enter_context
        base = [(nc.sbuf_base + 31) // 32 * 32]

        def at(name, shape, dt, offset):
            return nc.alloc_sbuf_tensor_at(name, shape, dt, offset=offset)

        def sb(name, shape, dt):
            t = at(name, shape, dt, base[0])
            size = 4
            for n in shape[1:]:
                size *= n
            base[0] += (size + 31) // 32 * 32
            return t

        x = sb("x", [P, KT, S], F32)
        ra_hi = sb("ra_hi", [P, KT, S], F32R)
        ra_lo = sb("ra_lo", [P, KT, S], F32R)
        rb_base = base[0]
        rb_hi = sb("rb_hi", [P, KT, S], F32R)
        rb_lo = sb("rb_lo", [P, KT, S], F32R)
        w_raw = [sb(f"w_raw{i}", [P, D], F32) for i in range(2)]
        w_hi = [sb(f"w_hi{i}", [P, D], F32R) for i in range(2)]
        w_lo = [sb(f"w_lo{i}", [P, D], F32R) for i in range(2)]
        rstd_b = sb("rstd_b", [P, S], F32)
        t_a = sb("t_a", [P, S], F32)
        t_b = sb("t_b", [P, S], F32)
        sq = sb("sq", [P, S], F32)
        sqacc = sb("sqacc", [P, S], F32)
        col = sb("col", [P, N_COLS], F32)
        ident = sb("ident", [P, P], F32)
        ones = sb("ones", [P, 1], F32)
        root = sb("root", [P, KT], F32)
        ssv = sb("ssv", [P, KT], F32)
        rstd_c = sb("rstd_c", [P, KT], F32)
        assert base[0] <= nc.sbuf_usable_end

        ps = [e(nc.psum_tensor(f"ps{i}", [P, S], F32)) for i in range(4)]

        def sem(name):
            return e(nc.semaphore(name))

        s_const = sem("s_const")
        s_x = [sem(f"s_x{i}") for i in range(4)]
        s_ones = sem("s_ones")
        s_w = [sem(f"s_w{i}") for i in range(2)]
        s_whi = sem("s_whi")
        s_wlo = sem("s_wlo")
        s_unit = sem("s_unit")
        s_gs = sem("s_gs")
        s_silu = sem("s_silu")
        s_us = sem("s_us")
        s_h = sem("s_h")
        s_hhi = sem("s_hhi")
        s_hlo = sem("s_hlo")
        s_down = sem("s_down")
        s_xadd = sem("s_xadd")
        s_ahi = sem("s_ahi")
        s_alo = sem("s_alo")
        s_sq = sem("s_sq")
        s_acc = sem("s_acc")
        s_ss = sem("s_ss")
        s_root = sem("s_root")
        s_nr = sem("s_nr")
        s_rc = sem("s_rc")
        s_rbc = sem("s_rbc")
        s_rb = sem("s_rb")
        s_out = sem("s_out")
        s_fin = sem("s_fin")

        def load_unit(sp, n, slot, first=False):
            if not first:
                sp.wait_ge(s_wlo, val(n - 1))
            sp.dma_start(w_raw[slot][:], w_stream[val(n)]).then_inc(s_w[slot], 16)

        def load_units(sp, start, count):
            with sp.Fori(0, count // 2) as reg:
                i = Lin(reg)
                for j in range(2):
                    load_unit(sp, i * 2 + (start + j), (start + j) % 2)
            if count % 2:
                load_unit(sp, start + count - 1, (start + count - 1) % 2)

        def split_hi(act, n, slot, done=None):
            act.wait_ge(s_w[slot], val((n - slot) * 8 + 16 if isinstance(n, int) else n * 8 + (16 - 8 * slot)))
            if done is not None:
                act.wait_ge(done[0], val(done[1]))
            nc.scalar.copy(w_hi[slot][:], w_raw[slot][:]).then_inc(s_whi, 1)

        def split_lo(dve, n, slot):
            dve.wait_ge(s_whi, val(n + 1))
            nc.vector.tensor_tensor(w_lo[slot][:], w_raw[slot][:], w_hi[slot][:].bitcast(F32),
                                    ALU.subtract).then_inc(s_wlo, 1)

        def products(pe, out_ps, slot, hi, lo, k_wait=None, ks=(0, KT)):
            for k in range(*ks):
                if k_wait is not None:
                    pe.wait_ge(k_wait[0], val(k_wait[1] + k + 1))
                w = slice(k * P, (k + 1) * P)
                for i, (wt, a) in enumerate(((w_hi, hi), (w_hi, lo), (w_lo, hi))):
                    for t in range(2):
                        mm = nc.tensor.matmul(out_ps[:, t * HALF:(t + 1) * HALF], wt[slot][:, w],
                                              a[:, k, t * HALF:(t + 1) * HALF],
                                              start=(k == 0 and i == 0), stop=(k == KT - 1 and i == 2))
            if ks[1] == KT:
                mm.then_inc(s_unit, 1)

        def pe_stats(pe, norm):
            pe.wait_ge(s_acc, val(KT * (norm + 1)))
            for j in range(KT):
                mm = nc.tensor.matmul(ps[2][:, j:j + 1], sqacc[:, j * P:(j + 1) * P], ones[:],
                                      start=(j == 0), stop=True, skip_group_check=True)
            mm.then_inc(s_ss, 1)
            pe.wait_ge(s_rc, val(norm + 1))
            for j in range(KT):
                mm = nc.tensor.matmul(ps[3][:, j * P:(j + 1) * P],
                                      rstd_c[:, j:j + 1].to_broadcast([P, P]), ident[:],
                                      start=(j % 4 == 0), stop=True, skip_group_check=True)
            mm.then_inc(s_rbc, 1)

        def act_norm_tile(act, norm, d, hi, ready):
            act.wait_ge(ready[0], ready[1])
            if d > 0 or norm > 0:
                act.wait_ge(s_acc, val(KT * norm + d))
            nc.scalar.activation(sq[:], x[:, d, :], ACT.Square).then_inc(s_sq, 1)
            if hi is not None:
                g = C_GAIN + norm * KT + d
                nc.scalar.activation(hi[:, d, :], x[:, d, :], ACT.Copy,
                                     scale=col[:, g:g + 1]).then_inc(s_ahi, 1)

        def act_stats(act, norm):
            act.wait_ge(s_ss, val(norm + 1))
            nc.scalar.activation(root[:], ps[2][:, 0:KT], ACT.Sqrt, bias=col[:, C_EPS:C_EPS + 1],
                                 scale=1.0 / D).then_inc(s_root, 1)
            act.wait_ge(s_rbc, val(norm + 1))
            nc.scalar.copy(rstd_b[:], ps[3][:]).then_inc(s_rb, 1)

        def dve_norm_tile(dve, norm, d, hi, lo):
            g = C_GAIN + norm * KT + d
            dve.wait_ge(s_ahi, val(KT * norm + d + 1))
            nc.vector.scalar_tensor_tensor(lo[:, d, :], x[:, d, :], col[:, g:g + 1],
                                           hi[:, d, :].bitcast(F32), ALU.mult,
                                           ALU.subtract).then_inc(s_alo, 1)

        def dve_stats(dve, norm):
            dve.wait_ge(s_root, val(norm + 1))
            nc.vector.reciprocal(rstd_c[:], root[:]).then_inc(s_nr, 1)
            nc.vector.tensor_scalar(ssv[:], ps[2][:, 0:KT], 1.0 / D, EPS, ALU.mult, ALU.add).then_inc(s_nr, 1)
            dve.wait_ge(s_nr, 5 * norm + 2)
            nc.vector.tensor_tensor(ssv[:], ssv[:], rstd_c[:], ALU.mult).then_inc(s_nr, 1)
            dve.wait_ge(s_nr, 5 * norm + 3)
            nc.vector.tensor_tensor(ssv[:], ssv[:], rstd_c[:], ALU.mult).then_inc(s_nr, 1)
            dve.wait_ge(s_nr, 5 * norm + 4)
            nc.vector.tensor_scalar(ssv[:], ssv[:], -0.5, 1.5, ALU.mult, ALU.add).then_inc(s_nr, 1)
            dve.wait_ge(s_nr, 5 * norm + 5)
            nc.vector.tensor_tensor(rstd_c[:], rstd_c[:], ssv[:], ALU.mult).then_inc(s_rc, 1)

        def pool_norm(pool, norm):
            for d in range(KT):
                pool.wait_ge(s_sq, val(KT * norm + d + 1))
                if d == 0:
                    if norm > 0:
                        pool.wait_ge(s_ss, val(norm))
                    nc.gpsimd.tensor_copy(sqacc[:], sq[:]).then_inc(s_acc, 1)
                else:
                    pool.wait_ge(s_acc, val(KT * norm + d))
                    nc.gpsimd.tensor_tensor(sqacc[:], sqacc[:], sq[:], ALU.add).then_inc(s_acc, 1)

        class Ffn:
            def __init__(self, index, unit0, m0, norm, act, hidden):
                self.unit0, self.m0, self.norm = unit0, m0, norm
                self.hi, self.lo = act
                self.h_hi, self.h_lo = hidden
                self.f0 = FT * index
                self.a0 = PAIRS * KT * index

            def slot(self, n):
                return (self.unit0 + n) % 2

        def pe_down(pe, o, n, slot, p, par, half, first=False):
            pe.wait_ge(s_wlo, val(n + 1))
            pe.wait_ge(s_hlo, val(p * 2 + (o.f0 + 2)))
            for dd in range(4):
                d_ps = ps[2 + dd % 2]
                if not (first and dd < 2):
                    pe.wait_ge(s_xadd, val(p * KT + (o.a0 + 4 * half + dd - 1)))
                for j in range(2):
                    w = slice(j * HALF + dd * P, j * HALF + (dd + 1) * P)
                    for i, (wt, h) in enumerate(((w_hi, o.h_hi), (w_hi, o.h_lo), (w_lo, o.h_hi))):
                        for t in range(2):
                            mm = nc.tensor.matmul(d_ps[:, t * HALF:(t + 1) * HALF], wt[slot][:, w],
                                                  h[:, 2 * par + j, t * HALF:(t + 1) * HALF],
                                                  start=(j == 0 and i == 0), stop=(j == 1 and i == 2))
                mm.then_inc(s_down, 1)

        def pe_ffn(pe, o):
            for n in range(4):
                pe.wait_ge(s_wlo, val(o.unit0 + n + 1))
                if o.norm == 2 and n < 2:
                    pe.wait_ge(s_xfin, KT - 1 + n)
                if n == 2:
                    pe.wait_ge(s_root, val(o.norm + 1))
                if n == 3:
                    pe.wait_ge(s_rb, val(o.norm + 1))
                products(pe, ps[n], o.slot(n), o.hi, o.lo, k_wait=(s_alo, KT * o.norm) if n == 0 else None)
                if n == 0:
                    pe_stats(pe, o.norm)

            def pair(n, p, par, first=False):
                for j in range(2):
                    pe.wait_ge(s_wlo, val(n + (3 * j + 1)))
                    pe.wait_ge(s_gs, val(p * 2 + (o.f0 + j)))
                    products(pe, ps[0], o.slot(j), o.hi, o.lo)
                    pe.wait_ge(s_wlo, val(n + (3 * j + 2)))
                    pe.wait_ge(s_us, val(p * 2 + (o.f0 + j)))
                    products(pe, ps[1], o.slot(j + 1), o.hi, o.lo)
                    pe_down(pe, o, n + (3 * j + 2), o.slot(j), p - 1, 1 - par, j, first and j == 0)

            pair(o.unit0 + 4, 1, 1, first=True)
            pair(o.unit0 + 10, 2, 0)
            with pe.Fori(0, (PAIRS - 3) // 2) as reg:
                i = Lin(reg)
                for j in range(2):
                    pair(i * 12 + (o.unit0 + 16 + 6 * j), i * 2 + (3 + j), 1 - j)
            for half in range(2):
                pe_down(pe, o, o.unit0 + FFN_UNITS - 2 + half, o.slot(half), PAIRS - 1, 0, half)

        def act_silu(act, o, f):
            act.wait_ge(s_gs, val(f + (o.f0 + 1)))
            nc.scalar.activation(t_a[:], t_a[:], ACT.Silu).then_inc(s_silu, 1)

        def act_hhi(act, o, f, hslot):
            act.wait_ge(s_h, val(f + (o.f0 + 1)))
            nc.scalar.copy(o.h_hi[:, hslot, :], t_b[:]).then_inc(s_hhi, 1)

        def act_ffn(act, o, tail):
            for n in range(4):
                split_hi(act, o.unit0 + n + 2, o.slot(n), (s_unit, o.m0 + n + 1))
                if n == 0:
                    act_stats(act, o.norm)
                if n % 2 == 0:
                    act_silu(act, o, n // 2)
                else:
                    act_hhi(act, o, n // 2, n // 2)

            def pair(n, p, par, last=False):
                for j in range(2):
                    f = p * 2 + j
                    split_hi(act, n + (3 * j + 2), o.slot(j), (s_unit, p * 4 + (o.m0 + 2 * j + 1)))
                    act_silu(act, o, f)
                    split_hi(act, n + (3 * j + 3), o.slot(j + 1), (s_unit, p * 4 + (o.m0 + 2 * j + 2)))
                    act_hhi(act, o, f, 2 * par + j)
                    if not (last and j == 1):
                        split_hi(act, n + (3 * j + 4), o.slot(j), (s_down, p * KT + (o.a0 + 4 * j - 4)))

            pair(o.unit0 + 4, 1, 1)
            pair(o.unit0 + 10, 2, 0)
            with act.Fori(0, (PAIRS - 3) // 2) as reg:
                i = Lin(reg)
                for j in range(2):
                    pair(i * 12 + (o.unit0 + 16 + 6 * j), i * 2 + (3 + j), 1 - j)
            tail(act)

        def dve_gs(dve, o, f, src, wait):
            if wait:
                dve.wait_ge(s_h, val(f + o.f0))
            nc.vector.tensor_tensor(t_a[:], src[:], rstd_b[:], ALU.mult).then_inc(s_gs, 1)

        def dve_us(dve, o, f, src, wait):
            if wait:
                dve.wait_ge(s_hlo, val(f + o.f0))
            nc.vector.tensor_tensor(t_b[:], src[:], rstd_b[:], ALU.mult).then_inc(s_us, 1)
            dve.wait_ge(s_silu, val(f + (o.f0 + 1)))
            dve.wait_ge(s_us, val(f + (o.f0 + 1)))
            nc.vector.tensor_tensor(t_b[:], t_b[:], t_a[:], ALU.mult).then_inc(s_h, 1)

        def dve_hlo(dve, o, f, hslot):
            dve.wait_ge(s_hhi, val(f + (o.f0 + 1)))
            nc.vector.tensor_tensor(o.h_lo[:, hslot, :], t_b[:], o.h_hi[:, hslot, :].bitcast(F32),
                                    ALU.subtract).then_inc(s_hlo, 1)

        def dve_xadd(dve, o, p, d):
            dve.wait_ge(s_down, val(p * KT + (o.a0 + d + 1)))
            dve.wait_ge(s_xadd, val(p * KT + (o.a0 + d - 7) if not isinstance(p, int) or p else o.a0))
            nc.vector.scalar_tensor_tensor(x[:, d, :], ps[2 + d % 2][:], 0.5, x[:, d, :],
                                           ALU.mult, ALU.add).then_inc(s_xadd, 1)

        def dve_ffn(dve, o, tail):
            if o.norm == 2:
                dve.wait_ge(s_xfin, KT)
            for n in range(4):
                split_lo(dve, o.unit0 + n + 2, o.slot(n))
                if n == 0:
                    dve_stats(dve, o.norm)
                    dve.wait_ge(s_rb, val(o.norm + 1))
                if n % 2 == 0:
                    dve_gs(dve, o, n // 2, ps[n], n > 0)
                else:
                    dve_us(dve, o, n // 2, ps[n], n > 1)
                    dve_hlo(dve, o, n // 2, n // 2)

            def pair(n, p, par, last=False):
                for j in range(2):
                    f = p * 2 + j
                    split_lo(dve, n + (3 * j + 2), o.slot(j))
                    dve.wait_ge(s_unit, val(p * 4 + (o.m0 + 2 * j + 1)))
                    dve_gs(dve, o, f, ps[0], True)
                    split_lo(dve, n + (3 * j + 3), o.slot(j + 1))
                    dve.wait_ge(s_unit, val(p * 4 + (o.m0 + 2 * j + 2)))
                    dve_us(dve, o, f, ps[1], True)
                    dve_xadd(dve, o, p - 1, 4 * j)
                    dve_hlo(dve, o, f, 2 * par + j)
                    for dd in range(1, 4):
                        dve_xadd(dve, o, p - 1, 4 * j + dd)
                    split_lo(dve, n + (3 * j + 4), o.slot(j))

            pair(o.unit0 + 4, 1, 1)
            pair(o.unit0 + 10, 2, 0)
            with dve.Fori(0, (PAIRS - 3) // 2) as reg:
                i = Lin(reg)
                for j in range(2):
                    pair(i * 12 + (o.unit0 + 16 + 6 * j), i * 2 + (3 + j), 1 - j)
            tail(dve)

        def dve_ffn_tail(dve, o, hi, lo):
            p = PAIRS - 1
            for d in range(KT):
                dve_xadd(dve, o, p, d)
                if hi is not None:
                    if d > 0:
                        dve_norm_tile(dve, o.norm + 1, d - 1, hi, lo)
                    if d == 3 or d == 7:
                        split_lo(dve, o.unit0 + FFN_UNITS + d // 4, o.slot(d // 4))
            if hi is not None:
                dve_norm_tile(dve, o.norm + 1, KT - 1, hi, lo)

        def act_ffn_tail(act, o, hi):
            last = o.a0 + KT * (PAIRS - 1)
            for d in range(KT):
                act_norm_tile(act, o.norm + 1, d, hi, (s_xadd, last + d + 1))
                if hi is not None and (d == 3 or d == 7):
                    split_hi(act, o.unit0 + FFN_UNITS + d // 4, o.slot(d // 4), (s_down, last + d + 1))


        def region(start, end):
            top = [start]

            def take(name, shape):
                size = 4
                for n in shape[1:]:
                    size *= n
                t = at(name, shape, F32, top[0])
                top[0] += (size + 31) // 32 * 32
                assert top[0] <= end, (name, top[0] - end)
                return t
            return take

        x_base = rb_base - 3 * KT * S * 4
        xr = region(x_base, x_base + KT * S * 4)
        m_rows = xr("m_rows", [MH, S])
        cb_all = xr("cb_all", [P, NB, 5, MH])
        mk0 = xr("mk0", [P, 2 * P])
        mk = xr("mk", [P, 2 * P])
        sinkc = xr("sinkc", [P, HEADS])
        sink8 = xr("sink8", [P, HEADS])
        mbig = xr("mbig", [P, P])
        selh = xr("selh", [MH, MH, P])
        sell = xr("sell", [P, P])
        

        pr = region(rb_base, rb_base + 2 * KT * S * 4)
        rope_c = pr("rope_c", [P, S])
        rope_s = pr("rope_s", [P, S])
        z = [pr(f"z{i}", [P, S + 4]) for i in range(2)]
        swapped = pr("swapped", [P, S])
        y = [pr(f"y{i}", [P, S]) for i in range(2)]
        rz_i = pr("rz_i", [MH, S])
        rz_f = pr("rz_f", [MH, S])
        r_t = pr("r_t", [MH, S])
        r_b = pr("r_b", [MH, S])
        r_d = pr("r_d", [MH, S])
        r_mp = pr("r_mp", [MH, NB])
        rows = pr("rows", [P, S])

        za = xr("za", [P, 12, P])
        kcat = xr("kcat", [P, KV_HEADS, 2 * P])
        vnat = xr("vnat", [P, 2, KV_HEADS, 2, HD])
        nd = xr("nd", [P, MH, NA + 1])
        cst = xr("cst", [P, MH, NA + 1])
        br = region(rb_base, rb_base + 2 * KT * S * 4)
        sm = [br(f"sm{i}", [P, S]) for i in range(2)]
        ptb = [br(f"ptb{i}", [P, S]) for i in range(2)]
        ht = br("ht", [P, KT, P])
        zm = br("zm", [P, 16, P])
        ot = br("ot", [P, KT, P])
        vmn = br("vmn", [P, MH, NA + 1])
        dm = br("dm", [P, MH * P])
        dt_ = br("dt", [P, MH * P])
        ptm = br("ptm", [P, MH * P])
        tmp = [br(f"tmp{i}", [P, NA + 1]) for i in range(2)]
        hn = br("hn", [P, S])
        ka = br("ka", [P, MH * P])
        turn = br("turn", [P, 1])
        mx = br("mx", [P, HEADS])
        nm = br("nm", [P, HEADS])
        sn = br("sn", [P, HEADS])
        es = br("es", [P, HEADS])
        rs = br("rs", [P, HEADS])
        rd = br("rd", [P, HEADS])
        cb = br("cb", [P, 5, MH])
        dn = br("dn", [P, MH])
        rn = br("rn", [P, MH])
        ssq = br("ssq", [P, MH])
        var = br("var", [P, MH])
        lv = br("lv", [P, MH])
        y0 = br("y0", [P, MH])
        yy = br("yy", [P, MH])
        yc = br("yc", [P, MH])
        scl = br("scl", [P, MH])

        s_cs = sem("s_cs")
        s_bconst = sem("s_bconst")
        s_xs = sem("s_xs")
        s_z = sem("s_z")
        s_pad = sem("s_pad")
        s_swap = sem("s_swap")
        s_rm = sem("s_rm")
        s_cv = sem("s_cv")
        s_csilu = sem("s_csilu")
        s_y = sem("s_y")
        s_st = [sem(f"s_st{i}") for i in range(2)]
        s_row = sem("s_row")
        s_rowa = sem("s_rowa")
        s_rt = sem("s_rt")
        s_cb = sem("s_cb")
        s_so = sem("s_so")
        s_sos = sem("s_sos")

        N_BCONST = 6

        def pe_proj(pe):
            pe.wait_ge(s_wlo, U_PROJ + 1)
            products(pe, ps[0], U_PROJ % 2, ra_hi, ra_lo, k_wait=(s_alo, KT))
            pe_stats(pe, 1)

            def units(first, count):
                with pe.Fori(0, count // 2) as reg:
                    i = Lin(reg, 2)
                    for j in range(2):
                        ee = i + (first + j)
                        pe.wait_ge(s_wlo, val(ee + (U_PROJ + 1)))
                        if first + j >= 2:
                            pe.wait_ge(s_z, val(ee - 1))
                        products(pe, ps[(first + j) % 2], (U_PROJ + first + j) % 2, ra_hi, ra_lo)

            pe.wait_ge(s_wlo, U_PROJ + 2)
            products(pe, ps[1], (U_PROJ + 1) % 2, ra_hi, ra_lo)
            pe.wait_ge(s_wlo, U_PROJ + 3)
            pe.wait_ge(s_z, 1)
            products(pe, ps[0], U_PROJ % 2, ra_hi, ra_lo)
            units(3, 24)
            pe.wait_ge(s_rowa, 6)
            for c in range(NB):
                mm = nc.tensor.transpose(ps[2][:, c * P:(c + 1) * P], rows[:, c * P:(c + 1) * P], ident[:])
            mm.then_inc(s_rt, 1)
            units(27, 4)
            pe.wait_ge(s_cb, 1)
            pe.wait_ge(s_bconst, 16 * N_BCONST)
            nc.tensor.matmul(ps[3][:, 0:NB * MH], sell[:], cb_all[:, :, 2, :], start=True,
                             stop=True).then_inc(s_so, 1)
            units(31, 6)

        def act_rope(act, ee, par, first=False):
            act.wait_ge(s_z, val(ee + 1))
            if not first:
                act.wait_ge(s_y, val(ee - 1))
            for q in range(4):
                o = q ^ 1
                nc.scalar.copy(swapped[32 * q:32 * q + 32, :],
                               z[par][32 * o:32 * o + 32, 3:3 + S]).then_inc(s_swap, 1)

        def act_proj(act):
            split_hi(act, U_PROJ + 2, U_PROJ % 2, (s_unit, M_PROJ + 1))
            act_stats(act, 1)
            for ee in (1, 2):
                split_hi(act, ee + U_PROJ + 2, ee % 2, (s_unit, ee + M_PROJ + 1))
                act_rope(act, ee, ee % 2, first=ee == 1)
            with act.Fori(0, N_ROPE // 2 - 1) as reg:
                for j in range(2):
                    ee = Lin(reg, 2, 3 + j)
                    split_hi(act, ee + (U_PROJ + 2), (1 + j) % 2, (s_unit, ee + (M_PROJ + 1)))
                    act_rope(act, ee, (1 + j) % 2)

            def raw(first, count):
                with act.Fori(0, count // 2) as reg:
                    for j in range(2):
                        ee = Lin(reg, 2, first + j)
                        split_hi(act, ee + (U_PROJ + 2), (first + j) % 2, (s_unit, ee + (M_PROJ + 1)))

            raw(11, 2)
            with act.Fori(0, N_CONV // 2) as reg:
                for j in range(2):
                    ee = Lin(reg, 2, 13 + j)
                    split_hi(act, ee + (U_PROJ + 2), (13 + j) % 2, (s_unit, ee + (M_PROJ + 1)))
                    act.wait_ge(s_cv, val(Lin(reg, 8, 4 * j + 4)))
                    if j == 0:
                        nc.scalar.activation(y[1][:], y[1][:], ACT.Silu).then_inc(s_y, 1)
                    else:
                        nc.scalar.activation(y[0][:], y[0][:], ACT.Silu).then_inc(s_csilu, 1)
                        act.wait_ge(s_csilu, val(Lin(reg, 1, 1)))
                        nc.scalar.activation(y[0][:], y[0][:], ACT.Copy,
                                             scale=float(DK) ** -0.5).then_inc(s_y, 1)
            raw(21, 2)
            act_rows1(act)
            raw(23, 2)
            act_rows2(act)
            raw(25, 12)

        def act_rows1(act):
            act.wait_ge(s_row, 3)
            nc.scalar.activation(r_t[:], rz_f[:], ACT.Abs).then_inc(s_rowa, 1)
            act.wait_ge(s_rowa, 1)
            nc.scalar.activation(r_t[:], r_t[:], ACT.Exp, scale=-1.0).then_inc(s_rowa, 1)
            act.wait_ge(s_rowa, 2)
            nc.scalar.activation(r_t[:], r_t[:], ACT.Ln, bias=1.0).then_inc(s_rowa, 1)

        def act_rows2(act):
            for i, (q, scale) in enumerate(((32, 1.0), (64, 1.0), (96, -1.0))):
                act.wait_ge(s_row, 17)
                nc.scalar.activation(rows[q:q + MH, :], rows[q:q + MH, :], ACT.Exp,
                                     scale=scale).then_inc(s_rowa, 1)

        def dve_rows0(dve):
            dve.wait_ge(s_unit, M_PROJ + 1)
            nc.vector.tensor_tensor(rz_f[:], ps[0][32:32 + MH, :], rstd_b[32:32 + MH, :],
                                    ALU.mult).then_inc(s_row, 1)
            dve.wait_ge(s_row, 1)
            nc.vector.tensor_tensor(rz_i[:], ps[0][0:MH, :], rstd_b[0:MH, :], ALU.mult).then_inc(s_z, 1)

        def dve_rows1(dve):
            dve.wait_ge(s_z, 1)
            nc.vector.tensor_scalar(rz_i[:], rz_i[:], col[0:MH, C_BI:C_BI + 1], None,
                                    ALU.add).then_inc(s_row, 1)
            nc.vector.tensor_scalar(rz_f[:], rz_f[:], col[0:MH, C_BF:C_BF + 1], None,
                                    ALU.add).then_inc(s_row, 1)
            nc.vector.memset(rows[:], 0.0).then_inc(s_row, 1)
            nc.vector.memset(r_d[:], 1.0).then_inc(s_row, 1)
            dve.wait_ge(s_row, 5)
            d_starts = r_d[:].rearrange("h (c l) -> h c l", l=P)
            nc.vector.memset(d_starts[:, :, 0:1], 0.0).then_inc(s_row, 1)
            nc.vector.memset(r_mp[:], 0.0).then_inc(s_row, 1)

        def dve_rows2(dve):
            chunk = lambda t: t[:].rearrange("h (c l) -> h c l", l=P)
            dve.wait_ge(s_rowa, 3)
            dve.wait_ge(s_row, 7)
            nc.vector.scalar_tensor_tensor(rz_f[:], rz_f[:], 0.0, r_t[:], ALU.min,
                                           ALU.subtract).then_inc(s_row, 1)
            dve.wait_ge(s_row, 8)
            nc.vector.tensor_tensor_scan(r_b[:], r_d[:], rz_f[:], 0.0, ALU.mult,
                                         ALU.add).then_inc(s_row, 1)
            dve.wait_ge(s_row, 9)
            nc.vector.tensor_tensor(rows[0:MH, :], rz_i[:], r_b[:], ALU.subtract).then_inc(s_row, 1)
            nc.vector.memset(r_d[:], 0.0).then_inc(s_row, 1)
            dve.wait_ge(s_row, 11)
            nc.vector.tensor_copy(chunk(r_d)[:, 1:, 0:1], chunk(r_b)[:, :-1, P - 1:P]).then_inc(s_row, 1)
            dve.wait_ge(s_row, 12)
            dve.wait_ge(s_xs, 16 * KT)
            nc.vector.tensor_tensor_scan(m_rows[:], r_d[:], rows[0:MH, :], 0.0, ALU.add,
                                         ALU.max).then_inc(s_row, 1)

        def dve_rows3(dve):
            chunk = lambda t: t.rearrange("h (c l) -> h c l", l=P)
            dve.wait_ge(s_row, 13)
            mc, bc = chunk(m_rows[:]), chunk(r_b[:])
            nc.vector.tensor_tensor(r_mp[:, 1:].unsqueeze(2), mc[:, :-1, P - 1:P], bc[:, :-1, P - 1:P],
                                    ALU.add).then_inc(s_row, 1)
            nc.vector.tensor_tensor(chunk(rows[32:32 + MH, :]), chunk(rows[0:MH, :]),
                                    mc[:, :, P - 1:P].to_broadcast([MH, NB, P]),
                                    ALU.subtract).then_inc(s_row, 1)
            nc.vector.tensor_tensor(rows[96:96 + MH, :], m_rows[:], r_b[:], ALU.add).then_inc(s_row, 1)
            dve.wait_ge(s_row, 16)
            nc.vector.tensor_tensor(chunk(rows[64:64 + MH, :]), r_mp[:].unsqueeze(2).to_broadcast([MH, NB, P]),
                                    mc, ALU.subtract).then_inc(s_row, 1)

        def dve_cols(dve):
            dve.wait_ge(s_rt, 1)
            nc.vector.tensor_copy(cb_all[:, :, 0:4, :],
                                  ps[2][:].rearrange("p (c k l) -> p c k l", c=NB, k=4)[:, :, :, 0:MH]
                                  ).then_inc(s_cb, 1)

        def dve_z(dve, ee, par):
            dve.wait_ge(s_unit, val(ee + (M_PROJ + 1)))
            nc.vector.tensor_tensor(z[par][:, 3:3 + S], ps[par][:], rstd_b[:], ALU.mult).then_inc(s_z, 1)

        def y_free(dve, ee, slot, peeled):
            if not peeled:
                dve.wait_ge(s_st[slot], val(ee * 8 + (-8 if slot else -16)))

        def dve_proj(dve):
            split_lo(dve, U_PROJ + 2, U_PROJ % 2)
            dve_stats(dve, 1)
            dve.wait_ge(s_rb, 2)
            dve_rows0(dve)
            nc.vector.memset(z[0][:, 0:3], 0.0).then_inc(s_pad, 1)
            nc.vector.memset(z[1][:, 0:3], 0.0).then_inc(s_pad, 1)
            dve.wait_ge(s_cs, 32)

            def rope(ee, par, peeled=False):
                split_lo(dve, ee + (U_PROJ + 2), par)
                if ee != 1:
                    dve.wait_ge(s_rm, val(ee * 2 - 2))
                dve_z(dve, ee, par)
                y_free(dve, ee, par, peeled)
                dve.wait_ge(s_z, val(ee + 1))
                nc.vector.tensor_tensor(y[par][:], z[par][:, 3:3 + S], rope_c[:], ALU.mult).then_inc(s_rm, 1)
                dve.wait_ge(s_swap, val(ee * 4))
                nc.vector.tensor_tensor(swapped[:], swapped[:], rope_s[:], ALU.mult).then_inc(s_rm, 1)
                dve.wait_ge(s_rm, val(ee * 2))
                nc.vector.tensor_tensor(y[par][:], y[par][:], swapped[:], ALU.add).then_inc(s_y, 1)

            def raw(ee, par):
                split_lo(dve, ee + (U_PROJ + 2), par)
                dve.wait_ge(s_unit, val(ee + (M_PROJ + 1)))
                y_free(dve, ee, par, False)
                nc.vector.tensor_tensor(y[par][:], ps[par][:], rstd_b[:], ALU.mult).then_inc(s_z, 1)

            rope(1, 1, True)
            rope(2, 0, True)
            with dve.Fori(0, N_ROPE // 2 - 1) as reg:
                for j in range(2):
                    rope(Lin(reg, 2, 3 + j), (1 + j) % 2)
            raw(11, 1)
            raw(12, 0)
            with dve.Fori(0, N_CONV // 2) as reg:
                for j in range(2):
                    ee, par = Lin(reg, 2, 13 + j), (1 + j) % 2
                    split_lo(dve, ee + (U_PROJ + 2), par)
                    dve.wait_ge(s_pad, 2)
                    dve_z(dve, ee, par)
                    y_free(dve, ee, par, False)
                    dve.wait_ge(s_z, val(ee + 1))
                    k0 = Lin(reg, 10, C_CONV + 5 * j)
                    c = lambda t: col[:, bass.ds(val(k0 + t), 1)]
                    nc.vector.tensor_scalar(y[par][:], z[par][:, 3:3 + S], c(3), c(4), ALU.mult,
                                            ALU.add).then_inc(s_cv, 1)
                    for t in (2, 1, 0):
                        dve.wait_ge(s_cv, val(Lin(reg, 8, 4 * j + 3 - t)))
                        nc.vector.scalar_tensor_tensor(y[par][:], z[par][:, t:t + S], c(t), y[par][:],
                                                       ALU.mult, ALU.add).then_inc(s_cv, 1)
            raw(21, 1)
            dve_rows1(dve)
            raw(22, 0)
            raw(23, 1)
            dve_rows2(dve)
            raw(24, 0)
            dve_rows3(dve)

            def raws(first, count):
                with dve.Fori(0, count // 2) as reg:
                    for j in range(2):
                        raw(Lin(reg, 2, first + j), (1 + j) % 2)

            raws(25, 4)
            dve_cols(dve)
            dve_block_init(dve)
            raws(29, 2)
            dve.wait_ge(s_so, 1)
            nc.vector.tensor_copy(cb_all[:, :, 4, :],
                                  ps[3][:, 0:NB * MH].rearrange("p (c h) -> p c h", c=NB)).then_inc(s_sos, 1)
            raws(31, 6)

        def sp_proj(sp):
            def store(ee, par, ready):
                sp.wait_ge(ready[0], val(ready[1]))
                sp.dma_start(zs[val(ee - 1)], y[par][:]).then_inc(s_st[par], 16)

            def tick(ee, k, ready):
                load_unit(sp, ee + (U_PROJ + 2), k % 2)
                store(ee - 1, 1 - k % 2, ready)

            sp.wait_ge(s_down, FT * KT // 2)
            sp.dma_start(rope_c[:], rope_cs[0]).then_inc(s_cs, 16)
            sp.dma_start(rope_s[:], rope_cs[1]).then_inc(s_cs, 16)
            load_unit(sp, U_PROJ + 2, U_PROJ % 2)
            load_unit(sp, U_PROJ + 3, (U_PROJ + 1) % 2)
            for d in range(KT):
                sp.wait_ge(s_xadd, PAIRS * KT - KT + d + 1)
                sp.dma_start(x_s[:, d, :], x[:, d, :]).then_inc(s_xs, 16)
            sp.wait_ge(s_xs, 16 * KT)
            for dst, src in ((mk0, masks[:, 0]), (mk, masks[:, 1]), (sinkc, sinks), (mbig, mask_big), (selh, sel_head),
                             (sell, sel_last)):
                sp.dma_start(dst[:], src).then_inc(s_bconst, 16)
            with sp.Fori(0, N_ROPE // 2) as reg:
                for j in range(2):
                    tick(Lin(reg, 2, 2 + j), j, (s_y, Lin(reg, 2, 1 + j)))
            for ee in (12, 13):
                tick(ee, ee, (s_z, ee))
            with sp.Fori(0, N_CONV // 2) as reg:
                for j in range(2):
                    tick(Lin(reg, 2, 14 + j), j, (s_y, Lin(reg, 2, N_ROPE + 1 + j)))
            for i in range(2):
                sp.wait_ge(s_st[i], 16 * 6)
            load_za(sp, 0)
            with sp.Fori(0, N_RAW // 2 - 1) as reg:
                for j in range(2):
                    tick(Lin(reg, 2, 22 + j), j, (s_z, Lin(reg, 2, 22 + j)))


        names = ("zal zml kc vt vn s sm nm sn p den rd pn pt pte pv on ots sc mb dm dx ptm vmt vme "
                 "kmt ka n1 n2 dc tmp nd c dd ssq lv hn htt hte hts gz init cbn vp").split()
        b = {name: sem(f"b_{name}") for name in names}
        s_gst = [sem(f"s_gst{i}") for i in range(2)]

        def lin(n, k, c):
            return n * k + c

        def pcol(g):
            return (g % 2) * HALF + (g // 2) * 2 * P

        def pe_htt(pe, n):
            pe.wait_ge(b["hn"], val(n))
            for t in range(KT):
                mm = nc.tensor.transpose(ps[3][:, t * P:(t + 1) * P], hn[:, t * P:(t + 1) * P], ident[:])
            mm.then_inc(b["htt"], 1)

        def pe_block(pe, n, first=False):
            def scores(j):
                for g in range(GROUP):
                    h = slice(64 * (g % 2), 64 * (g % 2) + 64)
                    mm = nc.tensor.matmul(ps[1 + j % 2][:, pcol(g):pcol(g) + 2 * P],
                                          za[h, 2 * j + g // 2, :], kcat[h, j, :], start=True, stop=True,
                                          skip_group_check=True)
                mm.then_inc(b["s"], 1)

            def turn_p(j):
                pe.wait_ge(b["pn"], val(lin(n, 4, j + 1)))
                for t in range(2 * GROUP):
                    mm = nc.tensor.transpose(ps[1 + j % 2][:, t * P:(t + 1) * P],
                                             sm[j % 2][:, t * P:(t + 1) * P], ident[:])
                mm.then_inc(b["pt"], 1)

            def weigh_v(j):
                pe.wait_ge(b["pte"], val(lin(n, 4, j + 1)))
                if j >= 2:
                    pe.wait_ge(b["on"], val(lin(n, 8, 2 * j - 2)))
                o = ps[3][:, (1 - j % 2) * HALF:(2 - j % 2) * HALF]
                p_t = ptb[j % 2][:].rearrange("p (g k q) -> p g k q", g=GROUP, k=2)
                for k in range(2):
                    mm = nc.tensor.matmul(o.rearrange("p (g q) -> p g q", g=GROUP), vnat[:, k, j, :, :],
                                          p_t[:, :, k, :], start=(k == 0), stop=(k == 1))
                mm.then_inc(b["pv"], 1)

            def gate(c, k0, k1):
                if k0 == 0:
                    pe.wait_ge(s_wlo, val(lin(n, 2, U_BLK + c + 1)))
                products(pe, ps[0], (U_BLK + c) % 2, ra_hi, ra_lo, ks=(k0, k1))

            pe.wait_ge(b["kc"], val(lin(n, 5, 5)))
            if not first:
                pe.wait_ge(b["nd"], val(lin(n, 4, 0)))
            scores(0)
            if not first:
                pe.wait_ge(b["tmp"], val(lin(n, 4, 0)))
            scores(1)
            if first:
                pe.wait_ge(s_z, PROJ_UNITS)
            else:
                pe.wait_ge(b["gz"], val(lin(n, 2, 0)))
            gate(0, 0, 2)
            if not first:
                pe.wait_ge(b["c"], val(lin(n, 4, 0)))
                pe_htt(pe, n)
            gate(0, 2, 3)
            if not first:
                pe.wait_ge(b["hte"], val(n))
            for t in range(2):
                mm = nc.tensor.transpose(ps[3][:, t * P:(t + 1) * P], za[:, 10 + t, :], ident[:])
            mm.then_inc(b["vt"], 1)
            gate(0, 3, 4)
            turn_p(0)
            turn_p(1)
            pe.wait_ge(b["vn"], val(lin(n, 1, 1)))
            weigh_v(0)
            scores(2)
            weigh_v(1)
            scores(3)
            gate(0, 4, 7)
            turn_p(2)
            gate(0, 7, 8)
            turn_p(3)
            weigh_v(2)
            pe.wait_ge(b["zml"], val(lin(n, 32, 32)))
            pe.wait_ge(b["gz"], val(lin(n, 2, 1)))
            for t in range(KT):
                mm = nc.tensor.transpose(ps[0][:, t * P:(t + 1) * P], zm[:, t, :], ident[:])
            mm.then_inc(b["vmt"], 1)
            for h in range(MH):
                mm = nc.tensor.matmul(ps[1][:, h * P:(h + 1) * P], selh[:, h, :],
                                      m_rows[:, bass.ds(val(lin(n, P, 0)), P)], start=True, stop=True,
                                      skip_group_check=True)
            mm.then_inc(b["mb"], 1)
            for h in range(MH):
                mm = nc.tensor.matmul(ps[1][:, HALF + h * P:HALF + (h + 1) * P], zm[:, KT + 2 * h + 1, :],
                                      zm[:, KT + 2 * h, :], start=True, stop=True, skip_group_check=True)
            mm.then_inc(b["sc"], 1)
            weigh_v(3)
            for h in range(MH):
                mm = nc.tensor.transpose(ps[2][:, h * P:(h + 1) * P], zm[:, KT + 2 * h + 1, :], ident[:])
            mm.then_inc(b["kmt"], 1)
            pe.wait_ge(b["vme"], val(lin(n, 1, 1)))
            gate(1, 0, 3)
            pe.wait_ge(b["ptm"], val(lin(n, 1, 1)))
            pe.wait_ge(b["on"], val(lin(n, 8, 8)))
            for h in range(MH):
                o = slice((h % 2) * HALF, (h % 2) * HALF + NA)
                if h == 2:
                    gate(1, 3, 5)
                if h >= 2:
                    pe.wait_ge(b["nd"], val(lin(n, 4, h - 1)))
                nc.tensor.matmul(ps[1][:, o], ptm[:, h * P:(h + 1) * P], vmn[:, h, 0:NA], start=True,
                                 stop=True).then_inc(b["n1"], 1)
                nc.tensor.matmul(ps[2][:, o], zm[:, KT + 2 * h, :], cst[:, h, 0:NA], start=True,
                                 stop=True).then_inc(b["n2"], 1)
                if h >= 2:
                    pe.wait_ge(b["c"], val(lin(n, 4, h - 1)))
                nc.tensor.matmul(ps[3][:, o], ka[:, h * P:(h + 1) * P], vmn[:, h, 0:NA], start=True,
                                 stop=True).then_inc(b["dc"], 1)
            gate(1, 5, 8)

        def act_keys(act, n):
            act.wait_ge(b["zal"], val(lin(n, 16, 16)))
            nc.scalar.copy(kcat[:, :, 0:P], kcat[:, :, P:2 * P]).then_inc(b["kc"], 1)
            act.wait_ge(b["kc"], val(lin(n, 5, 1)))
            for a in range(2):
                for c in range(2):
                    nc.scalar.copy(kcat[64 * a:64 * a + 64, c::2, P:2 * P],
                                   za[64 * c:64 * c + 64, 8:10, :]).then_inc(b["kc"], 1)

        def act_hte(act, n):
            act.wait_ge(b["htt"], val(n))
            if not isinstance(n, int) or n > 1:
                act.wait_ge(b["hts"], val(lin(n, 16, -16)))
            nc.scalar.copy(ht[:], ps[3][:].rearrange("p (t l) -> p t l", t=KT)).then_inc(b["hte"], 1)

        def act_block(act, n, first=False, last=False):
            def exps(j):
                act.wait_ge(b["nm"], val(lin(n, 4, j + 1)))
                for g in range(GROUP):
                    h = GROUP * j + g
                    p = sm[j % 2][:, pcol(g):pcol(g) + 2 * P]
                    nc.scalar.activation(p, p, ACT.Exp, bias=nm[:, h:h + 1], scale=HD ** -0.5,
                                         accum_out=rs[:, h:h + 1]).then_inc(b["p"], 1)
                act.wait_ge(b["sn"], val(lin(n, 4, j + 1)))
                q = slice(GROUP * j, GROUP * (j + 1))
                nc.scalar.activation(es[:, q], sn[:, q], ACT.Exp).then_inc(b["p"], 1)

            def take_p(j):
                act.wait_ge(b["pt"], val(lin(n, 4, j + 1)))
                if j >= 2:
                    act.wait_ge(b["pv"], val(lin(n, 4, j - 1)))
                nc.scalar.copy(ptb[j % 2][:], ps[1 + j % 2][:]).then_inc(b["pte"], 1)

            exps(0)
            if not first:
                act_hte(act, n)
            exps(1)
            if not first:
                split_hi(act, lin(n, 2, U_BLK + 1), (U_BLK + 1) % 2, (s_unit, lin(n, 2, M_BLK)))
            take_p(0)
            take_p(1)
            exps(2)
            exps(3)
            split_hi(act, lin(n, 2, U_BLK + 2), U_BLK % 2, (s_unit, lin(n, 2, M_BLK + 1)))
            take_p(2)
            take_p(3)
            act.wait_ge(b["vmt"], val(lin(n, 1, 1)))
            nc.scalar.copy(vmn[:, :, 0:DV], ps[0][:].rearrange("p (h v) -> p h v", h=MH)).then_inc(b["vme"], 1)
            act.wait_ge(b["dm"], val(lin(n, 1, 1)))
            for h in range(MH):
                q = slice(h * P, (h + 1) * P)
                nc.scalar.activation(dt_[:, q], dm[:, q], ACT.Exp, bias=cb[:, 0, h:h + 1],
                                     scale=-1.0).then_inc(b["dx"], 1)
            if not last:
                act_keys(act, n + 1)
            for h in range(MH):
                act.wait_ge(b["n2"], val(lin(n, 4, h + 1)))
                if h >= 2:
                    act.wait_ge(b["nd"], val(lin(n, 4, h - 1)))
                nc.scalar.activation(tmp[h % 2][:, 0:NA], ps[2][:, (h % 2) * HALF:(h % 2) * HALF + NA],
                                     ACT.Copy, scale=cb[:, 2, h:h + 1]).then_inc(b["tmp"], 1)
            act.wait_ge(b["dd"], val(lin(n, 9, 3)))
            for h in range(MH):
                nc.scalar.activation(hn[:, h * DV:(h + 1) * DV], nd[:, h, 0:DV], ACT.Square,
                                     scale=rn[:, h:h + 1], accum_out=ssq[:, h:h + 1]).then_inc(b["ssq"], 1)
            act.wait_ge(b["dd"], val(lin(n, 9, 4)))
            nc.scalar.activation(lv[:], var[:], ACT.Ln).then_inc(b["lv"], 1)
            act.wait_ge(b["lv"], val(lin(n, 2, 1)))
            nc.scalar.activation(y0[:], lv[:], ACT.Exp, scale=-0.5).then_inc(b["lv"], 1)

        def dve_hn(dve, n):
            dve.wait_ge(b["lv"], val(lin(n, 2, 0)))
            nc.vector.tensor_tensor(yy[:], y0[:], y0[:], ALU.mult).then_inc(b["dd"], 1)
            dve.wait_ge(b["dd"], val(lin(n, 9, -4)))
            nc.vector.tensor_tensor(yy[:], yy[:], var[:], ALU.mult).then_inc(b["dd"], 1)
            dve.wait_ge(b["dd"], val(lin(n, 9, -3)))
            nc.vector.tensor_scalar(yy[:], yy[:], -0.5, 1.5, ALU.mult, ALU.add).then_inc(b["dd"], 1)
            dve.wait_ge(b["dd"], val(lin(n, 9, -2)))
            nc.vector.tensor_tensor(yc[:], yy[:], y0[:], ALU.mult).then_inc(b["dd"], 1)
            dve.wait_ge(b["dd"], val(lin(n, 9, -1)))
            nc.vector.tensor_tensor(scl[:], yc[:], rn[:], ALU.mult).then_inc(b["dd"], 1)
            dve.wait_ge(b["dd"], val(lin(n, 9, 0)))
            nc.vector.tensor_tensor(hn[:].rearrange("p (h v) -> p h v", h=MH), nd[:, :, 0:DV],
                                    scl[:].unsqueeze(2).to_broadcast([P, MH, DV]),
                                    ALU.mult).then_inc(b["hn"], 1)

        def dve_block(dve, n, first=False):
            def maxima(j):
                dve.wait_ge(b["s"], val(lin(n, 4, j + 1)))
                nc.vector.memset(turn[:], 0.0)
                for g in range(GROUP):
                    h = GROUP * j + g
                    q = slice(pcol(g), pcol(g) + 2 * P)
                    nc.vector.tensor_tensor_reduce(sm[j % 2][:, q], ps[1 + j % 2][:, q], (mk0 if first else mk)[:],
                                                   1.0, sink8[:, h:h + 1], ALU.add, ALU.max,
                                                   mx[:, h:h + 1]).then_inc(b["sm"], 1)
                q = slice(GROUP * j, GROUP * (j + 1))
                dve.wait_ge(b["sm"], val(lin(n, 16, 4 * j + 4)))
                nc.vector.tensor_scalar(nm[:, q], mx[:, q], -HD ** -0.5, None, ALU.mult).then_inc(b["nm"], 1)
                dve.wait_ge(b["nm"], val(lin(n, 4, j + 1)))
                nc.vector.tensor_tensor(sn[:, q], sinkc[:, q], nm[:, q], ALU.add).then_inc(b["sn"], 1)

            def divisors(j):
                q = slice(GROUP * j, GROUP * (j + 1))
                dve.wait_ge(b["p"], val(lin(n, 20, 5 * j + 5)))
                nc.vector.tensor_tensor(rd[:, q], rs[:, q], es[:, q], ALU.add).then_inc(b["den"], 1)
                dve.wait_ge(b["den"], val(lin(n, 4, j + 1)))
                nc.vector.reciprocal(rd[:, q], rd[:, q]).then_inc(b["rd"], 1)
                dve.wait_ge(b["rd"], val(lin(n, 4, j + 1)))
                p = sm[j % 2][:].rearrange("p (a b k) -> p a b k", a=2, b=2)
                nc.vector.tensor_tensor(p, p, rd[:, q].rearrange("p (b a) -> p a b", a=2).unsqueeze(3)
                                        .to_broadcast([P, 2, 2, 2 * P]), ALU.mult).then_inc(b["pn"], 1)

            def outputs(j):
                dve.wait_ge(b["pv"], val(lin(n, 4, j + 1)))
                if j == 0:
                    if first:
                        dve.wait_ge(s_st[1], 16 * (Z_TILES // 2))
                    else:
                        dve.wait_ge(b["ots"], val(lin(n, 16, 0)))
                for a in range(2):
                    rows_a, c0 = slice(64 * a, 64 * a + 64), (1 - j % 2) * HALF + 2 * P * a
                    nc.vector.tensor_copy(ot[rows_a, 2 * j:2 * j + 2, :],
                                          ps[3][rows_a, c0:c0 + 2 * P].rearrange("p (t q) -> p t q", t=2)
                                          ).then_inc(b["on"], 1)

            maxima(0)
            if not first:
                dve_hn(dve, n)
                dve.wait_ge(b["hn"], val(n))
            nc.vector.tensor_copy(cb[:], cb_all[:, bass.ds(val(n), 1), :, :].rearrange("p c k h -> p (c k) h")
                                  ).then_inc(b["cbn"], 1)
            nc.vector.tensor_copy(vnat[:, 0], vnat[:, 1]).then_inc(b["vp"], 1)
            maxima(1)
            divisors(0)
            dve.wait_ge(b["vt"], val(lin(n, 1, 1)))
            dve.wait_ge(b["vp"], val(lin(n, 1, 1)))
            nc.vector.tensor_copy(vnat[:, 1], ps[3][:, 0:2 * P].rearrange("p (j v) -> p j v", j=KV_HEADS)
                                  .unsqueeze(2).to_broadcast([P, KV_HEADS, 2, HD])).then_inc(b["vn"], 1)
            divisors(1)
            if not first:
                split_lo(dve, lin(n, 2, U_BLK + 1), (U_BLK + 1) % 2)
            outputs(0)
            maxima(2)
            outputs(1)
            maxima(3)
            divisors(2)
            divisors(3)
            dve.wait_ge(s_unit, val(lin(n, 2, M_BLK + 1)))
            if not first:
                dve.wait_ge(s_gst[0], val(lin(n, 16, 0)))
            nc.vector.tensor_tensor(t_a[:], ps[0][:], rstd_b[:], ALU.mult).then_inc(b["gz"], 1)
            split_lo(dve, lin(n, 2, U_BLK + 2), U_BLK % 2)
            outputs(2)
            dve.wait_ge(b["mb"], val(lin(n, 1, 1)))
            nc.vector.tensor_tensor(dm[:].rearrange("p (h l) -> p h l", h=MH),
                                    ps[1][:, 0:HALF].rearrange("p (h l) -> p h l", h=MH),
                                    mbig[:].unsqueeze(1).to_broadcast([P, MH, P]), ALU.add).then_inc(b["dm"], 1)
            outputs(3)
            dve.wait_ge(b["kmt"], val(lin(n, 1, 1)))
            dve.wait_ge(b["cbn"], val(lin(n, 1, 1)))
            nc.vector.tensor_tensor(ka[:].rearrange("p (h l) -> p h l", h=MH),
                                    ps[2][:, 0:HALF].rearrange("p (h l) -> p h l", h=MH),
                                    cb[:, 1, :].unsqueeze(2).to_broadcast([P, MH, P]),
                                    ALU.mult).then_inc(b["ka"], 1)
            dve.wait_ge(b["sc"], val(lin(n, 1, 1)))
            dve.wait_ge(b["dx"], val(lin(n, 4, 4)))
            nc.vector.tensor_tensor(ptm[:], ps[1][:, HALF:2 * HALF], dt_[:], ALU.mult).then_inc(b["ptm"], 1)
            for h in range(MH):
                o = slice((h % 2) * HALF, (h % 2) * HALF + NA)
                dve.wait_ge(b["n1"], val(lin(n, 4, h + 1)))
                dve.wait_ge(b["tmp"], val(lin(n, 4, h + 1)))
                nc.vector.tensor_tensor(nd[:, h, 0:NA], ps[1][:, o], tmp[h % 2][:, 0:NA],
                                        ALU.add).then_inc(b["nd"], 1)
                dve.wait_ge(b["dc"], val(lin(n, 4, h + 1)))
                nc.vector.scalar_tensor_tensor(cst[:, h, 0:NA], cst[:, h, 0:NA], cb[:, 4, h:h + 1],
                                               ps[3][:, o], ALU.mult, ALU.add).then_inc(b["c"], 1)
            dve.wait_ge(b["nd"], val(lin(n, 4, 4)))
            nc.vector.tensor_tensor(dn[:], nd[:, :, DV], cb[:, 3, :], ALU.max).then_inc(b["dd"], 1)
            dve.wait_ge(b["dd"], val(lin(n, 9, 1)))
            nc.vector.scalar_tensor_tensor(dn[:], nd[:, :, DV], -1.0, dn[:], ALU.mult,
                                           ALU.max).then_inc(b["dd"], 1)
            dve.wait_ge(b["dd"], val(lin(n, 9, 2)))
            nc.vector.reciprocal(rn[:], dn[:]).then_inc(b["dd"], 1)
            dve.wait_ge(b["ssq"], val(lin(n, 4, 4)))
            nc.vector.tensor_scalar(var[:], ssq[:], 1.0 / DV, EPS, ALU.mult, ALU.add).then_inc(b["dd"], 1)
            dve.wait_ge(s_unit, val(lin(n, 2, M_BLK + 2)))
            if not first:
                dve.wait_ge(s_gst[1], val(lin(n, 16, 0)))
            nc.vector.tensor_tensor(t_b[:], ps[0][:], rstd_b[:], ALU.mult).then_inc(b["gz"], 1)

        def load_za(sp, n):
            sp.dma_start(za[:], zs[0:12, :, bass.ds(val(lin(n, P, 0)), P)].rearrange("t p c -> p t c")
                         ).then_inc(b["zal"], 16)

        def load_zm(sp, n):
            sp.wait_ge(s_st[0], 16 * (Z_TILES // 2))
            for i, t in enumerate((N_ROPE + 10, N_ROPE + 2)):
                sp.dma_start(zm[:, 8 * i:8 * i + 8, :],
                             zs[t:t + 8, :, bass.ds(val(lin(n, P, 0)), P)].rearrange("t p c -> p t c")
                             ).then_inc(b["zml"], 16)

        def store_ht(sp, n):
            sp.wait_ge(b["hte"], val(n))
            sp.dma_start(mem_s[:, :, bass.ds(val(n * P), P)].rearrange("t p c -> p t c"),
                         ht[:]).then_inc(b["hts"], 16)

        def sp_block(sp, n, first=False, last=False):
            if not first:
                load_unit(sp, lin(n, 2, U_BLK + 2), U_BLK % 2)
                store_ht(sp, n)
            if not last:
                sp.wait_ge(b["s"], val(lin(n, 4, 4)))
                load_za(sp, n + 1)
            load_unit(sp, lin(n, 2, U_BLK + 3), (U_BLK + 1) % 2)
            sp.wait_ge(b["gz"], val(lin(n, 2, 1)))
            sp.dma_start(gs[val(lin(n, 2, 0))], t_a[:]).then_inc(s_gst[0], 16)
            sp.wait_ge(b["on"], val(lin(n, 8, 8)))
            sp.dma_start(att_s[:, :, bass.ds(val(n * P + P), P)].rearrange("t p c -> p t c"),
                         ot[:]).then_inc(b["ots"], 16)
            if not last:
                sp.wait_ge(b["n2"], val(lin(n, 4, 4)))
                load_zm(sp, n + 1)
            sp.wait_ge(b["gz"], val(lin(n, 2, 2)))
            sp.dma_start(gs[val(lin(n, 2, 1))], t_b[:]).then_inc(s_gst[1], 16)

        def sp_blocks(sp):
            for i in range(2):
                sp.wait_ge(s_st[i], 16 * (Z_TILES // 2))
            load_zm(sp, 0)
            sp_block(sp, 0, first=True)
            with sp.Fori(1, NB - 1) as reg:
                sp_block(sp, Lin(reg))
            sp_block(sp, NB - 1, last=True)
            store_ht(sp, NB)

        def pe_blocks(pe):
            pe.wait_ge(s_z, PROJ_UNITS - 1)
            pe.wait_ge(s_sos, 1)
            pe_block(pe, 0, first=True)
            with pe.Fori(1, NB) as reg:
                pe_block(pe, Lin(reg))
            pe.wait_ge(b["c"], 4 * NB)
            pe_htt(pe, NB)

        def act_blocks(act):
            act.wait_ge(b["init"], 4)
            act_keys(act, 0)
            act_block(act, 0, first=True)
            with act.Fori(1, NB - 1) as reg:
                act_block(act, Lin(reg))
            act_block(act, NB - 1, last=True)
            act_hte(act, NB)
            split_hi(act, U_BLK + 2 * NB + 1, (U_BLK + 1) % 2, (s_unit, M_BLK + 2 * NB))

        def dve_block_init(dve):
            dve.wait_ge(s_bconst, 16 * N_BCONST)
            nc.vector.memset(kcat[:], 0.0).then_inc(b["init"], 1)
            nc.vector.memset(vnat[:], 0.0).then_inc(b["init"], 1)
            nc.vector.memset(cst[:], 0.0).then_inc(b["init"], 1)
            nc.vector.tensor_scalar(sink8[:], sinkc[:], HD ** 0.5, None, ALU.mult).then_inc(b["init"], 1)

        def dve_blocks(dve):
            nc.vector.memset(vmn[:, :, DV:DV + 1], 1.0).then_inc(b["init"], 1)
            dve.wait_ge(b["init"], 5)
            dve.wait_ge(s_sos, 1)
            dve_block(dve, 0, first=True)
            with dve.Fori(1, NB) as reg:
                dve_block(dve, Lin(reg))
            dve_hn(dve, NB)
            split_lo(dve, U_BLK + 2 * NB + 1, (U_BLK + 1) % 2)

        s_ld = [sem(f"s_ld{i}") for i in range(4)]
        s_fhi = sem("s_fhi")
        s_flo = sem("s_flo")
        s_sg = sem("s_sg")
        s_sgo = sem("s_sgo")
        s_ym = sem("s_ym")
        s_ysum = sem("s_ysum")
        s_mem = sem("s_mem")
        s_xfin = sem("s_xfin")
        stage = [t_a, t_b, rstd_b, sq]
        w_slot = [U_MERGE % 2, 1 - U_MERGE % 2]

        def pe_merge(pe):
            for part, (hi, lo) in enumerate(((ra_hi, ra_lo), (rb_hi, rb_lo), (ra_hi, ra_lo))):
                def unit(c, k_wait=None):
                    u = c + (U_MERGE + KT * part)
                    j = (c if isinstance(c, int) else c.a) % 2
                    pe.wait_ge(s_wlo, val(u + 1))
                    if part == 0:
                        if isinstance(c, int):
                            if c == 0:
                                pe.wait_ge(b["gz"], 2 * NB)
                            else:
                                pe.wait_ge(b["nd"], MH * NB)
                        else:
                            pe.wait_ge(s_ym, val(c - 1))
                    elif part == 1:
                        pe.wait_ge(s_ym, val(c + (KT - 1)))
                    elif isinstance(c, int):
                        pe.wait_ge(s_ym, 2 * KT - 1 + c)
                    else:
                        pe.wait_ge(s_xfin, val(c - 1))
                    products(pe, ps[j], w_slot[j], hi, lo, k_wait=k_wait)

                unit(0, k_wait=(s_flo, KT * part))
                unit(1)
                with pe.Fori(0, KT // 2 - 1) as reg:
                    for j in range(2):
                        unit(Lin(reg, 2, 2 + j))

        def act_merge(act):
            for k in range(KT):
                act.wait_ge(s_ld[k % 4], 16 * (k // 4 + 1))
                act.wait_ge(s_unit, M_MERGE)
                nc.scalar.copy(ra_hi[:, k, :], stage[k % 4][:]).then_inc(s_fhi, 1)

            def branch(part):
                with act.Fori(0, KT // 2) as reg:
                    for j in range(2):
                        c = Lin(reg, 2, j)
                        act.wait_ge(s_ld[0], val(c * 16 + (32 + 16 + KT * 16 * part)))
                        nc.scalar.activation(t_a[:], t_a[:], ACT.Sigmoid).then_inc(s_sg, 1)
                        if part == 0:
                            act.wait_ge(s_ld[2], val(c * 16 + (32 + 16)))
                            nc.scalar.activation(rstd_b[:], rstd_b[:], ACT.Sigmoid).then_inc(s_sgo, 1)
                        split_hi(act, c + (U_MERGE + KT * part + 2), w_slot[j],
                                 (s_unit, c + (M_MERGE + KT * part + 1)))
                        if part == 0:
                            act.wait_ge(s_mem, val(c + 1))
                            nc.scalar.copy(rb_hi[:, bass.ds(val(c), 1), :].rearrange("p o s -> p (o s)"),
                                           t_b[:]).then_inc(s_fhi, 1)
                        else:
                            act.wait_ge(s_ysum, val(c + 1))
                            nc.scalar.copy(ra_hi[:, bass.ds(val(c), 1), :].rearrange("p o s -> p (o s)"),
                                           x[:, bass.ds(val(c), 1), :].rearrange("p o s -> p (o s)")
                                           ).then_inc(s_fhi, 1)

            branch(0)
            branch(1)
            for c in range(KT):
                split_hi(act, U_MERGE + 2 * KT + c + 2, w_slot[c % 2], (s_unit, M_MERGE + 2 * KT + c + 1))
                act_norm_tile(act, 2, c, rb_hi, (s_xfin, c + 1))

        def dve_merge(dve):
            for k in range(KT):
                dve.wait_ge(s_fhi, k + 1)
                nc.vector.tensor_tensor(ra_lo[:, k, :], stage[k % 4][:], ra_hi[:, k, :].bitcast(F32),
                                        ALU.subtract).then_inc(s_flo, 1)

            def tile_of(t, c):
                return t[:, bass.ds(val(c), 1), :].rearrange("p o s -> p (o s)")

            with dve.Fori(0, KT // 2) as reg:
                for j in range(2):
                    c = Lin(reg, 2, j)
                    dve.wait_ge(s_ld[1], val(c * 16 + (32 + 16)))
                    dve.wait_ge(s_sgo, val(c + 1))
                    nc.vector.scalar_tensor_tensor(t_b[:], t_b[:], col[:, bass.ds(val(c + C_HN), 1)], rstd_b[:],
                                                   ALU.mult, ALU.mult).then_inc(s_mem, 1)
                    split_lo(dve, c + (U_MERGE + 2), w_slot[j])
                    dve.wait_ge(s_unit, val(c + (M_MERGE + 1)))
                    dve.wait_ge(s_sg, val(c + 1))
                    nc.vector.tensor_tensor(tile_of(x, c), ps[j][:], t_a[:], ALU.mult).then_inc(s_ym, 1)
                    dve.wait_ge(s_fhi, val(c + (KT + 1)))
                    nc.vector.tensor_tensor(tile_of(rb_lo, c), t_b[:], tile_of(rb_hi, c).bitcast(F32),
                                            ALU.subtract).then_inc(s_flo, 1)
            with dve.Fori(0, KT // 2) as reg:
                for j in range(2):
                    c = Lin(reg, 2, j)
                    split_lo(dve, c + (U_MERGE + KT + 2), w_slot[j])
                    dve.wait_ge(s_unit, val(c + (M_MERGE + KT + 1)))
                    dve.wait_ge(s_sg, val(c + (KT + 1)))
                    nc.vector.tensor_tensor(t_a[:], ps[j][:], t_a[:], ALU.mult).then_inc(s_ym, 1)
                    dve.wait_ge(s_ym, val(c + (KT + 1)))
                    nc.vector.tensor_tensor(tile_of(x, c), tile_of(x, c), t_a[:], ALU.add).then_inc(s_ysum, 1)
                    dve.wait_ge(s_fhi, val(c + (2 * KT + 1)))
                    nc.vector.tensor_tensor(tile_of(ra_lo, c), tile_of(x, c), tile_of(ra_hi, c).bitcast(F32),
                                            ALU.subtract).then_inc(s_flo, 1)
            for c in range(KT):
                split_lo(dve, U_MERGE + 2 * KT + c + 2, w_slot[c % 2])
                dve.wait_ge(s_unit, M_MERGE + 2 * KT + c + 1)
                dve.wait_ge(s_ld[1], 16 * (2 + KT + c + 1))
                nc.vector.tensor_tensor(x[:, c, :], ps[c % 2][:], t_b[:], ALU.add).then_inc(s_xfin, 1)
                dve_norm_tile(dve, 2, c, rb_hi, rb_lo)

        def sp_merge(sp):
            for i in range(2):
                sp.wait_ge(s_gst[i], 16 * NB)
            sp.wait_ge(b["ots"], 16 * NB)
            for k in range(KT):
                if k >= 4:
                    sp.wait_ge(s_flo, k - 3)
                sp.dma_start(stage[k % 4][:], att_s[k, :, P:]).then_inc(s_ld[k % 4], 16)

            def tick(c, j, part):
                if part == 0:
                    sp.wait_ge(s_flo, val(c + KT))
                    sp.dma_start(t_b[:], mem_s[val(c), :, P:]).then_inc(s_ld[1], 16)
                    sp.dma_start(rstd_b[:], zs[val(c + (N_ROPE + 18))]).then_inc(s_ld[2], 16)
                    sp.dma_start(t_a[:], gs[val(c * 2)]).then_inc(s_ld[0], 16)
                else:
                    if c != 0:
                        sp.wait_ge(s_ysum, val(c))
                    sp.dma_start(t_a[:], gs[val(c * 2 + 1)]).then_inc(s_ld[0], 16)
                load_unit(sp, c + (U_MERGE + KT * part + 2), w_slot[j])

            sp.wait_ge(b["hts"], 16 * NB)
            with sp.Fori(0, KT // 2) as reg:
                for j in range(2):
                    tick(Lin(reg, 2, j), j, 0)
            sp.wait_ge(s_flo, 2 * KT)
            tick(0, 0, 1)
            tick(1, 1, 1)
            with sp.Fori(0, KT // 2 - 1) as reg:
                for j in range(2):
                    tick(Lin(reg, 2, 2 + j), j, 1)
            for c in range(KT):
                if c:
                    sp.wait_ge(s_xfin, c)
                sp.dma_start(t_b[:], x_s[:, c, :]).then_inc(s_ld[1], 16)
                load_unit(sp, U_MERGE + 2 * KT + c + 2, w_slot[c % 2])


        ffn1 = Ffn(0, 0, 0, 0, (ra_hi, ra_lo), (rb_hi, rb_lo))
        ffn2 = Ffn(1, U_FFN2, M_FFN2, 2, (rb_hi, rb_lo), (ra_hi, ra_lo))

        block = e(nc.Block())

        @block.sync
        def _(sp):
            sp.dma_start(col[:], cols).then_inc(s_const, 16)
            sp.dma_start(ident[:], ident_d).then_inc(s_const, 16)
            for i in range(4):
                sp.dma_start(x[:, 2 * i:2 * i + 2, :], x_t[:, 2 * i:2 * i + 2, :]).then_inc(s_x[i], 16)
                if i == 0:
                    for n in range(2):
                        load_unit(sp, n, n, first=True)
            load_units(sp, 2, FFN_UNITS)
            sp_proj(sp)
            sp_blocks(sp)
            sp_merge(sp)
            load_units(sp, U_FFN2 + 2, FFN_UNITS - 2)
            for d in range(KT):
                sp.wait_ge(s_fin, d + 1)
                sp.dma_start(out[:, d, :], x[:, d, :]).then_inc(s_out, 16)
            sp.wait_ge(s_out, 16 * KT)

        @block.tensor
        def _(pe):
            pe.wait_ge(s_const, 32)
            pe.wait_ge(s_ones, 1)
            pe_ffn(pe, ffn1)
            pe_proj(pe)
            pe_blocks(pe)
            pe_merge(pe)
            pe_ffn(pe, ffn2)
            pe_stats(pe, 3)

        @block.scalar
        def _(act):
            act.wait_ge(s_const, 32)
            for d in range(KT):
                act_norm_tile(act, 0, d, ra_hi, (s_x[d // 2], 16))
                if d < 2:
                    split_hi(act, d, d)
            act_ffn(act, ffn1, lambda act: act_ffn_tail(act, ffn1, ra_hi))
            act_proj(act)
            act_blocks(act)
            act_merge(act)
            act_ffn(act, ffn2, lambda act: act_ffn_tail(act, ffn2, None))
            act_stats(act, 3)

        @block.vector
        def _(dve):
            nc.vector.memset(ones[:], 1.0).then_inc(s_ones, 1)
            dve.wait_ge(s_const, 32)
            for d in range(KT):
                dve_norm_tile(dve, 0, d, ra_hi, ra_lo)
                if d < 2:
                    split_lo(dve, d, d)
            dve_ffn(dve, ffn1, lambda dve: dve_ffn_tail(dve, ffn1, ra_hi, ra_lo))
            dve_proj(dve)
            dve_blocks(dve)
            dve_merge(dve)
            dve_ffn(dve, ffn2, lambda dve: dve_ffn_tail(dve, ffn2, None, None))
            dve_stats(dve, 3)
            dve.wait_ge(s_rb, 4)
            for d in range(KT):
                g = C_GAIN + 3 * KT + d
                nc.vector.scalar_tensor_tensor(x[:, d, :], x[:, d, :], col[:, g:g + 1], rstd_b[:],
                                               ALU.mult, ALU.mult).then_inc(s_fin, 1)

        @block.gpsimd
        def _(pool):
            for norm in range(4):
                pool_norm(pool, norm)


def tile_weights(w):
    return w.reshape(KT, P, w.shape[1] // P, P).transpose(2, 1, 0, 3).reshape(-1, P, D)


def tile_down(w):
    return w.reshape(PAIRS, 2, P, 2, HALF).transpose(0, 3, 2, 1, 4).reshape(-1, P, D)


def ffn_stream(gate, up, down):
    g, u, d = tile_weights(gate), tile_weights(up), tile_down(down)
    parts = [g[0:1], u[0:1], g[1:2], u[1:2]]
    for p in range(1, PAIRS):
        for j in range(2):
            f, h = 2 * p + j, 2 * (p - 1) + j
            parts += [g[f:f + 1], u[f:f + 1], d[h:h + 1]]
    return parts + [d[-2:]]


def projection_columns(a):
    w = a["w_in"][0]
    at = np.cumsum([0, D, 256, 256, 512, 512, D, D, MH, MH, D, D])
    q, k, v, qm, km, vm, om, i, f, ga, gm = [w[:, at[n]:at[n + 1]] for n in range(11)]
    gates = np.zeros((D, P), w.dtype)
    gates[:, 0:MH], gates[:, 32:32 + MH] = i, f
    turns = [t[:, c * P:(c + 1) * P] for c in range(MH) for t in (qm, km)]
    ends = [t[:, c * P:(c + 1) * P] for c in range(KT) for t in (ga, gm)]
    return np.concatenate([gates, q, k, v] + turns + [vm, om] + ends, axis=1)


def kernel(**inputs):
    import concourse.bacc as bacc
    from concourse.bass_utils import run_bass_kernel_spmd

    a = {k: np.asarray(v) for k, v in inputs.items()}
    w_stream = np.concatenate(
        ffn_stream(a["ffn1_w_gate"][0], a["ffn1_w_up"][0], a["ffn1_w_down"][0])
        + [tile_weights(projection_columns(a))]
        + [tile_weights(a[k][0]) for k in ("w_att", "w_mlstm", "w_out")]
        + ffn_stream(a["ffn2_w_gate"][0], a["ffn2_w_up"][0], a["ffn2_w_down"][0]))
    x_t = np.ascontiguousarray(a["x"][0].T.reshape(KT, P, S).transpose(1, 0, 2))

    def by_tile(v):
        return v.reshape(KT, P).T

    def on_heads(v):
        return np.concatenate([v, np.zeros(P - MH, v.dtype)])[:, None]

    conv = np.concatenate([a["conv_w"][0], a["conv_b"]], axis=0).reshape(5, 2, MH, P)
    cols = np.concatenate([by_tile(a["ffn1_norm"][0]), by_tile(a["mix_norm"][0]), by_tile(a["ffn2_norm"][0]),
                           by_tile(a["final_norm"]), np.full((P, 1), EPS, np.float32),
                           by_tile(a["head_norm"][0]), on_heads(a["b_i"][0]), on_heads(a["b_f"][0]),
                           conv.transpose(3, 2, 1, 0).reshape(P, 40)], axis=1)
    pos = np.arange(S, dtype=np.float32)
    freq = np.float32(10000.0) ** (-np.arange(HD // 2, dtype=np.float32) / np.float32(HD // 2))
    angle = (pos[None, :] * freq[:, None]).astype(np.float32)
    sin, cos = np.sin(angle), np.cos(angle)
    rope_cs = np.stack([np.tile(cos, (4, 1)), np.tile(np.concatenate([-sin, sin]), (2, 1))]).astype(np.float32)
    l, m = np.arange(P)[:, None], np.arange(P)[None, :]
    prev = np.where(m > l, 0.0, -BIG)
    cur = np.where(m <= l, 0.0, -BIG)
    masks = np.stack([np.concatenate([before, cur], axis=1)
                      for before in (np.full((P, P), -BIG), prev)], axis=1).astype(np.float32)
    mask_big = np.where(l > m, BIG, 0.0).astype(np.float32)
    sel_head = np.zeros((MH, MH, P), np.float32)
    for h in range(MH):
        sel_head[h, h] = 1.0
    sel_last = np.zeros((P, P), np.float32)
    sel_last[P - 1] = 1.0
    arrays = {"w_stream": w_stream, "x_t": x_t, "cols": np.ascontiguousarray(cols),
              "ident_d": np.eye(P, dtype=np.float32),
              "sinks": np.ascontiguousarray(np.broadcast_to(a["attn_sinks"], (P, HEADS))),
              "rope_cs": rope_cs, "masks": masks, "mask_big": mask_big, "sel_head": sel_head,
              "sel_last": sel_last}
    nc = bacc.Bacc("TRN2", target_bir_lowering=False, num_devices=1)
    args = [nc.dram_tensor(k, v.shape, F32, kind="ExternalInput").ap() for k, v in arrays.items()]
    args.append(nc.dram_tensor("out_t", (P, KT, S), F32, kind="ExternalOutput").ap())
    for name, shape in (("zs", (Z_TILES, P, S)), ("gs", (2 * KT, P, S)), ("att_s", (KT, P, P + S)),
                        ("mem_s", (KT, P, P + S)), ("x_s", (P, KT, S))):
        args.append(nc.dram_tensor(name, shape, F32, kind="Internal").ap())
    hybrid_layer(nc, *args)
    r = run_bass_kernel_spmd(nc, [arrays], core_ids=[0])
    out_t = r.results[0]["out_t"]
    return np.ascontiguousarray(out_t.transpose(1, 0, 2).reshape(D, S).T)[None]
```

```python
from contextlib import ExitStack

import numpy as np

import concourse.bass as bass
from concourse import mybir
from concourse.alu_op_type import AluOpType as ALU

ACT = mybir.ActivationFunctionType
F32 = mybir.dt.float32
F32R = mybir.dt.float32r

P = 128
D = 1024
S = 1024
KT = D // P
HALF = 512
F = 2816
FT = F // P
PAIRS = FT // 2
EPS = 1e-5

FFN_UNITS = 3 * FT

C_GAIN = 0
C_EPS = 32
C_HN = 33
C_BI, C_BF = 41, 42
C_CONV = 43
N_COLS = C_CONV + 5 * 8

HEADS, KV_HEADS, HD = 16, 4, 64
GROUP = HEADS // KV_HEADS
MH = 4
DV = D // MH
DK = DV // 2
NA = DV + 1
NB = S // P
BIG = 1e30

N_ROPE, N_RAW, N_CONV = 10, 18, 8
Z_TILES = N_ROPE + N_RAW + N_CONV
PROJ_UNITS = 1 + Z_TILES
U_PROJ = FFN_UNITS
U_BLK = U_PROJ + PROJ_UNITS
U_MERGE = U_BLK + 2 * NB
U_FFN2 = U_MERGE + 3 * KT
M_PROJ = 2 * FT
M_BLK = M_PROJ + PROJ_UNITS
M_MERGE = M_BLK + 2 * NB
M_FFN2 = M_MERGE + 3 * KT


class Lin:
    def __init__(self, reg, m=1, a=0):
        self.reg, self.m, self.a = reg, m, a

    def __mul__(self, k):
        return Lin(self.reg, self.m * k, self.a * k)

    def __add__(self, k):
        return Lin(self.reg, self.m, self.a + k)

    __radd__ = __add__

    def __sub__(self, k):
        return self + -k


def val(v):
    return v.reg * v.m + v.a if isinstance(v, Lin) else v


def hybrid_layer(nc, w_stream, x_t, cols, ident_d, sinks, rope_cs, masks, mask_big, sel_head, sel_last,
                 out, zs, gs, att_s, mem_s, x_s):
    with ExitStack() as ctx:
        e = ctx.enter_context
        base = [(nc.sbuf_base + 31) // 32 * 32]

        def at(name, shape, dt, offset):
            return nc.alloc_sbuf_tensor_at(name, shape, dt, offset=offset)

        def sb(name, shape, dt):
            t = at(name, shape, dt, base[0])
            size = 4
            for n in shape[1:]:
                size *= n
            base[0] += (size + 31) // 32 * 32
            return t

        x = sb("x", [P, KT, S], F32)
        ra_hi = sb("ra_hi", [P, KT, S], F32R)
        ra_lo = sb("ra_lo", [P, KT, S], F32R)
        rb_base = base[0]
        rb_hi = sb("rb_hi", [P, KT, S], F32R)
        rb_lo = sb("rb_lo", [P, KT, S], F32R)
        w_raw = [sb(f"w_raw{i}", [P, D], F32) for i in range(2)]
        w_hi = [sb(f"w_hi{i}", [P, D], F32R) for i in range(2)]
        w_lo = [sb(f"w_lo{i}", [P, D], F32R) for i in range(2)]
        rstd_b = sb("rstd_b", [P, S], F32)
        t_a = sb("t_a", [P, S], F32)
        t_b = sb("t_b", [P, S], F32)
        sq = [sb("sq", [P, S], F32), t_a]
        sqacc = sb("sqacc", [P, S], F32)
        col = sb("col", [P, N_COLS], F32)
        ident = sb("ident", [P, P], F32)
        ones = sb("ones", [P, 1], F32)
        root = sb("root", [P, KT], F32)
        ssv = sb("ssv", [P, KT], F32)
        rstd_c = sb("rstd_c", [P, KT], F32)
        assert base[0] <= nc.sbuf_usable_end

        ps = [e(nc.psum_tensor(f"ps{i}", [P, S], F32)) for i in range(4)]

        def sem(name):
            return e(nc.semaphore(name))

        s_const = sem("s_const")
        s_x = [sem(f"s_x{i}") for i in range(KT)]
        s_ones = sem("s_ones")
        s_w = [sem(f"s_w{i}") for i in range(2)]
        s_whi = sem("s_whi")
        s_wlo = sem("s_wlo")
        s_unit = sem("s_unit")
        s_gs = sem("s_gs")
        s_silu = sem("s_silu")
        s_us = sem("s_us")
        s_h = sem("s_h")
        s_hhi = sem("s_hhi")
        s_hlo = sem("s_hlo")
        s_down = sem("s_down")
        s_xadd = sem("s_xadd")
        s_ahi = sem("s_ahi")
        s_alo = sem("s_alo")
        s_sq = sem("s_sq")
        s_acc = sem("s_acc")
        s_ss = sem("s_ss")
        s_root = sem("s_root")
        s_nr = sem("s_nr")
        s_rc = sem("s_rc")
        s_rbc = sem("s_rbc")
        s_rb = sem("s_rb")
        s_out = sem("s_out")
        s_fin = sem("s_fin")

        def load_unit(sp, n, slot, first=False):
            if not first:
                sp.wait_ge(s_wlo, val(n - 1))
            sp.dma_start(w_raw[slot][:], w_stream[val(n)]).then_inc(s_w[slot], 16)

        def load_units(sp, start, count):
            with sp.Fori(0, count // 2) as reg:
                i = Lin(reg)
                for j in range(2):
                    load_unit(sp, i * 2 + (start + j), (start + j) % 2)
            if count % 2:
                load_unit(sp, start + count - 1, (start + count - 1) % 2)

        def split_hi(act, n, slot, done=None):
            act.wait_ge(s_w[slot], val((n - slot) * 8 + 16 if isinstance(n, int) else n * 8 + (16 - 8 * slot)))
            if done is not None:
                act.wait_ge(done[0], val(done[1]))
            nc.scalar.copy(w_hi[slot][:], w_raw[slot][:]).then_inc(s_whi, 1)

        def split_lo(dve, n, slot):
            dve.wait_ge(s_whi, val(n + 1))
            nc.vector.tensor_tensor(w_lo[slot][:], w_raw[slot][:], w_hi[slot][:].bitcast(F32),
                                    ALU.subtract).then_inc(s_wlo, 1)

        def products(pe, out_ps, slot, hi, lo, k_wait=None, ks=(0, KT)):
            for k in range(*ks):
                if k_wait is not None:
                    pe.wait_ge(k_wait[0], val(k_wait[1] + k + 1))
                w = slice(k * P, (k + 1) * P)
                for i, (wt, a) in enumerate(((w_hi, hi), (w_hi, lo), (w_lo, hi))):
                    for t in range(2):
                        mm = nc.tensor.matmul(out_ps[:, t * HALF:(t + 1) * HALF], wt[slot][:, w],
                                              a[:, k, t * HALF:(t + 1) * HALF],
                                              start=(k == 0 and i == 0), stop=(k == KT - 1 and i == 2))
            if ks[1] == KT:
                mm.then_inc(s_unit, 1)

        def pe_sums(pe, norm):
            pe.wait_ge(s_acc, KT * (norm + 1) - (norm == 3))
            for j in range(KT):
                mm = nc.tensor.matmul(ps[2][:, j:j + 1], sqacc[:, j * P:(j + 1) * P], ones[:],
                                      start=(j == 0), stop=(norm < 3), skip_group_check=True)
            if norm == 3:
                pe.wait_ge(s_sq, (KT - 1) * (norm + 1))
                for j in range(KT):
                    mm = nc.tensor.matmul(ps[2][:, j:j + 1], sq[(KT - 2) % 2][:, j * P:(j + 1) * P], ones[:],
                                          start=False, stop=True, skip_group_check=True)
            mm.then_inc(s_ss, 1)

        def pe_spread(pe, norm):
            pe.wait_ge(s_rc, val(norm + 1))
            for j in range(KT):
                mm = nc.tensor.matmul(ps[3][:, j * P:(j + 1) * P],
                                      rstd_c[:, j:j + 1].to_broadcast([P, P]), ident[:],
                                      start=(j % 4 == 0), stop=True, skip_group_check=True)
                if j == KT - 1 or (norm == 3 and j == KT // 2 - 1):
                    mm.then_inc(s_rbc, 1)

        def act_norm_tile(act, norm, d, hi, ready):
            act.wait_ge(ready[0], ready[1])
            if hi is not None:
                g = C_GAIN + norm * KT + d
                nc.scalar.activation(hi[:, d, :], x[:, d, :], ACT.Copy,
                                     scale=col[:, g:g + 1]).then_inc(s_ahi, 1)
            if d == 0:
                if norm > 0:
                    act.wait_ge(s_ss, norm)
                nc.scalar.activation(sqacc[:], x[:, d, :], ACT.Square).then_inc(s_acc, 1)
            else:
                if d >= 3:
                    act.wait_ge(s_acc, KT * norm + d - 1)
                nc.scalar.activation(sq[(d - 1) % 2][:], x[:, d, :], ACT.Square).then_inc(s_sq, 1)

        def act_root(act, norm):
            act.wait_ge(s_ss, val(norm + 1))
            nc.scalar.activation(root[:], ps[2][:, 0:KT], ACT.Sqrt, bias=col[:, C_EPS:C_EPS + 1],
                                 scale=1.0 / D).then_inc(s_root, 1)

        def act_stats(act, norm):
            act_root(act, norm)
            act.wait_ge(s_rbc, val(norm + 1))
            nc.scalar.copy(rstd_b[:], ps[3][:]).then_inc(s_rb, 1)

        def dve_norm_tile(dve, norm, d, hi, lo):
            g = C_GAIN + norm * KT + d
            dve.wait_ge(s_ahi, val(KT * norm + d + 1))
            nc.vector.scalar_tensor_tensor(lo[:, d, :], x[:, d, :], col[:, g:g + 1],
                                           hi[:, d, :].bitcast(F32), ALU.mult,
                                           ALU.subtract).then_inc(s_alo, 1)

        def dve_stats(dve, norm):
            dve.wait_ge(s_root, val(norm + 1))
            nc.vector.reciprocal(rstd_c[:], root[:]).then_inc(s_nr, 1)
            nc.vector.tensor_scalar(ssv[:], ps[2][:, 0:KT], 1.0 / D, EPS, ALU.mult, ALU.add).then_inc(s_nr, 1)
            dve.wait_ge(s_nr, 5 * norm + 2)
            nc.vector.tensor_tensor(ssv[:], ssv[:], rstd_c[:], ALU.mult).then_inc(s_nr, 1)
            dve.wait_ge(s_nr, 5 * norm + 3)
            nc.vector.tensor_tensor(ssv[:], ssv[:], rstd_c[:], ALU.mult).then_inc(s_nr, 1)
            dve.wait_ge(s_nr, 5 * norm + 4)
            nc.vector.tensor_scalar(ssv[:], ssv[:], -0.5, 1.5, ALU.mult, ALU.add).then_inc(s_nr, 1)
            dve.wait_ge(s_nr, 5 * norm + 5)
            nc.vector.tensor_tensor(rstd_c[:], rstd_c[:], ssv[:], ALU.mult).then_inc(s_rc, 1)

        def pool_norm(pool, norm):
            for d in range(1, KT - (norm == 3)):
                pool.wait_ge(s_sq, (KT - 1) * norm + d)
                pool.wait_ge(s_acc, KT * norm + d)
                nc.gpsimd.tensor_tensor(sqacc[:], sqacc[:], sq[(d - 1) % 2][:], ALU.add).then_inc(s_acc, 1)

        class Ffn:
            def __init__(self, index, unit0, m0, norm, act, hidden):
                self.unit0, self.m0, self.norm = unit0, m0, norm
                self.hi, self.lo = act
                self.h_hi, self.h_lo = hidden
                self.f0 = FT * index
                self.a0 = PAIRS * KT * index

            def slot(self, n):
                return (self.unit0 + n) % 2

        def pe_down(pe, o, n, slot, p, par, half, first=False):
            pe.wait_ge(s_wlo, val(n + 1))
            pe.wait_ge(s_hlo, val(p * 2 + (o.f0 + 2)))
            for dd in range(4):
                d_ps = ps[2 + dd % 2]
                if not (first and dd < 2):
                    pe.wait_ge(s_xadd, val(p * KT + (o.a0 + 4 * half + dd - 1)))
                for j in range(2):
                    w = slice(j * HALF + dd * P, j * HALF + (dd + 1) * P)
                    for i, (wt, h) in enumerate(((w_hi, o.h_hi), (w_hi, o.h_lo), (w_lo, o.h_hi))):
                        for t in range(2):
                            mm = nc.tensor.matmul(d_ps[:, t * HALF:(t + 1) * HALF], wt[slot][:, w],
                                                  h[:, 2 * par + j, t * HALF:(t + 1) * HALF],
                                                  start=(j == 0 and i == 0), stop=(j == 1 and i == 2))
                mm.then_inc(s_down, 1)

        def pe_ffn(pe, o):
            for n in range(4):
                pe.wait_ge(s_wlo, val(o.unit0 + n + 1))
                if o.norm == 2 and n < 2:
                    pe.wait_ge(s_xfin, KT - 1 + n)
                if n == 2:
                    pe.wait_ge(s_root, val(o.norm + 1))
                if n == 3:
                    pe.wait_ge(s_rb, val(o.norm + 1))
                if n == 0:
                    products(pe, ps[0], o.slot(0), o.hi, o.lo, k_wait=(s_alo, KT * o.norm))
                elif n == 1:
                    products(pe, ps[1], o.slot(1), o.hi, o.lo, ks=(0, 3))
                    pe_sums(pe, o.norm)
                    products(pe, ps[1], o.slot(1), o.hi, o.lo, ks=(3, 6))
                    pe_spread(pe, o.norm)
                    products(pe, ps[1], o.slot(1), o.hi, o.lo, ks=(6, KT))
                else:
                    products(pe, ps[n], o.slot(n), o.hi, o.lo)

            def pair(n, p, par, first=False):
                for j in range(2):
                    pe.wait_ge(s_wlo, val(n + (3 * j + 1)))
                    pe.wait_ge(s_gs, val(p * 2 + (o.f0 + j)))
                    products(pe, ps[0], o.slot(j), o.hi, o.lo)
                    pe.wait_ge(s_wlo, val(n + (3 * j + 2)))
                    pe.wait_ge(s_us, val(p * 2 + (o.f0 + j)))
                    products(pe, ps[1], o.slot(j + 1), o.hi, o.lo)
                    pe_down(pe, o, n + (3 * j + 2), o.slot(j), p - 1, 1 - par, j, first and j == 0)

            pair(o.unit0 + 4, 1, 1, first=True)
            pair(o.unit0 + 10, 2, 0)
            with pe.Fori(0, (PAIRS - 3) // 2) as reg:
                i = Lin(reg)
                for j in range(2):
                    pair(i * 12 + (o.unit0 + 16 + 6 * j), i * 2 + (3 + j), 1 - j)
            for half in range(2):
                pe_down(pe, o, o.unit0 + FFN_UNITS - 2 + half, o.slot(half), PAIRS - 1, 0, half)

        def act_silu(act, o, f):
            act.wait_ge(s_gs, val(f + (o.f0 + 1)))
            nc.scalar.activation(t_a[:], t_a[:], ACT.Silu).then_inc(s_silu, 1)

        def act_hhi(act, o, f, hslot):
            act.wait_ge(s_h, val(f + (o.f0 + 1)))
            nc.scalar.copy(o.h_hi[:, hslot, :], t_b[:]).then_inc(s_hhi, 1)

        def act_ffn(act, o, tail):
            for n in range(4):
                split_hi(act, o.unit0 + n + 2, o.slot(n), (s_unit, o.m0 + n + 1))
                if n == 0:
                    act_stats(act, o.norm)
                if n % 2 == 0:
                    act_silu(act, o, n // 2)
                else:
                    act_hhi(act, o, n // 2, n // 2)

            def pair(n, p, par, last=False):
                for j in range(2):
                    f = p * 2 + j
                    split_hi(act, n + (3 * j + 2), o.slot(j), (s_unit, p * 4 + (o.m0 + 2 * j + 1)))
                    act_silu(act, o, f)
                    split_hi(act, n + (3 * j + 3), o.slot(j + 1), (s_unit, p * 4 + (o.m0 + 2 * j + 2)))
                    act_hhi(act, o, f, 2 * par + j)
                    if not (last and j == 1):
                        split_hi(act, n + (3 * j + 4), o.slot(j), (s_down, p * KT + (o.a0 + 4 * j - 4)))

            pair(o.unit0 + 4, 1, 1)
            pair(o.unit0 + 10, 2, 0)
            with act.Fori(0, (PAIRS - 3) // 2) as reg:
                i = Lin(reg)
                for j in range(2):
                    pair(i * 12 + (o.unit0 + 16 + 6 * j), i * 2 + (3 + j), 1 - j)
            tail(act)

        def dve_gs(dve, o, f, src, wait):
            if wait:
                dve.wait_ge(s_h, val(f + o.f0))
            nc.vector.tensor_tensor(t_a[:], src[:], rstd_b[:], ALU.mult).then_inc(s_gs, 1)

        def dve_us(dve, o, f, src, wait):
            if wait:
                dve.wait_ge(s_hlo, val(f + o.f0))
            nc.vector.tensor_tensor(t_b[:], src[:], rstd_b[:], ALU.mult).then_inc(s_us, 1)

        def dve_h(dve, o, f):
            dve.wait_ge(s_silu, val(f + (o.f0 + 1)))
            dve.wait_ge(s_us, val(f + (o.f0 + 1)))
            nc.vector.tensor_tensor(t_b[:], t_b[:], t_a[:], ALU.mult).then_inc(s_h, 1)

        def dve_hlo(dve, o, f, hslot):
            dve.wait_ge(s_hhi, val(f + (o.f0 + 1)))
            nc.vector.tensor_tensor(o.h_lo[:, hslot, :], t_b[:], o.h_hi[:, hslot, :].bitcast(F32),
                                    ALU.subtract).then_inc(s_hlo, 1)

        def dve_xadd(dve, o, p, d):
            dve.wait_ge(s_down, val(p * KT + (o.a0 + d + 1)))
            dve.wait_ge(s_xadd, val(p * KT + (o.a0 + d - 7) if not isinstance(p, int) or p else o.a0))
            nc.vector.scalar_tensor_tensor(x[:, d, :], ps[2 + d % 2][:], 0.5, x[:, d, :],
                                           ALU.mult, ALU.add).then_inc(s_xadd, 1)

        def dve_ffn(dve, o, tail):
            if o.norm == 2:
                dve.wait_ge(s_xfin, KT)
            for n in range(4):
                split_lo(dve, o.unit0 + n + 2, o.slot(n))
                if n == 0:
                    dve_stats(dve, o.norm)
                    dve.wait_ge(s_rb, val(o.norm + 1))
                if n % 2 == 0:
                    dve_gs(dve, o, n // 2, ps[n], n > 0)
                else:
                    dve_us(dve, o, n // 2, ps[n], n > 1)
                    dve_h(dve, o, n // 2)
                    dve_hlo(dve, o, n // 2, n // 2)

            def pair(n, p, par, last=False):
                for j in range(2):
                    f = p * 2 + j
                    split_lo(dve, n + (3 * j + 2), o.slot(j))
                    dve.wait_ge(s_unit, val(p * 4 + (o.m0 + 2 * j + 1)))
                    dve_gs(dve, o, f, ps[0], True)
                    split_lo(dve, n + (3 * j + 3), o.slot(j + 1))
                    dve.wait_ge(s_unit, val(p * 4 + (o.m0 + 2 * j + 2)))
                    dve_us(dve, o, f, ps[1], True)
                    dve_xadd(dve, o, p - 1, 4 * j)
                    dve_h(dve, o, f)
                    dve_xadd(dve, o, p - 1, 4 * j + 1)
                    dve_hlo(dve, o, f, 2 * par + j)
                    for dd in range(2, 4):
                        dve_xadd(dve, o, p - 1, 4 * j + dd)
                    split_lo(dve, n + (3 * j + 4), o.slot(j))

            pair(o.unit0 + 4, 1, 1)
            pair(o.unit0 + 10, 2, 0)
            with dve.Fori(0, (PAIRS - 3) // 2) as reg:
                i = Lin(reg)
                for j in range(2):
                    pair(i * 12 + (o.unit0 + 16 + 6 * j), i * 2 + (3 + j), 1 - j)
            tail(dve)

        def dve_ffn_tail(dve, o, hi, lo):
            p = PAIRS - 1
            for d in range(KT):
                dve_xadd(dve, o, p, d)
                if hi is not None:
                    if d > 0:
                        dve_norm_tile(dve, o.norm + 1, d - 1, hi, lo)
                    if d == 3 or d == 7:
                        split_lo(dve, o.unit0 + FFN_UNITS + d // 4, o.slot(d // 4))
            if hi is not None:
                dve_norm_tile(dve, o.norm + 1, KT - 1, hi, lo)

        def act_ffn_tail(act, o, hi):
            last = o.a0 + KT * (PAIRS - 1)
            for d in range(KT):
                act_norm_tile(act, o.norm + 1, d, hi, (s_xadd, last + d + 1))
                if hi is not None and (d == 3 or d == 7):
                    split_hi(act, o.unit0 + FFN_UNITS + d // 4, o.slot(d // 4), (s_down, last + d + 1))


        def region(start, end):
            top = [start]

            def take(name, shape, dt=F32):
                size = 4
                for n in shape[1:]:
                    size *= n
                t = at(name, shape, dt, top[0])
                top[0] += (size + 31) // 32 * 32
                assert top[0] <= end, (name, top[0] - end)
                return t
            return take

        x_base = rb_base - 3 * KT * S * 4
        xr = region(x_base, x_base + KT * S * 4)
        m_rows = xr("m_rows", [MH, S])
        cb_all = xr("cb_all", [P, NB, 5, MH])
        mk0 = xr("mk0", [P, 2 * P])
        mk = xr("mk", [P, 2 * P])
        sinkc = xr("sinkc", [P, HEADS])
        sink8 = xr("sink8", [P, HEADS])
        mbig = xr("mbig", [P, P])
        selh = xr("selh", [MH, MH, P])
        sell = xr("sell", [P, P])
        

        pr = region(rb_base, rb_base + 2 * KT * S * 4)
        rope_c = pr("rope_c", [P, S])
        rope_s = pr("rope_s", [P, S])
        z = [pr(f"z{i}", [P, S + 4]) for i in range(2)]
        swapped = pr("swapped", [P, S])
        y = [pr(f"y{i}", [P, S]) for i in range(2)]
        rz_i = pr("rz_i", [MH, S])
        rz_f = pr("rz_f", [MH, S])
        r_t = pr("r_t", [MH, S])
        r_b = pr("r_b", [MH, S])
        r_d = pr("r_d", [MH, S])
        r_mp = pr("r_mp", [MH, NB])
        rows = pr("rows", [P, S])

        k_hi = xr("k_hi", [P, KV_HEADS, 2 * P], F32R)
        k_lo = xr("k_lo", [P, KV_HEADS, 2 * P], F32R)
        zv = xr("zv", [P, 2, P])
        vnat = xr("vnat", [P, 2, KV_HEADS, 2, HD])
        nd = xr("nd", [P, MH, NA + 1])
        cst = xr("cst", [P, MH, NA + 1])
        br = region(rb_base, rb_base + 2 * KT * S * 4)
        zq = br("zq", [P, HEADS, P])
        q_hl = br("q_hl", [P, HEADS, P], F32R)
        zk = br("zk", [P, KV_HEADS, P])
        zm = br("zm", [P, 16, P])
        ot = br("ot", [P, KT, P])
        sm = [br(f"sm{i}", [P, S]) for i in range(2)]
        ptb = [br(f"ptb{i}", [P, S]) for i in range(2)]
        vmn = br("vmn", [P, MH, NA + 1])
        dm = br("dm", [P, MH * P])
        dt_ = br("dt", [P, MH * P])
        ptm = br("ptm", [P, MH * P])
        tmp = [br(f"tmp{i}", [P, NA + 1]) for i in range(2)]
        hn, ht = sq[0], sqacc
        ka = br("ka", [P, MH * P])
        turn = br("turn", [P, 1])
        mx = br("mx", [P, HEADS])
        nm = br("nm", [P, HEADS])
        sn = br("sn", [P, HEADS])
        es = br("es", [P, HEADS])
        rs = br("rs", [P, HEADS])
        rd = br("rd", [P, HEADS])
        cb = br("cb", [P, 5, MH])
        dn = br("dn", [P, MH])
        rn = br("rn", [P, MH])
        ssq = br("ssq", [P, MH])
        var = br("var", [P, MH])
        half_var = br("half_var", [P, MH])
        three_halves = br("three_halves", [P, MH])
        lv = br("lv", [P, MH])
        y0 = br("y0", [P, MH])
        yy = br("yy", [P, MH])
        yc = br("yc", [P, MH])
        scl = br("scl", [P, MH])

        s_cs = sem("s_cs")
        s_bconst = sem("s_bconst")
        s_xs = sem("s_xs")
        s_z = sem("s_z")
        s_pad = sem("s_pad")
        s_swap = sem("s_swap")
        s_rm = sem("s_rm")
        s_cv = sem("s_cv")
        s_csilu = sem("s_csilu")
        s_y = sem("s_y")
        s_st = [sem(f"s_st{i}") for i in range(2)]
        s_row = sem("s_row")
        s_rowa = sem("s_rowa")
        s_rt = sem("s_rt")
        s_cb = sem("s_cb")
        s_so = sem("s_so")
        s_sos = sem("s_sos")

        N_BCONST = 6

        def pe_proj(pe):
            pe.wait_ge(s_wlo, U_PROJ + 1)
            products(pe, ps[0], U_PROJ % 2, ra_hi, ra_lo, k_wait=(s_alo, KT))

            def units(first, count):
                with pe.Fori(0, count // 2) as reg:
                    i = Lin(reg, 2)
                    for j in range(2):
                        ee = i + (first + j)
                        pe.wait_ge(s_wlo, val(ee + (U_PROJ + 1)))
                        if first + j >= 2:
                            pe.wait_ge(s_z, val(ee - 1))
                        products(pe, ps[(first + j) % 2], (U_PROJ + first + j) % 2, ra_hi, ra_lo)

            pe.wait_ge(s_wlo, U_PROJ + 2)
            products(pe, ps[1], (U_PROJ + 1) % 2, ra_hi, ra_lo, ks=(0, 2))
            pe_sums(pe, 1)
            products(pe, ps[1], (U_PROJ + 1) % 2, ra_hi, ra_lo, ks=(2, 5))
            pe_spread(pe, 1)
            products(pe, ps[1], (U_PROJ + 1) % 2, ra_hi, ra_lo, ks=(5, KT))
            pe.wait_ge(s_wlo, U_PROJ + 3)
            pe.wait_ge(s_z, 1)
            products(pe, ps[0], U_PROJ % 2, ra_hi, ra_lo)
            units(3, 24)
            pe.wait_ge(s_rowa, 6)
            for c in range(NB):
                mm = nc.tensor.transpose(ps[2][:, c * P:(c + 1) * P], rows[:, c * P:(c + 1) * P], ident[:])
            mm.then_inc(s_rt, 1)
            units(27, 4)
            pe.wait_ge(s_cb, 1)
            pe.wait_ge(s_bconst, 16 * N_BCONST)
            nc.tensor.matmul(ps[3][:, 0:NB * MH], sell[:], cb_all[:, :, 2, :], start=True,
                             stop=True).then_inc(s_so, 1)
            units(31, 6)

        def act_rope(act, ee, par, first=False):
            act.wait_ge(s_z, val(ee + 1))
            if not first:
                act.wait_ge(s_y, val(ee - 1))
            for q in range(4):
                o = q ^ 1
                nc.scalar.copy(swapped[32 * q:32 * q + 32, :],
                               z[par][32 * o:32 * o + 32, 3:3 + S]).then_inc(s_swap, 1)

        def act_proj(act):
            split_hi(act, U_PROJ + 2, U_PROJ % 2, (s_unit, M_PROJ + 1))
            act_stats(act, 1)
            for ee in (1, 2):
                split_hi(act, ee + U_PROJ + 2, ee % 2, (s_unit, ee + M_PROJ + 1))
                act_rope(act, ee, ee % 2, first=ee == 1)
            with act.Fori(0, N_ROPE // 2 - 1) as reg:
                for j in range(2):
                    ee = Lin(reg, 2, 3 + j)
                    split_hi(act, ee + (U_PROJ + 2), (1 + j) % 2, (s_unit, ee + (M_PROJ + 1)))
                    act_rope(act, ee, (1 + j) % 2)

            def raw(first, count):
                with act.Fori(0, count // 2) as reg:
                    for j in range(2):
                        ee = Lin(reg, 2, first + j)
                        split_hi(act, ee + (U_PROJ + 2), (first + j) % 2, (s_unit, ee + (M_PROJ + 1)))

            raw(11, 2)
            with act.Fori(0, N_CONV // 2) as reg:
                for j in range(2):
                    ee = Lin(reg, 2, 13 + j)
                    split_hi(act, ee + (U_PROJ + 2), (13 + j) % 2, (s_unit, ee + (M_PROJ + 1)))
                    act.wait_ge(s_cv, val(Lin(reg, 8, 4 * j + 4)))
                    if j == 0:
                        nc.scalar.activation(y[1][:], y[1][:], ACT.Silu).then_inc(s_y, 1)
                    else:
                        nc.scalar.activation(y[0][:], y[0][:], ACT.Silu).then_inc(s_csilu, 1)
                        act.wait_ge(s_csilu, val(Lin(reg, 1, 1)))
                        nc.scalar.activation(y[0][:], y[0][:], ACT.Copy,
                                             scale=float(DK) ** -0.5).then_inc(s_y, 1)
            raw(21, 2)
            act_rows1(act)
            raw(23, 2)
            act_rows2(act)
            raw(25, 10)
            act.wait_ge(b["init"], 5)
            act_keys(act, 0)
            raw(35, 2)

        def act_rows1(act):
            act.wait_ge(s_row, 3)
            nc.scalar.activation(r_t[:], rz_f[:], ACT.Abs).then_inc(s_rowa, 1)
            act.wait_ge(s_rowa, 1)
            nc.scalar.activation(r_t[:], r_t[:], ACT.Exp, scale=-1.0).then_inc(s_rowa, 1)
            act.wait_ge(s_rowa, 2)
            nc.scalar.activation(r_t[:], r_t[:], ACT.Ln, bias=1.0).then_inc(s_rowa, 1)

        def act_rows2(act):
            for i, (q, scale) in enumerate(((32, 1.0), (64, 1.0), (96, -1.0))):
                act.wait_ge(s_row, 17)
                nc.scalar.activation(rows[q:q + MH, :], rows[q:q + MH, :], ACT.Exp,
                                     scale=scale).then_inc(s_rowa, 1)

        def dve_rows0(dve):
            dve.wait_ge(s_unit, M_PROJ + 1)
            nc.vector.tensor_tensor(rz_f[:], ps[0][32:32 + MH, :], rstd_b[32:32 + MH, :],
                                    ALU.mult).then_inc(s_row, 1)
            dve.wait_ge(s_row, 1)
            nc.vector.tensor_tensor(rz_i[:], ps[0][0:MH, :], rstd_b[0:MH, :], ALU.mult).then_inc(s_z, 1)

        def dve_rows1(dve):
            dve.wait_ge(s_z, 1)
            nc.vector.tensor_scalar(rz_i[:], rz_i[:], col[0:MH, C_BI:C_BI + 1], None,
                                    ALU.add).then_inc(s_row, 1)
            nc.vector.tensor_scalar(rz_f[:], rz_f[:], col[0:MH, C_BF:C_BF + 1], None,
                                    ALU.add).then_inc(s_row, 1)
            nc.vector.memset(rows[:], 0.0).then_inc(s_row, 1)
            nc.vector.memset(r_d[:], 1.0).then_inc(s_row, 1)
            dve.wait_ge(s_row, 5)
            d_starts = r_d[:].rearrange("h (c l) -> h c l", l=P)
            nc.vector.memset(d_starts[:, :, 0:1], 0.0).then_inc(s_row, 1)
            nc.vector.memset(r_mp[:], 0.0).then_inc(s_row, 1)

        def dve_rows2(dve):
            chunk = lambda t: t[:].rearrange("h (c l) -> h c l", l=P)
            dve.wait_ge(s_rowa, 3)
            dve.wait_ge(s_row, 7)
            nc.vector.scalar_tensor_tensor(rz_f[:], rz_f[:], 0.0, r_t[:], ALU.min,
                                           ALU.subtract).then_inc(s_row, 1)
            dve.wait_ge(s_row, 8)
            nc.vector.tensor_tensor_scan(r_b[:], r_d[:], rz_f[:], 0.0, ALU.mult,
                                         ALU.add).then_inc(s_row, 1)
            dve.wait_ge(s_row, 9)
            nc.vector.tensor_tensor(rows[0:MH, :], rz_i[:], r_b[:], ALU.subtract).then_inc(s_row, 1)
            nc.vector.memset(r_d[:], 0.0).then_inc(s_row, 1)
            dve.wait_ge(s_row, 11)
            nc.vector.tensor_copy(chunk(r_d)[:, 1:, 0:1], chunk(r_b)[:, :-1, P - 1:P]).then_inc(s_row, 1)
            dve.wait_ge(s_row, 12)
            dve.wait_ge(s_xs, 16 * KT)
            nc.vector.tensor_tensor_scan(m_rows[:], r_d[:], rows[0:MH, :], 0.0, ALU.add,
                                         ALU.max).then_inc(s_row, 1)

        def dve_rows3(dve):
            chunk = lambda t: t.rearrange("h (c l) -> h c l", l=P)
            dve.wait_ge(s_row, 13)
            mc, bc = chunk(m_rows[:]), chunk(r_b[:])
            nc.vector.tensor_tensor(r_mp[:, 1:].unsqueeze(2), mc[:, :-1, P - 1:P], bc[:, :-1, P - 1:P],
                                    ALU.add).then_inc(s_row, 1)
            nc.vector.tensor_tensor(chunk(rows[32:32 + MH, :]), chunk(rows[0:MH, :]),
                                    mc[:, :, P - 1:P].to_broadcast([MH, NB, P]),
                                    ALU.subtract).then_inc(s_row, 1)
            nc.vector.tensor_tensor(rows[96:96 + MH, :], m_rows[:], r_b[:], ALU.add).then_inc(s_row, 1)
            dve.wait_ge(s_row, 16)
            nc.vector.tensor_tensor(chunk(rows[64:64 + MH, :]), r_mp[:].unsqueeze(2).to_broadcast([MH, NB, P]),
                                    mc, ALU.subtract).then_inc(s_row, 1)

        def dve_cols(dve):
            dve.wait_ge(s_rt, 1)
            nc.vector.tensor_copy(cb_all[:, :, 0:4, :],
                                  ps[2][:].rearrange("p (c k l) -> p c k l", c=NB, k=4)[:, :, :, 0:MH]
                                  ).then_inc(s_cb, 1)

        def dve_z(dve, ee, par):
            dve.wait_ge(s_unit, val(ee + (M_PROJ + 1)))
            nc.vector.tensor_tensor(z[par][:, 3:3 + S], ps[par][:], rstd_b[:], ALU.mult).then_inc(s_z, 1)

        def y_free(dve, ee, slot, peeled):
            if not peeled:
                dve.wait_ge(s_st[slot], val(ee * 8 + (-8 if slot else -16)))

        def dve_proj(dve):
            split_lo(dve, U_PROJ + 2, U_PROJ % 2)
            dve_stats(dve, 1)
            dve.wait_ge(s_rb, 2)
            dve_rows0(dve)
            nc.vector.memset(z[0][:, 0:3], 0.0).then_inc(s_pad, 1)
            nc.vector.memset(z[1][:, 0:3], 0.0).then_inc(s_pad, 1)
            dve.wait_ge(s_cs, 32)

            def rope(ee, par, peeled=False):
                split_lo(dve, ee + (U_PROJ + 2), par)
                if ee != 1:
                    dve.wait_ge(s_rm, val(ee * 2 - 2))
                dve_z(dve, ee, par)
                y_free(dve, ee, par, peeled)
                dve.wait_ge(s_z, val(ee + 1))
                nc.vector.tensor_tensor(y[par][:], z[par][:, 3:3 + S], rope_c[:], ALU.mult).then_inc(s_rm, 1)
                dve.wait_ge(s_swap, val(ee * 4))
                nc.vector.tensor_tensor(swapped[:], swapped[:], rope_s[:], ALU.mult).then_inc(s_rm, 1)
                dve.wait_ge(s_rm, val(ee * 2))
                nc.vector.tensor_tensor(y[par][:], y[par][:], swapped[:], ALU.add).then_inc(s_y, 1)

            def raw(ee, par):
                split_lo(dve, ee + (U_PROJ + 2), par)
                dve.wait_ge(s_unit, val(ee + (M_PROJ + 1)))
                y_free(dve, ee, par, False)
                nc.vector.tensor_tensor(y[par][:], ps[par][:], rstd_b[:], ALU.mult).then_inc(s_z, 1)

            rope(1, 1, True)
            rope(2, 0, True)
            with dve.Fori(0, N_ROPE // 2 - 1) as reg:
                for j in range(2):
                    rope(Lin(reg, 2, 3 + j), (1 + j) % 2)
            raw(11, 1)
            raw(12, 0)
            with dve.Fori(0, N_CONV // 2) as reg:
                for j in range(2):
                    ee, par = Lin(reg, 2, 13 + j), (1 + j) % 2
                    split_lo(dve, ee + (U_PROJ + 2), par)
                    dve.wait_ge(s_pad, 2)
                    dve_z(dve, ee, par)
                    y_free(dve, ee, par, False)
                    dve.wait_ge(s_z, val(ee + 1))
                    k0 = Lin(reg, 10, C_CONV + 5 * j)
                    c = lambda t: col[:, bass.ds(val(k0 + t), 1)]
                    nc.vector.tensor_scalar(y[par][:], z[par][:, 3:3 + S], c(3), c(4), ALU.mult,
                                            ALU.add).then_inc(s_cv, 1)
                    for t in (2, 1, 0):
                        dve.wait_ge(s_cv, val(Lin(reg, 8, 4 * j + 3 - t)))
                        nc.vector.scalar_tensor_tensor(y[par][:], z[par][:, t:t + S], c(t), y[par][:],
                                                       ALU.mult, ALU.add).then_inc(s_cv, 1)
            raw(21, 1)
            dve_rows1(dve)
            raw(22, 0)
            raw(23, 1)
            dve_rows2(dve)
            raw(24, 0)
            dve_rows3(dve)

            def raws(first, count):
                with dve.Fori(0, count // 2) as reg:
                    for j in range(2):
                        raw(Lin(reg, 2, first + j), (1 + j) % 2)

            raws(25, 4)
            dve_cols(dve)
            dve_block_init(dve)
            raws(29, 2)
            dve.wait_ge(s_so, 1)
            nc.vector.tensor_copy(cb_all[:, :, 4, :],
                                  ps[3][:, 0:NB * MH].rearrange("p (c h) -> p c h", c=NB)).then_inc(s_sos, 1)
            raws(31, 4)
            dve_keys(dve, 0)
            raws(35, 2)

        def sp_proj(sp):
            def store(ee, par, ready):
                sp.wait_ge(ready[0], val(ready[1]))
                sp.dma_start(zs[val(ee - 1)], y[par][:]).then_inc(s_st[par], 16)

            def tick(ee, k, ready):
                load_unit(sp, ee + (U_PROJ + 2), k % 2)
                store(ee - 1, 1 - k % 2, ready)

            sp.wait_ge(s_down, FT * KT // 2)
            sp.dma_start(rope_c[:], rope_cs[0]).then_inc(s_cs, 16)
            sp.dma_start(rope_s[:], rope_cs[1]).then_inc(s_cs, 16)
            load_unit(sp, U_PROJ + 2, U_PROJ % 2)
            load_unit(sp, U_PROJ + 3, (U_PROJ + 1) % 2)
            for d in range(KT):
                sp.wait_ge(s_xadd, PAIRS * KT - KT + d + 1)
                sp.dma_start(x_s[:, d, :], x[:, d, :]).then_inc(s_xs, 16)
            sp.wait_ge(s_xs, 16 * KT)
            for dst, src in ((mk0, masks[:, 0]), (mk, masks[:, 1]), (sinkc, sinks), (mbig, mask_big), (selh, sel_head),
                             (sell, sel_last)):
                sp.dma_start(dst[:], src).then_inc(s_bconst, 16)
            with sp.Fori(0, N_ROPE // 2) as reg:
                for j in range(2):
                    tick(Lin(reg, 2, 2 + j), j, (s_y, Lin(reg, 2, 1 + j)))
            for ee in (12, 13):
                tick(ee, ee, (s_z, ee))
            with sp.Fori(0, N_CONV // 2) as reg:
                for j in range(2):
                    tick(Lin(reg, 2, 14 + j), j, (s_y, Lin(reg, 2, N_ROPE + 1 + j)))
            for i in range(2):
                sp.wait_ge(s_st[i], 16 * 6)
            load_za(sp, 0)
            load_zv(sp, 0)
            with sp.Fori(0, N_RAW // 2 - 1) as reg:
                for j in range(2):
                    tick(Lin(reg, 2, 22 + j), j, (s_z, Lin(reg, 2, 22 + j)))


        names = ("zql zvl zml kp kh ql vt vn s sm nm sn p den rd pn pt pte pv on ots sc mb dm dx ptm vmt vme "
                 "kmt ka n1 n2 dc tmp nd c dd ssq lv hn htt hte hts gz init cbn vp klp ns").split()
        b = {name: sem(f"b_{name}") for name in names}
        s_gst = [sem(f"s_gst{i}") for i in range(2)]
        s_ld = [sem(f"s_ld{i}") for i in range(4)]
        s_fhi = sem("s_fhi")
        s_flo = sem("s_flo")
        att_stage = [sm[0], sm[1], ptb[0], ptb[1]]

        def lin(n, k, c):
            return n * k + c

        def pcol(g):
            return (g % 2) * HALF + (g // 2) * 2 * P

        def pe_htt(pe, n):
            pe.wait_ge(b["hn"], val(n))
            for t in range(KT):
                mm = nc.tensor.transpose(ps[3][:, t * P:(t + 1) * P], hn[:, t * P:(t + 1) * P], ident[:])
            mm.then_inc(b["htt"], 1)

        def pe_block(pe, n, first=False):
            def scores(j):
                for g in range(GROUP):
                    o = ps[1 + j % 2][:, pcol(g):pcol(g) + 2 * P]
                    nc.tensor.matmul(o, q_hl[:, GROUP * j + g, :], k_hi[:, j, :], start=True, stop=False,
                                     skip_group_check=True)
                    mm = nc.tensor.matmul(o, q_hl[0:HD, GROUP * j + g, :], k_lo[0:HD, j, :], start=False,
                                          stop=True, skip_group_check=True)
                mm.then_inc(b["s"], 1)

            def turn_p(j):
                pe.wait_ge(b["pn"], val(lin(n, 4, j + 1)))
                for t in range(1, 2 * GROUP, 2) if first else range(2 * GROUP):
                    mm = nc.tensor.transpose(ps[1 + j % 2][:, t * P:(t + 1) * P],
                                             sm[j % 2][:, t * P:(t + 1) * P], ident[:])
                mm.then_inc(b["pt"], 1)

            def weigh_v(j):
                pe.wait_ge(b["pte"], val(lin(n, 4, j + 1)))
                if j >= 2:
                    pe.wait_ge(b["on"], val(lin(n, 8, 2 * j - 2)))
                o = ps[3][:, (1 - j % 2) * HALF:(2 - j % 2) * HALF]
                p_t = ptb[j % 2][:].rearrange("p (g k q) -> p g k q", g=GROUP, k=2)
                for k in ((1,) if first else (0, 1)):
                    mm = nc.tensor.matmul(o.rearrange("p (g q) -> p g q", g=GROUP), vnat[:, k, j, :, :],
                                          p_t[:, :, k, :], start=(first or k == 0), stop=(k == 1))
                mm.then_inc(b["pv"], 1)

            def gate(c, k0, k1):
                if k0 == 0:
                    pe.wait_ge(s_wlo, val(lin(n, 2, U_BLK + c + 1)))
                products(pe, ps[0], (U_BLK + c) % 2, ra_hi, ra_lo, ks=(k0, k1))

            pe.wait_ge(b["ql"], val(lin(n, 2, 2)))
            if not first:
                pe.wait_ge(b["nd"], val(lin(n, 4, 0)))
            scores(0)
            if not first:
                pe.wait_ge(b["tmp"], val(lin(n, 4, 0)))
            scores(1)
            if first:
                pe.wait_ge(s_z, PROJ_UNITS)
            else:
                pe.wait_ge(b["gz"], val(lin(n, 2, 0)))
            gate(0, 0, 4)
            if not first:
                pe.wait_ge(b["c"], val(lin(n, 4, 0)))
                pe_htt(pe, n)
            turn_p(0)
            if not first:
                pe.wait_ge(b["hte"], val(n))
            pe.wait_ge(b["zvl"], val(lin(n, 16, 16)))
            for t in range(2):
                mm = nc.tensor.transpose(ps[3][:, t * P:(t + 1) * P], zv[:, t, :], ident[:])
            mm.then_inc(b["vt"], 1)
            turn_p(1)
            pe.wait_ge(b["vn"], val(lin(n, 1, 1)))
            weigh_v(0)
            scores(2)
            weigh_v(1)
            scores(3)
            gate(0, 4, 7)
            turn_p(2)
            gate(0, 7, 8)
            turn_p(3)
            weigh_v(2)
            pe.wait_ge(b["zml"], val(lin(n, 32, 32)))
            pe.wait_ge(b["gz"], val(lin(n, 2, 1)))
            for t in range(KT):
                mm = nc.tensor.transpose(ps[0][:, t * P:(t + 1) * P], zm[:, t, :], ident[:])
            mm.then_inc(b["vmt"], 1)
            for h in range(MH):
                mm = nc.tensor.matmul(ps[1][:, h * P:(h + 1) * P], selh[:, h, :],
                                      m_rows[:, bass.ds(val(lin(n, P, 0)), P)], start=True, stop=True,
                                      skip_group_check=True)
            mm.then_inc(b["mb"], 1)
            for h in range(MH):
                mm = nc.tensor.matmul(ps[1][:, HALF + h * P:HALF + (h + 1) * P], zm[:, KT + 2 * h + 1, :],
                                      zm[:, KT + 2 * h, :], start=True, stop=True, skip_group_check=True)
            mm.then_inc(b["sc"], 1)
            weigh_v(3)
            for h in range(MH):
                mm = nc.tensor.transpose(ps[2][:, h * P:(h + 1) * P], zm[:, KT + 2 * h + 1, :], ident[:])
            mm.then_inc(b["kmt"], 1)
            pe.wait_ge(b["vme"], val(lin(n, 1, 1)))
            gate(1, 0, 3)
            pe.wait_ge(b["ptm"], val(lin(n, 1, 1)))
            pe.wait_ge(b["on"], val(lin(n, 8, 8)))
            for h in range(MH):
                o = slice((h % 2) * HALF, (h % 2) * HALF + NA)
                if h == 2:
                    gate(1, 3, 5)
                if h >= 2:
                    pe.wait_ge(b["nd"], val(lin(n, 4, h - 1)))
                nc.tensor.matmul(ps[1][:, o], ptm[:, h * P:(h + 1) * P], vmn[:, h, 0:NA], start=True,
                                 stop=True).then_inc(b["n1"], 1)
                nc.tensor.matmul(ps[2][:, o], zm[:, KT + 2 * h, :], cst[:, h, 0:NA], start=True,
                                 stop=True).then_inc(b["n2"], 1)
                if h >= 2:
                    pe.wait_ge(b["c"], val(lin(n, 4, h - 1)))
                nc.tensor.matmul(ps[3][:, o], ka[:, h * P:(h + 1) * P], vmn[:, h, 0:NA], start=True,
                                 stop=True).then_inc(b["dc"], 1)
            gate(1, 5, 8)

        def act_keys(act, n):
            if not isinstance(n, int) or n:
                act.wait_ge(b["s"], val(lin(n, 4, 0)))
            act.wait_ge(b["zql"], val(lin(n, 128, 128)))
            nc.scalar.copy(k_hi[:, :, 0:P], k_hi[:, :, P:2 * P]).then_inc(b["kp"], 1)
            nc.scalar.copy(q_hl[:], zq[:]).then_inc(b["kh"], 1)
            act.wait_ge(b["kp"], val(lin(n, 1, 1)))
            nc.scalar.copy(k_hi[:, :, P:2 * P], zk[:]).then_inc(b["kh"], 1)

        def dve_keys(dve, n):
            dve.wait_ge(b["kh"], val(lin(n, 2, 2)))
            nc.vector.tensor_tensor(q_hl[HD:P, :, :], zq[HD:P, :, :], q_hl[HD:P, :, :].bitcast(F32),
                                    ALU.subtract).then_inc(b["ql"], 1)
            nc.vector.tensor_copy(k_lo[0:HD, :, 0:P], k_lo[0:HD, :, P:2 * P].bitcast(F32)).then_inc(b["klp"], 1)
            dve.wait_ge(b["klp"], val(lin(n, 1, 1)))
            nc.vector.tensor_tensor(k_lo[0:HD, :, P:2 * P], zk[0:HD], k_hi[0:HD, :, P:2 * P].bitcast(F32),
                                    ALU.subtract).then_inc(b["ql"], 1)

        def pool_hn(pool, n):
            pool.wait_ge(b["lv"], val(lin(n, 2, 0)))
            nc.gpsimd.tensor_tensor(yy[:], y0[:], y0[:], ALU.mult).then_inc(b["ns"], 1)
            pool.wait_ge(b["ns"], val(lin(n, 5, -4)))
            pool.wait_ge(b["dd"], val(lin(n, 5, 0)))
            nc.gpsimd.tensor_tensor(yy[:], yy[:], half_var[:], ALU.mult).then_inc(b["ns"], 1)
            pool.wait_ge(b["ns"], val(lin(n, 5, -3)))
            nc.gpsimd.tensor_tensor(yy[:], yy[:], three_halves[:], ALU.add).then_inc(b["ns"], 1)
            pool.wait_ge(b["ns"], val(lin(n, 5, -2)))
            nc.gpsimd.tensor_tensor(yc[:], yy[:], y0[:], ALU.mult).then_inc(b["ns"], 1)
            pool.wait_ge(b["ns"], val(lin(n, 5, -1)))
            nc.gpsimd.tensor_tensor(scl[:], yc[:], rn[:], ALU.mult).then_inc(b["ns"], 1)
            pool.wait_ge(b["ns"], val(lin(n, 5, 0)))
            nc.gpsimd.tensor_tensor(hn[:].rearrange("p (h v) -> p h v", h=MH), nd[:, :, 0:DV],
                                    scl[:].unsqueeze(2).to_broadcast([P, MH, DV]),
                                    ALU.mult).then_inc(b["hn"], 1)

        def act_hte(act, n):
            act.wait_ge(b["htt"], val(n))
            if not isinstance(n, int) or n > 1:
                act.wait_ge(b["hts"], val(lin(n, 16, -16)))
            nc.scalar.copy(ht[:], ps[3][:]).then_inc(b["hte"], 1)

        def act_att_hi(act, k):
            act.wait_ge(s_ld[k % 4], 16 * (k // 4 + 1))
            act.wait_ge(s_unit, M_MERGE)
            nc.scalar.copy(ra_hi[:, k, :], att_stage[k % 4][:]).then_inc(s_fhi, 1)

        def dve_att_lo(dve, k):
            dve.wait_ge(s_fhi, k + 1)
            nc.vector.tensor_tensor(ra_lo[:, k, :], att_stage[k % 4][:], ra_hi[:, k, :].bitcast(F32),
                                    ALU.subtract).then_inc(s_flo, 1)

        def load_att(sp, k):
            if k >= 4:
                sp.wait_ge(s_flo, k - 3)
            sp.dma_start(att_stage[k % 4][:], att_s[k, :, P:]).then_inc(s_ld[k % 4], 16)

        def act_block(act, n, first=False, last=False):
            def exps(j):
                act.wait_ge(b["nm"], val(lin(n, 4, j + 1)))
                for g in range(GROUP):
                    h = GROUP * j + g
                    p = sm[j % 2][:, pcol(g):pcol(g) + 2 * P]
                    nc.scalar.activation(p, p, ACT.Exp, bias=nm[:, h:h + 1], scale=HD ** -0.5,
                                         accum_out=rs[:, h:h + 1]).then_inc(b["p"], 1)
                act.wait_ge(b["sn"], val(lin(n, 4, j + 1)))
                q = slice(GROUP * j, GROUP * (j + 1))
                nc.scalar.activation(es[:, q], sn[:, q], ACT.Exp).then_inc(b["p"], 1)

            def take_p(j):
                act.wait_ge(b["pt"], val(lin(n, 4, j + 1)))
                if j >= 2:
                    act.wait_ge(b["pv"], val(lin(n, 4, j - 1)))
                nc.scalar.copy(ptb[j % 2][:], ps[1 + j % 2][:]).then_inc(b["pte"], 1)

            exps(0)
            exps(1)
            if not first:
                act_hte(act, n)
            take_p(0)
            if not first:
                split_hi(act, lin(n, 2, U_BLK + 1), (U_BLK + 1) % 2, (s_unit, lin(n, 2, M_BLK)))
            take_p(1)
            exps(2)
            exps(3)
            take_p(2)
            split_hi(act, lin(n, 2, U_BLK + 2), U_BLK % 2, (s_unit, lin(n, 2, M_BLK + 1)))
            take_p(3)
            act.wait_ge(b["vmt"], val(lin(n, 1, 1)))
            nc.scalar.copy(vmn[:, :, 0:DV], ps[0][:].rearrange("p (h v) -> p h v", h=MH)).then_inc(b["vme"], 1)
            act.wait_ge(b["dm"], val(lin(n, 1, 1)))
            for h in range(MH):
                q = slice(h * P, (h + 1) * P)
                nc.scalar.activation(dt_[:, q], dm[:, q], ACT.Exp, bias=cb[:, 0, h:h + 1],
                                     scale=-1.0).then_inc(b["dx"], 1)
            if not last:
                act_keys(act, n + 1)
            for h in range(MH):
                act.wait_ge(b["n2"], val(lin(n, 4, h + 1)))
                if h >= 2:
                    act.wait_ge(b["nd"], val(lin(n, 4, h - 1)))
                nc.scalar.activation(tmp[h % 2][:, 0:NA], ps[2][:, (h % 2) * HALF:(h % 2) * HALF + NA],
                                     ACT.Copy, scale=cb[:, 2, h:h + 1]).then_inc(b["tmp"], 1)
            act.wait_ge(b["dd"], val(lin(n, 5, 3)))
            for h in range(MH):
                nc.scalar.activation(hn[:, h * DV:(h + 1) * DV], nd[:, h, 0:DV], ACT.Square,
                                     scale=rn[:, h:h + 1], accum_out=ssq[:, h:h + 1]).then_inc(b["ssq"], 1)
            if last:
                for k in range(4):
                    act_att_hi(act, k)
            act.wait_ge(b["dd"], val(lin(n, 5, 4)))
            nc.scalar.activation(lv[:], var[:], ACT.Ln).then_inc(b["lv"], 1)
            act.wait_ge(b["lv"], val(lin(n, 2, 1)))
            nc.scalar.activation(y0[:], lv[:], ACT.Exp, scale=-0.5).then_inc(b["lv"], 1)

        def dve_block(dve, n, first=False, last=False):
            def maxima(j):
                dve.wait_ge(b["s"], val(lin(n, 4, j + 1)))
                nc.vector.memset(turn[:], 0.0)
                for g in range(GROUP):
                    h = GROUP * j + g
                    q = slice(pcol(g), pcol(g) + 2 * P)
                    nc.vector.tensor_tensor_reduce(sm[j % 2][:, q], ps[1 + j % 2][:, q], (mk0 if first else mk)[:],
                                                   1.0, sink8[:, h:h + 1], ALU.add, ALU.max,
                                                   mx[:, h:h + 1]).then_inc(b["sm"], 1)
                q = slice(GROUP * j, GROUP * (j + 1))
                dve.wait_ge(b["sm"], val(lin(n, 16, 4 * j + 4)))
                nc.vector.tensor_scalar(nm[:, q], mx[:, q], -HD ** -0.5, None, ALU.mult).then_inc(b["nm"], 1)
                dve.wait_ge(b["nm"], val(lin(n, 4, j + 1)))
                nc.vector.tensor_tensor(sn[:, q], sinkc[:, q], nm[:, q], ALU.add).then_inc(b["sn"], 1)

            def divisors(j):
                q = slice(GROUP * j, GROUP * (j + 1))
                dve.wait_ge(b["p"], val(lin(n, 20, 5 * j + 5)))
                nc.vector.tensor_tensor(rd[:, q], rs[:, q], es[:, q], ALU.add).then_inc(b["den"], 1)
                dve.wait_ge(b["den"], val(lin(n, 4, j + 1)))
                nc.vector.reciprocal(rd[:, q], rd[:, q]).then_inc(b["rd"], 1)
                dve.wait_ge(b["rd"], val(lin(n, 4, j + 1)))
                p = sm[j % 2][:].rearrange("p (a b k) -> p a b k", a=2, b=2)
                nc.vector.tensor_tensor(p, p, rd[:, q].rearrange("p (b a) -> p a b", a=2).unsqueeze(3)
                                        .to_broadcast([P, 2, 2, 2 * P]), ALU.mult).then_inc(b["pn"], 1)

            def outputs(j):
                dve.wait_ge(b["pv"], val(lin(n, 4, j + 1)))
                if j == 0:
                    if first:
                        dve.wait_ge(s_st[1], 16 * (Z_TILES // 2))
                    else:
                        dve.wait_ge(b["ots"], val(lin(n, 16, 0)))
                for a in range(2):
                    rows_a, c0 = slice(64 * a, 64 * a + 64), (1 - j % 2) * HALF + 2 * P * a
                    nc.vector.tensor_copy(ot[rows_a, 2 * j:2 * j + 2, :],
                                          ps[3][rows_a, c0:c0 + 2 * P].rearrange("p (t q) -> p t q", t=2)
                                          ).then_inc(b["on"], 1)

            maxima(0)
            maxima(1)
            divisors(0)
            divisors(1)
            nc.vector.tensor_copy(cb[:], cb_all[:, bass.ds(val(n), 1), :, :].rearrange("p c k h -> p (c k) h")
                                  ).then_inc(b["cbn"], 1)
            nc.vector.tensor_copy(vnat[:, 0], vnat[:, 1]).then_inc(b["vp"], 1)
            dve.wait_ge(b["vt"], val(lin(n, 1, 1)))
            dve.wait_ge(b["vp"], val(lin(n, 1, 1)))
            nc.vector.tensor_copy(vnat[:, 1], ps[3][:, 0:2 * P].rearrange("p (j v) -> p j v", j=KV_HEADS)
                                  .unsqueeze(2).to_broadcast([P, KV_HEADS, 2, HD])).then_inc(b["vn"], 1)
            outputs(0)
            maxima(2)
            outputs(1)
            maxima(3)
            divisors(2)
            divisors(3)
            dve.wait_ge(s_unit, val(lin(n, 2, M_BLK + 1)))
            if not first:
                dve.wait_ge(s_gst[0], val(lin(n, 16, 0)))
            nc.vector.tensor_tensor(t_a[:], ps[0][:], rstd_b[:], ALU.mult).then_inc(b["gz"], 1)
            if not first:
                split_lo(dve, lin(n, 2, U_BLK + 1), (U_BLK + 1) % 2)
            split_lo(dve, lin(n, 2, U_BLK + 2), U_BLK % 2)
            outputs(2)
            dve.wait_ge(b["mb"], val(lin(n, 1, 1)))
            nc.vector.tensor_tensor(dm[:].rearrange("p (h l) -> p h l", h=MH),
                                    ps[1][:, 0:HALF].rearrange("p (h l) -> p h l", h=MH),
                                    mbig[:].unsqueeze(1).to_broadcast([P, MH, P]), ALU.add).then_inc(b["dm"], 1)
            outputs(3)
            dve.wait_ge(b["kmt"], val(lin(n, 1, 1)))
            dve.wait_ge(b["cbn"], val(lin(n, 1, 1)))
            nc.vector.tensor_tensor(ka[:].rearrange("p (h l) -> p h l", h=MH),
                                    ps[2][:, 0:HALF].rearrange("p (h l) -> p h l", h=MH),
                                    cb[:, 1, :].unsqueeze(2).to_broadcast([P, MH, P]),
                                    ALU.mult).then_inc(b["ka"], 1)
            dve.wait_ge(b["sc"], val(lin(n, 1, 1)))
            dve.wait_ge(b["dx"], val(lin(n, 4, 4)))
            nc.vector.tensor_tensor(ptm[:], ps[1][:, HALF:2 * HALF], dt_[:], ALU.mult).then_inc(b["ptm"], 1)
            if not last:
                dve_keys(dve, n + 1)
            for h in range(MH):
                o = slice((h % 2) * HALF, (h % 2) * HALF + NA)
                dve.wait_ge(b["n1"], val(lin(n, 4, h + 1)))
                dve.wait_ge(b["tmp"], val(lin(n, 4, h + 1)))
                nc.vector.tensor_tensor(nd[:, h, 0:NA], ps[1][:, o], tmp[h % 2][:, 0:NA],
                                        ALU.add).then_inc(b["nd"], 1)
                dve.wait_ge(b["dc"], val(lin(n, 4, h + 1)))
                nc.vector.scalar_tensor_tensor(cst[:, h, 0:NA], cst[:, h, 0:NA], cb[:, 4, h:h + 1],
                                               ps[3][:, o], ALU.mult, ALU.add).then_inc(b["c"], 1)
            dve.wait_ge(b["nd"], val(lin(n, 4, 4)))
            if not first:
                dve.wait_ge(b["hn"], val(n))
            nc.vector.tensor_tensor(dn[:], nd[:, :, DV], cb[:, 3, :], ALU.max).then_inc(b["dd"], 1)
            dve.wait_ge(b["dd"], val(lin(n, 5, 1)))
            nc.vector.scalar_tensor_tensor(dn[:], nd[:, :, DV], -1.0, dn[:], ALU.mult,
                                           ALU.max).then_inc(b["dd"], 1)
            dve.wait_ge(b["dd"], val(lin(n, 5, 2)))
            nc.vector.reciprocal(rn[:], dn[:]).then_inc(b["dd"], 1)
            dve.wait_ge(b["ssq"], val(lin(n, 4, 4)))
            nc.vector.tensor_scalar(var[:], ssq[:], 1.0 / DV, EPS, ALU.mult, ALU.add).then_inc(b["dd"], 1)
            nc.vector.tensor_scalar(half_var[:], ssq[:], -0.5 / DV, -0.5 * EPS, ALU.mult,
                                    ALU.add).then_inc(b["dd"], 1)
            dve.wait_ge(s_unit, val(lin(n, 2, M_BLK + 2)))
            if not first:
                dve.wait_ge(s_gst[1], val(lin(n, 16, 0)))
            nc.vector.tensor_tensor(t_b[:], ps[0][:], rstd_b[:], ALU.mult).then_inc(b["gz"], 1)

        def load_za(sp, n):
            for dst, t0, t1 in ((zq, 0, 8), (zk, 8, 10)):
                for half in range(2):
                    for odd in range(2):
                        sp.dma_start(dst[HD * half:HD * (half + 1), odd::2, :],
                                     zs[t0:t1, HD * odd:HD * (odd + 1), bass.ds(val(lin(n, P, 0)), P)]
                                     .rearrange("t p c -> p t c")).then_inc(b["zql"], 16)

        def load_zv(sp, n):
            sp.dma_start(zv[:], zs[10:12, :, bass.ds(val(lin(n, P, 0)), P)].rearrange("t p c -> p t c")
                         ).then_inc(b["zvl"], 16)

        def load_zm(sp, n):
            sp.wait_ge(s_st[0], 16 * (Z_TILES // 2))
            for i, t in enumerate((N_ROPE + 10, N_ROPE + 2)):
                sp.dma_start(zm[:, 8 * i:8 * i + 8, :],
                             zs[t:t + 8, :, bass.ds(val(lin(n, P, 0)), P)].rearrange("t p c -> p t c")
                             ).then_inc(b["zml"], 16)

        def store_ht(sp, n):
            sp.wait_ge(b["hte"], val(n))
            sp.dma_start(mem_s[:, :, bass.ds(val(n * P), P)].rearrange("t p c -> p t c"),
                         ht[:].rearrange("p (t l) -> p t l", t=KT)).then_inc(b["hts"], 16)

        def sp_block(sp, n, first=False, last=False):
            if not first:
                load_unit(sp, lin(n, 2, U_BLK + 2), U_BLK % 2)
                store_ht(sp, n)
            if not last:
                sp.wait_ge(b["ql"], val(lin(n, 2, 2)))
                load_za(sp, n + 1)
                sp.wait_ge(b["vt"], val(lin(n, 1, 1)))
                load_zv(sp, n + 1)
            load_unit(sp, lin(n, 2, U_BLK + 3), (U_BLK + 1) % 2)
            sp.wait_ge(b["gz"], val(lin(n, 2, 1)))
            sp.dma_start(gs[val(lin(n, 2, 0))], t_a[:]).then_inc(s_gst[0], 16)
            sp.wait_ge(b["on"], val(lin(n, 8, 8)))
            sp.dma_start(att_s[:, :, bass.ds(val(n * P + P), P)].rearrange("t p c -> p t c"),
                         ot[:]).then_inc(b["ots"], 16)
            if last:
                sp.wait_ge(b["ots"], 16 * NB)
                for k in range(4):
                    load_att(sp, k)
            else:
                sp.wait_ge(b["n2"], val(lin(n, 4, 4)))
                load_zm(sp, n + 1)
            sp.wait_ge(b["gz"], val(lin(n, 2, 2)))
            sp.dma_start(gs[val(lin(n, 2, 1))], t_b[:]).then_inc(s_gst[1], 16)

        def sp_blocks(sp):
            for i in range(2):
                sp.wait_ge(s_st[i], 16 * (Z_TILES // 2))
            load_zm(sp, 0)
            sp_block(sp, 0, first=True)
            with sp.Fori(1, NB - 1) as reg:
                sp_block(sp, Lin(reg))
            sp_block(sp, NB - 1, last=True)
            for k in range(4, KT):
                load_att(sp, k)

        def pe_blocks(pe):
            pe.wait_ge(s_z, PROJ_UNITS - 1)
            pe.wait_ge(s_sos, 1)
            pe_block(pe, 0, first=True)
            with pe.Fori(1, NB) as reg:
                pe_block(pe, Lin(reg))

        def act_blocks(act):
            act_block(act, 0, first=True)
            with act.Fori(1, NB - 1) as reg:
                act_block(act, Lin(reg))
            act_block(act, NB - 1, last=True)

        def dve_block_init(dve):
            dve.wait_ge(s_bconst, 16 * N_BCONST)
            nc.vector.memset(k_hi[:].bitcast(F32), 0.0).then_inc(b["init"], 1)
            nc.vector.memset(k_lo[:].bitcast(F32), 0.0).then_inc(b["init"], 1)
            nc.vector.memset(vnat[:], 0.0).then_inc(b["init"], 1)
            nc.vector.memset(cst[:], 0.0).then_inc(b["init"], 1)
            nc.vector.tensor_scalar(sink8[:], sinkc[:], HD ** 0.5, None, ALU.mult).then_inc(b["init"], 1)

        def dve_blocks(dve):
            nc.vector.memset(vmn[:, :, DV:DV + 1], 1.0).then_inc(b["init"], 1)
            nc.vector.memset(three_halves[:], 1.5).then_inc(b["init"], 1)
            dve.wait_ge(b["init"], 7)
            dve.wait_ge(s_sos, 1)
            dve_block(dve, 0, first=True)
            with dve.Fori(1, NB - 1) as reg:
                dve_block(dve, Lin(reg))
            dve_block(dve, NB - 1, last=True)

        s_sg = sem("s_sg")
        s_sgo = sem("s_sgo")
        s_ym = sem("s_ym")
        s_ysum = sem("s_ysum")
        s_mem = sem("s_mem")
        s_xfin = sem("s_xfin")
        s_lg = [sem(f"s_lg{i}") for i in range(2)]
        s_lo = [sem(f"s_lo{i}") for i in range(2)]
        s_lm = [sem(f"s_lm{i}") for i in range(2)]
        s_lx = sem("s_lx")
        w_slot = [U_MERGE % 2, 1 - U_MERGE % 2]
        gate_stage = [[x[:, KT - 1, :], t_a], [rstd_b, sqacc]]
        o_stage = [rstd_b, sqacc]
        mem_stage = [t_b, sq[0]]

        def pe_merge(pe):
            for part, (hi, lo) in enumerate(((ra_hi, ra_lo), (rb_hi, rb_lo), (ra_hi, ra_lo))):
                def unit(c, k_wait=None, ks=(0, KT)):
                    u = c + (U_MERGE + KT * part)
                    j = (c if isinstance(c, int) else c.a) % 2
                    pe.wait_ge(s_wlo, val(u + 1))
                    if part == 0:
                        if isinstance(c, int):
                            if c == 0:
                                pe.wait_ge(b["gz"], 2 * NB)
                            else:
                                pe.wait_ge(b["nd"], MH * NB)
                        else:
                            pe.wait_ge(s_ym, val(c - 1))
                    elif part == 1:
                        pe.wait_ge(s_ym, val(c + (KT - 1)))
                    elif isinstance(c, int):
                        pe.wait_ge(s_ym, 2 * KT - 1 + c)
                    else:
                        pe.wait_ge(s_xfin, val(c - 1))
                    products(pe, ps[j], w_slot[j], hi, lo, k_wait=k_wait, ks=ks)

                unit(0, k_wait=(s_flo, KT * part))
                if part == 0:
                    pe.wait_ge(b["c"], 4 * NB)
                    pe_htt(pe, NB)
                unit(1)
                with pe.Fori(0, KT // 2 - 1) as reg:
                    for j in range(2):
                        unit(Lin(reg, 2, 2 + j))

        def act_merge(act):
            for k in range(4, KT):
                act_att_hi(act, k)
            split_hi(act, U_MERGE + 1, w_slot[1], (s_unit, M_MERGE))
            act_hte(act, NB)

            def branch(part):
                with act.Fori(0, KT // 2) as reg:
                    for j in range(2):
                        c = Lin(reg, 2, j)
                        gate = gate_stage[part][j][:]
                        act.wait_ge(s_lg[j], val(Lin(reg, 16, 16 + 16 * KT // 2 * part)))
                        nc.scalar.activation(gate, gate, ACT.Sigmoid).then_inc(s_sg, 1)
                        split_hi(act, c + (U_MERGE + KT * part + 2), w_slot[j],
                                 (s_unit, c + (M_MERGE + KT * part + 1)))
                        if part == 0:
                            act.wait_ge(s_lo[j], val(Lin(reg, 16, 16)))
                            nc.scalar.activation(o_stage[j][:], o_stage[j][:], ACT.Sigmoid).then_inc(s_sgo, 1)
                            act.wait_ge(s_mem, val(c + 1))
                            nc.scalar.copy(rb_hi[:, bass.ds(val(c), 1), :].rearrange("p o s -> p (o s)"),
                                           mem_stage[j][:]).then_inc(s_fhi, 1)
                        else:
                            act.wait_ge(s_ysum, val(c + 1))
                            nc.scalar.copy(ra_hi[:, bass.ds(val(c), 1), :].rearrange("p o s -> p (o s)"),
                                           x[:, bass.ds(val(c), 1), :].rearrange("p o s -> p (o s)")
                                           ).then_inc(s_fhi, 1)

            branch(0)
            branch(1)
            for c in range(KT):
                split_hi(act, U_MERGE + 2 * KT + c + 2, w_slot[c % 2], (s_unit, M_MERGE + 2 * KT + c + 1))
                act_norm_tile(act, 2, c, rb_hi, (s_xfin, c + 1))

        def dve_merge(dve):
            for k in range(KT):
                dve_att_lo(dve, k)
            split_lo(dve, U_MERGE + 1, w_slot[1])

            def tile_of(t, c):
                return t[:, bass.ds(val(c), 1), :].rearrange("p o s -> p (o s)")

            with dve.Fori(0, KT // 2) as reg:
                for j in range(2):
                    c = Lin(reg, 2, j)
                    split_lo(dve, c + (U_MERGE + 2), w_slot[j])
                    dve.wait_ge(s_unit, val(c + (M_MERGE + 1)))
                    dve.wait_ge(s_sg, val(c + 1))
                    nc.vector.tensor_tensor(tile_of(x, c), ps[j][:], gate_stage[0][j][:], ALU.mult).then_inc(s_ym, 1)
                    dve.wait_ge(s_lm[j], val(Lin(reg, 16, 16)))
                    dve.wait_ge(s_sgo, val(c + 1))
                    nc.vector.scalar_tensor_tensor(mem_stage[j][:], mem_stage[j][:],
                                                   col[:, bass.ds(val(c + C_HN), 1)], o_stage[j][:],
                                                   ALU.mult, ALU.mult).then_inc(s_mem, 1)
                    dve.wait_ge(s_fhi, val(c + (KT + 1)))
                    nc.vector.tensor_tensor(tile_of(rb_lo, c), mem_stage[j][:], tile_of(rb_hi, c).bitcast(F32),
                                            ALU.subtract).then_inc(s_flo, 1)
            with dve.Fori(0, KT // 2) as reg:
                for j in range(2):
                    c = Lin(reg, 2, j)
                    gate = gate_stage[1][j][:]
                    split_lo(dve, c + (U_MERGE + KT + 2), w_slot[j])
                    dve.wait_ge(s_unit, val(c + (M_MERGE + KT + 1)))
                    dve.wait_ge(s_sg, val(c + (KT + 1)))
                    nc.vector.tensor_tensor(gate, ps[j][:], gate, ALU.mult).then_inc(s_ym, 1)
                    dve.wait_ge(s_ym, val(c + (KT + 1)))
                    nc.vector.tensor_tensor(tile_of(x, c), tile_of(x, c), gate, ALU.add).then_inc(s_ysum, 1)
                    dve.wait_ge(s_fhi, val(c + (2 * KT + 1)))
                    nc.vector.tensor_tensor(tile_of(ra_lo, c), tile_of(x, c), tile_of(ra_hi, c).bitcast(F32),
                                            ALU.subtract).then_inc(s_flo, 1)
            for c in range(KT):
                split_lo(dve, U_MERGE + 2 * KT + c + 2, w_slot[c % 2])
                dve.wait_ge(s_unit, M_MERGE + 2 * KT + c + 1)
                dve.wait_ge(s_lx, 16 * (c + 1))
                nc.vector.tensor_tensor(x[:, c, :], ps[c % 2][:], t_b[:], ALU.add).then_inc(s_xfin, 1)
                dve_norm_tile(dve, 2, c, rb_hi, rb_lo)

        def sp_merge(sp):
            for i in range(2):
                sp.wait_ge(s_gst[i], 16 * NB)

            def load_gate(c, j, part):
                sp.dma_start(gate_stage[part][j][:], gs[val(c * 2 + part)]).then_inc(s_lg[j], 16)

            def load_mem(c, j):
                sp.dma_start(o_stage[j][:], zs[val(c + (N_ROPE + 18))]).then_inc(s_lo[j], 16)
                sp.dma_start(mem_stage[j][:], mem_s[val(c), :, P:]).then_inc(s_lm[j], 16)

            for c in range(2):
                load_gate(c, c, 0)
                load_unit(sp, U_MERGE + c + 2, w_slot[c])
            store_ht(sp, NB)
            sp.wait_ge(b["hts"], 16 * NB)
            for c in range(2):
                load_mem(c, c)
            with sp.Fori(0, KT // 2 - 1) as reg:
                for j in range(2):
                    c = Lin(reg, 2, 2 + j)
                    sp.wait_ge(s_ym, val(c - 1))
                    load_gate(c, j, 0)
                    sp.wait_ge(s_flo, val(c + (KT - 1)))
                    load_mem(c, j)
                    load_unit(sp, c + (U_MERGE + 2), w_slot[j])
            for c in range(2):
                sp.wait_ge(s_mem, KT - 1 + c)
                load_gate(c, c, 1)
                load_unit(sp, U_MERGE + KT + c + 2, w_slot[c])
            with sp.Fori(0, KT // 2 - 1) as reg:
                for j in range(2):
                    c = Lin(reg, 2, 2 + j)
                    sp.wait_ge(s_ysum, val(c - 1))
                    load_gate(c, j, 1)
                    load_unit(sp, c + (U_MERGE + KT + 2), w_slot[j])
            sp.wait_ge(s_flo, 2 * KT)
            for c in range(KT):
                if c:
                    sp.wait_ge(s_xfin, c)
                sp.dma_start(t_b[:], x_s[:, c, :]).then_inc(s_lx, 16)
                load_unit(sp, U_MERGE + 2 * KT + c + 2, w_slot[c % 2])

        ffn1 = Ffn(0, 0, 0, 0, (ra_hi, ra_lo), (rb_hi, rb_lo))
        ffn2 = Ffn(1, U_FFN2, M_FFN2, 2, (rb_hi, rb_lo), (ra_hi, ra_lo))

        block = e(nc.Block())

        @block.sync
        def _(sp):
            sp.dma_start(x[:, 0, :], x_t[:, 0, :]).then_inc(s_x[0], 16)
            sp.dma_start(col[:], cols).then_inc(s_const, 16)
            sp.dma_start(ident[:], ident_d).then_inc(s_const, 16)
            for i in range(1, KT):
                if i in (1, 3):
                    load_unit(sp, i // 2, i // 2, first=True)
                sp.dma_start(x[:, i, :], x_t[:, i, :]).then_inc(s_x[i], 16)
            load_units(sp, 2, FFN_UNITS)
            sp_proj(sp)
            sp_blocks(sp)
            sp_merge(sp)
            load_units(sp, U_FFN2 + 2, FFN_UNITS - 2)
            for half in range(2):
                c = slice(half * HALF, (half + 1) * HALF)
                for d in range(0, KT, 2):
                    sp.wait_ge(s_fin, half * KT + d + 2)
                    sp.dma_start(out[:, d:d + 2, c], x[:, d:d + 2, c]).then_inc(s_out, 16)
            sp.wait_ge(s_out, 16 * KT)

        @block.tensor
        def _(pe):
            pe.wait_ge(s_const, 32)
            pe.wait_ge(s_ones, 1)
            pe_ffn(pe, ffn1)
            pe_proj(pe)
            pe_blocks(pe)
            pe_merge(pe)
            pe_ffn(pe, ffn2)
            pe_sums(pe, 3)
            pe_spread(pe, 3)

        @block.scalar
        def _(act):
            act.wait_ge(s_const, 32)
            for d in range(KT):
                act_norm_tile(act, 0, d, ra_hi, (s_x[d], 16))
                if d % 2 == 0 and d < 4:
                    split_hi(act, d // 2, d // 2)
            act_ffn(act, ffn1, lambda act: act_ffn_tail(act, ffn1, ra_hi))
            act_proj(act)
            act_blocks(act)
            act_merge(act)
            act_ffn(act, ffn2, lambda act: act_ffn_tail(act, ffn2, None))
            act_root(act, 3)

        @block.vector
        def _(dve):
            nc.vector.memset(ones[:], 1.0).then_inc(s_ones, 1)
            dve.wait_ge(s_const, 32)
            for d in range(KT):
                dve_norm_tile(dve, 0, d, ra_hi, ra_lo)
                if d % 2 == 0 and d < 4:
                    split_lo(dve, d // 2, d // 2)
            dve_ffn(dve, ffn1, lambda dve: dve_ffn_tail(dve, ffn1, ra_hi, ra_lo))
            dve_proj(dve)
            dve_blocks(dve)
            dve_merge(dve)
            dve_ffn(dve, ffn2, lambda dve: dve_ffn_tail(dve, ffn2, None, None))
            dve_stats(dve, 3)
            for half in range(2):
                dve.wait_ge(s_rbc, 4 + half)
                c = slice(half * HALF, (half + 1) * HALF)
                for d in range(KT):
                    g = C_GAIN + 3 * KT + d
                    nc.vector.scalar_tensor_tensor(x[:, d, c], x[:, d, c], col[:, g:g + 1], ps[3][:, c],
                                                   ALU.mult, ALU.mult).then_inc(s_fin, 1)

        @block.gpsimd
        def _(pool):
            pool_norm(pool, 0)
            pool_norm(pool, 1)
            pool.wait_ge(b["init"], 7)
            with pool.Fori(1, NB + 1) as reg:
                pool_hn(pool, Lin(reg))
            pool_norm(pool, 2)
            pool_norm(pool, 3)


def tile_weights(w):
    return w.reshape(KT, P, w.shape[1] // P, P).transpose(2, 1, 0, 3).reshape(-1, P, D)


def tile_down(w):
    return w.reshape(PAIRS, 2, P, 2, HALF).transpose(0, 3, 2, 1, 4).reshape(-1, P, D)


def ffn_stream(gate, up, down):
    g, u, d = tile_weights(gate), tile_weights(up), tile_down(down)
    parts = [g[0:1], u[0:1], g[1:2], u[1:2]]
    for p in range(1, PAIRS):
        for j in range(2):
            f, h = 2 * p + j, 2 * (p - 1) + j
            parts += [g[f:f + 1], u[f:f + 1], d[h:h + 1]]
    return parts + [d[-2:]]


def projection_columns(a):
    w = a["w_in"][0]
    at = np.cumsum([0, D, 256, 256, 512, 512, D, D, MH, MH, D, D])
    q, k, v, qm, km, vm, om, i, f, ga, gm = [w[:, at[n]:at[n + 1]] for n in range(11)]
    gates = np.zeros((D, P), w.dtype)
    gates[:, 0:MH], gates[:, 32:32 + MH] = i, f
    turns = [t[:, c * P:(c + 1) * P] for c in range(MH) for t in (qm, km)]
    ends = [t[:, c * P:(c + 1) * P] for c in range(KT) for t in (ga, gm)]
    return np.concatenate([gates, q, k, v] + turns + [vm, om] + ends, axis=1)


def kernel(**inputs):
    import concourse.bacc as bacc
    from concourse.bass_utils import run_bass_kernel_spmd

    a = {k: np.asarray(v) for k, v in inputs.items()}
    w_stream = np.concatenate(
        ffn_stream(a["ffn1_w_gate"][0], a["ffn1_w_up"][0], a["ffn1_w_down"][0])
        + [tile_weights(projection_columns(a))]
        + [tile_weights(a[k][0]) for k in ("w_att", "w_mlstm", "w_out")]
        + ffn_stream(a["ffn2_w_gate"][0], a["ffn2_w_up"][0], a["ffn2_w_down"][0]))
    x_t = np.ascontiguousarray(a["x"][0].T.reshape(KT, P, S).transpose(1, 0, 2))

    def by_tile(v):
        return v.reshape(KT, P).T

    def on_heads(v):
        return np.concatenate([v, np.zeros(P - MH, v.dtype)])[:, None]

    conv = np.concatenate([a["conv_w"][0], a["conv_b"]], axis=0).reshape(5, 2, MH, P)
    cols = np.concatenate([by_tile(a["ffn1_norm"][0]), by_tile(a["mix_norm"][0]), by_tile(a["ffn2_norm"][0]),
                           by_tile(a["final_norm"]), np.full((P, 1), EPS, np.float32),
                           by_tile(a["head_norm"][0]), on_heads(a["b_i"][0]), on_heads(a["b_f"][0]),
                           conv.transpose(3, 2, 1, 0).reshape(P, 40)], axis=1)
    pos = np.arange(S, dtype=np.float32)
    freq = np.float32(10000.0) ** (-np.arange(HD // 2, dtype=np.float32) / np.float32(HD // 2))
    angle = (pos[None, :] * freq[:, None]).astype(np.float32)
    sin, cos = np.sin(angle), np.cos(angle)
    rope_cs = np.stack([np.tile(cos, (4, 1)), np.tile(np.concatenate([-sin, sin]), (2, 1))]).astype(np.float32)
    l, m = np.arange(P)[:, None], np.arange(P)[None, :]
    prev = np.where(m > l, 0.0, -BIG)
    cur = np.where(m <= l, 0.0, -BIG)
    masks = np.stack([np.concatenate([before, cur], axis=1)
                      for before in (np.full((P, P), -BIG), prev)], axis=1).astype(np.float32)
    mask_big = np.where(l > m, BIG, 0.0).astype(np.float32)
    sel_head = np.zeros((MH, MH, P), np.float32)
    for h in range(MH):
        sel_head[h, h] = 1.0
    sel_last = np.zeros((P, P), np.float32)
    sel_last[P - 1] = 1.0
    arrays = {"w_stream": w_stream, "x_t": x_t, "cols": np.ascontiguousarray(cols),
              "ident_d": np.eye(P, dtype=np.float32),
              "sinks": np.ascontiguousarray(np.broadcast_to(a["attn_sinks"], (P, HEADS))),
              "rope_cs": rope_cs, "masks": masks, "mask_big": mask_big, "sel_head": sel_head,
              "sel_last": sel_last}
    nc = bacc.Bacc("TRN2", target_bir_lowering=False, num_devices=1)
    args = [nc.dram_tensor(k, v.shape, F32, kind="ExternalInput").ap() for k, v in arrays.items()]
    args.append(nc.dram_tensor("out_t", (P, KT, S), F32, kind="ExternalOutput").ap())
    for name, shape in (("zs", (Z_TILES, P, S)), ("gs", (2 * KT, P, S)), ("att_s", (KT, P, P + S)),
                        ("mem_s", (KT, P, P + S)), ("x_s", (P, KT, S))):
        args.append(nc.dram_tensor(name, shape, F32, kind="Internal").ap())
    hybrid_layer(nc, *args)
    r = run_bass_kernel_spmd(nc, [arrays], core_ids=[0])
    out_t = r.results[0]["out_t"]
    return np.ascontiguousarray(out_t.transpose(1, 0, 2).reshape(D, S).T)[None]
```

```python
from contextlib import ExitStack

import numpy as np

import concourse.bass as bass
from concourse import mybir
from concourse.alu_op_type import AluOpType as ALU

ACT = mybir.ActivationFunctionType
F32 = mybir.dt.float32
F32R = mybir.dt.float32r

P = 128
D = 1024
S = 1024
KT = D // P
HALF = 512
F = 2816
FT = F // P
PAIRS = FT // 2
EPS = 1e-5

FFN_UNITS = 3 * FT

C_GAIN = 0
C_EPS = 32
C_HN = 33
C_BI, C_BF = 41, 42
C_CONV = 43
N_COLS = C_CONV + 5 * 8

HEADS, KV_HEADS, HD = 16, 4, 64
GROUP = HEADS // KV_HEADS
MH = 4
DV = D // MH
DK = DV // 2
NA = DV + 1
NB = S // P
BIG = 1e30

N_ROPE, N_RAW, N_CONV = 10, 18, 8
Z_TILES = N_ROPE + N_RAW + N_CONV
PROJ_UNITS = 1 + Z_TILES
U_PROJ = FFN_UNITS
U_BLK = U_PROJ + PROJ_UNITS
U_MERGE = U_BLK + 2 * NB
U_FFN2 = U_MERGE + 3 * KT
M_PROJ = 2 * FT
M_BLK = M_PROJ + PROJ_UNITS
M_MERGE = M_BLK + 2 * NB
M_FFN2 = M_MERGE + 3 * KT


class Lin:
    def __init__(self, reg, m=1, a=0):
        self.reg, self.m, self.a = reg, m, a

    def __mul__(self, k):
        return Lin(self.reg, self.m * k, self.a * k)

    def __add__(self, k):
        return Lin(self.reg, self.m, self.a + k)

    __radd__ = __add__

    def __sub__(self, k):
        return self + -k


def val(v):
    return v.reg * v.m + v.a if isinstance(v, Lin) else v


def hybrid_layer(nc, w_stream, x_t, cols, ident_d, sinks, rope_cs, masks, mask_big, sel_head, sel_last,
                 out, zs, gs, att_s, mem_s, x_s):
    with ExitStack() as ctx:
        e = ctx.enter_context
        base = [(nc.sbuf_base + 31) // 32 * 32]

        def at(name, shape, dt, offset):
            return nc.alloc_sbuf_tensor_at(name, shape, dt, offset=offset)

        def sb(name, shape, dt):
            t = at(name, shape, dt, base[0])
            size = 4
            for n in shape[1:]:
                size *= n
            base[0] += (size + 31) // 32 * 32
            return t

        x = sb("x", [P, KT, S], F32)
        ra_hi = sb("ra_hi", [P, KT, S], F32R)
        ra_lo = sb("ra_lo", [P, KT, S], F32R)
        rb_base = base[0]
        rb_hi = sb("rb_hi", [P, KT, S], F32R)
        rb_lo = sb("rb_lo", [P, KT, S], F32R)
        w_raw = [sb(f"w_raw{i}", [P, D], F32) for i in range(2)]
        w_hi = [sb(f"w_hi{i}", [P, D], F32R) for i in range(2)]
        w_lo = [sb(f"w_lo{i}", [P, D], F32R) for i in range(2)]
        rstd_b = sb("rstd_b", [P, S], F32)
        t_a = sb("t_a", [P, S], F32)
        t_b = sb("t_b", [P, S], F32)
        sq = [sb("sq", [P, S], F32), t_a]
        sqacc = sb("sqacc", [P, S], F32)
        col = sb("col", [P, N_COLS], F32)
        ident = sb("ident", [P, P], F32)
        ones = sb("ones", [P, 1], F32)
        root = sb("root", [P, KT], F32)
        ssv = sb("ssv", [P, KT], F32)
        rstd_c = sb("rstd_c", [P, KT], F32)
        assert base[0] <= nc.sbuf_usable_end

        ps = [e(nc.psum_tensor(f"ps{i}", [P, S], F32)) for i in range(4)]

        def sem(name):
            return e(nc.semaphore(name))

        s_const = sem("s_const")
        s_x = [sem(f"s_x{i}") for i in range(KT)]
        s_ones = sem("s_ones")
        s_w = [sem(f"s_w{i}") for i in range(2)]
        s_whi = sem("s_whi")
        s_wlo = sem("s_wlo")
        s_unit = sem("s_unit")
        s_gs = sem("s_gs")
        s_silu = sem("s_silu")
        s_us = sem("s_us")
        s_h = sem("s_h")
        s_hhi = sem("s_hhi")
        s_hlo = sem("s_hlo")
        s_down = sem("s_down")
        s_xadd = sem("s_xadd")
        s_ahi = sem("s_ahi")
        s_alo = sem("s_alo")
        s_sq = sem("s_sq")
        s_acc = sem("s_acc")
        s_ss = sem("s_ss")
        s_root = sem("s_root")
        s_nr = sem("s_nr")
        s_rc = sem("s_rc")
        s_rbc = sem("s_rbc")
        s_rb = sem("s_rb")
        s_out = sem("s_out")
        s_fin = sem("s_fin")
        s_gain = sem("s_gain")
        s_fin_pool = sem("s_fin_pool")

        def load_unit(sp, n, slot, first=False):
            if not first:
                sp.wait_ge(s_wlo, val(n - 1))
            sp.dma_start(w_raw[slot][:], w_stream[val(n)]).then_inc(s_w[slot], 16)

        def load_units(sp, start, count):
            with sp.Fori(0, count // 2) as reg:
                i = Lin(reg)
                for j in range(2):
                    load_unit(sp, i * 2 + (start + j), (start + j) % 2)
            if count % 2:
                load_unit(sp, start + count - 1, (start + count - 1) % 2)

        def split_hi(act, n, slot, done=None):
            act.wait_ge(s_w[slot], val((n - slot) * 8 + 16 if isinstance(n, int) else n * 8 + (16 - 8 * slot)))
            if done is not None:
                act.wait_ge(done[0], val(done[1]))
            nc.scalar.copy(w_hi[slot][:], w_raw[slot][:]).then_inc(s_whi, 1)

        def split_lo(dve, n, slot):
            dve.wait_ge(s_whi, val(n + 1))
            nc.vector.tensor_tensor(w_lo[slot][:], w_raw[slot][:], w_hi[slot][:].bitcast(F32),
                                    ALU.subtract).then_inc(s_wlo, 1)

        def products(pe, out_ps, slot, hi, lo, k_wait=None, ks=(0, KT)):
            for k in range(*ks):
                if k_wait is not None:
                    pe.wait_ge(k_wait[0], val(k_wait[1] + k + 1))
                w = slice(k * P, (k + 1) * P)
                for i, (wt, a) in enumerate(((w_hi, hi), (w_hi, lo), (w_lo, hi))):
                    for t in range(2):
                        mm = nc.tensor.matmul(out_ps[:, t * HALF:(t + 1) * HALF], wt[slot][:, w],
                                              a[:, k, t * HALF:(t + 1) * HALF],
                                              start=(k == 0 and i == 0), stop=(k == KT - 1 and i == 2))
            if ks[1] == KT:
                mm.then_inc(s_unit, 1)

        def pe_sums(pe, norm):
            pe.wait_ge(s_acc, KT * (norm + 1) - (norm == 3))
            for j in range(KT):
                mm = nc.tensor.matmul(ps[2][:, j:j + 1], sqacc[:, j * P:(j + 1) * P], ones[:],
                                      start=(j == 0), stop=(norm < 3), skip_group_check=True)
            if norm == 3:
                pe.wait_ge(s_sq, (KT - 1) * (norm + 1))
                for j in range(KT):
                    mm = nc.tensor.matmul(ps[2][:, j:j + 1], sq[(KT - 2) % 2][:, j * P:(j + 1) * P], ones[:],
                                          start=False, stop=True, skip_group_check=True)
            mm.then_inc(s_ss, 1)

        def pe_spread(pe, norm):
            pe.wait_ge(s_rc, val(norm + 1))
            for j in range(KT):
                mm = nc.tensor.matmul(ps[3][:, j * P:(j + 1) * P],
                                      rstd_c[:, j:j + 1].to_broadcast([P, P]), ident[:],
                                      start=(j % 4 == 0), stop=True, skip_group_check=True)
                if j == KT - 1 or (norm == 3 and j == KT // 2 - 1):
                    mm.then_inc(s_rbc, 1)

        def act_norm_tile(act, norm, d, hi, ready, unit=None):
            act.wait_ge(ready[0], ready[1])
            if hi is not None:
                g = C_GAIN + norm * KT + d
                nc.scalar.activation(hi[:, d, :], x[:, d, :], ACT.Copy,
                                     scale=col[:, g:g + 1]).then_inc(s_ahi, 1)
            if unit is not None:
                split_hi(act, unit, unit)
            if d == 0:
                if norm > 0:
                    act.wait_ge(s_ss, norm)
                nc.scalar.activation(sqacc[:], x[:, d, :], ACT.Square).then_inc(s_acc, 1)
            else:
                if d >= 3:
                    act.wait_ge(s_acc, KT * norm + d - 1)
                nc.scalar.activation(sq[(d - 1) % 2][:], x[:, d, :], ACT.Square).then_inc(s_sq, 1)

        def act_root(act, norm):
            act.wait_ge(s_ss, val(norm + 1))
            nc.scalar.activation(root[:], ps[2][:, 0:KT], ACT.Sqrt, bias=col[:, C_EPS:C_EPS + 1],
                                 scale=1.0 / D).then_inc(s_root, 1)

        def act_stats(act, norm):
            act_root(act, norm)
            act.wait_ge(s_rbc, val(norm + 1))
            nc.scalar.copy(rstd_b[:], ps[3][:]).then_inc(s_rb, 1)

        def dve_norm_tile(dve, norm, d, hi, lo):
            g = C_GAIN + norm * KT + d
            dve.wait_ge(s_ahi, val(KT * norm + d + 1))
            nc.vector.scalar_tensor_tensor(lo[:, d, :], x[:, d, :], col[:, g:g + 1],
                                           hi[:, d, :].bitcast(F32), ALU.mult,
                                           ALU.subtract).then_inc(s_alo, 1)

        def dve_stats(dve, norm):
            dve.wait_ge(s_root, val(norm + 1))
            nc.vector.reciprocal(rstd_c[:], root[:]).then_inc(s_nr, 1)
            nc.vector.tensor_scalar(ssv[:], ps[2][:, 0:KT], 1.0 / D, EPS, ALU.mult, ALU.add).then_inc(s_nr, 1)
            dve.wait_ge(s_nr, 5 * norm + 2)
            nc.vector.tensor_tensor(ssv[:], ssv[:], rstd_c[:], ALU.mult).then_inc(s_nr, 1)
            dve.wait_ge(s_nr, 5 * norm + 3)
            nc.vector.tensor_tensor(ssv[:], ssv[:], rstd_c[:], ALU.mult).then_inc(s_nr, 1)
            dve.wait_ge(s_nr, 5 * norm + 4)
            nc.vector.tensor_scalar(ssv[:], ssv[:], -0.5, 1.5, ALU.mult, ALU.add).then_inc(s_nr, 1)
            dve.wait_ge(s_nr, 5 * norm + 5)
            nc.vector.tensor_tensor(rstd_c[:], rstd_c[:], ssv[:], ALU.mult).then_inc(s_rc, 1)

        def pool_norm(pool, norm):
            for d in range(1, KT - (norm == 3)):
                pool.wait_ge(s_sq, (KT - 1) * norm + d)
                pool.wait_ge(s_acc, KT * norm + d)
                nc.gpsimd.tensor_tensor(sqacc[:], sqacc[:], sq[(d - 1) % 2][:], ALU.add).then_inc(s_acc, 1)

        class Ffn:
            def __init__(self, index, unit0, m0, norm, act, hidden):
                self.unit0, self.m0, self.norm = unit0, m0, norm
                self.hi, self.lo = act
                self.h_hi, self.h_lo = hidden
                self.f0 = FT * index
                self.a0 = PAIRS * KT * index

            def slot(self, n):
                return (self.unit0 + n) % 2

        def pe_down(pe, o, n, slot, p, par, half, first=False):
            pe.wait_ge(s_wlo, val(n + 1))
            pe.wait_ge(s_hlo, val(p * 2 + (o.f0 + 2)))
            for dd in range(4):
                d_ps = ps[2 + dd % 2]
                if not (first and dd < 2):
                    pe.wait_ge(s_xadd, val(p * KT + (o.a0 + 4 * half + dd - 1)))
                for j in range(2):
                    w = slice(j * HALF + dd * P, j * HALF + (dd + 1) * P)
                    for i, (wt, h) in enumerate(((w_hi, o.h_hi), (w_hi, o.h_lo), (w_lo, o.h_hi))):
                        for t in range(2):
                            mm = nc.tensor.matmul(d_ps[:, t * HALF:(t + 1) * HALF], wt[slot][:, w],
                                                  h[:, 2 * par + j, t * HALF:(t + 1) * HALF],
                                                  start=(j == 0 and i == 0), stop=(j == 1 and i == 2))
                mm.then_inc(s_down, 1)

        def pe_ffn(pe, o):
            for n in range(4):
                pe.wait_ge(s_wlo, val(o.unit0 + n + 1))
                if o.norm == 2 and n < 2:
                    pe.wait_ge(s_xfin, KT - 1 + n)
                if n == 2:
                    pe.wait_ge(s_root, val(o.norm + 1))
                if n == 3:
                    pe.wait_ge(s_rb, val(o.norm + 1))
                if n == 0:
                    products(pe, ps[0], o.slot(0), o.hi, o.lo, k_wait=(s_alo, KT * o.norm))
                elif n == 1:
                    products(pe, ps[1], o.slot(1), o.hi, o.lo, ks=(0, 3))
                    pe_sums(pe, o.norm)
                    products(pe, ps[1], o.slot(1), o.hi, o.lo, ks=(3, 6))
                    pe_spread(pe, o.norm)
                    products(pe, ps[1], o.slot(1), o.hi, o.lo, ks=(6, KT))
                else:
                    products(pe, ps[n], o.slot(n), o.hi, o.lo)

            def pair(n, p, par, first=False):
                for j in range(2):
                    pe.wait_ge(s_wlo, val(n + (3 * j + 1)))
                    pe.wait_ge(s_gs, val(p * 2 + (o.f0 + j)))
                    products(pe, ps[0], o.slot(j), o.hi, o.lo)
                    pe.wait_ge(s_wlo, val(n + (3 * j + 2)))
                    pe.wait_ge(s_us, val(p * 2 + (o.f0 + j)))
                    products(pe, ps[1], o.slot(j + 1), o.hi, o.lo)
                    pe_down(pe, o, n + (3 * j + 2), o.slot(j), p - 1, 1 - par, j, first and j == 0)

            pair(o.unit0 + 4, 1, 1, first=True)
            pair(o.unit0 + 10, 2, 0)
            with pe.Fori(0, (PAIRS - 3) // 2) as reg:
                i = Lin(reg)
                for j in range(2):
                    pair(i * 12 + (o.unit0 + 16 + 6 * j), i * 2 + (3 + j), 1 - j)
            for half in range(2):
                pe_down(pe, o, o.unit0 + FFN_UNITS - 2 + half, o.slot(half), PAIRS - 1, 0, half)

        def act_silu(act, o, f):
            act.wait_ge(s_gs, val(f + (o.f0 + 1)))
            nc.scalar.activation(t_a[:], t_a[:], ACT.Silu).then_inc(s_silu, 1)

        def act_hhi(act, o, f, hslot):
            act.wait_ge(s_h, val(f + (o.f0 + 1)))
            nc.scalar.copy(o.h_hi[:, hslot, :], t_b[:]).then_inc(s_hhi, 1)

        def act_ffn(act, o, tail):
            for n in range(4):
                split_hi(act, o.unit0 + n + 2, o.slot(n), (s_unit, o.m0 + n + 1))
                if n == 0:
                    act_stats(act, o.norm)
                if n % 2 == 0:
                    act_silu(act, o, n // 2)
                else:
                    act_hhi(act, o, n // 2, n // 2)

            def pair(n, p, par, last=False):
                for j in range(2):
                    f = p * 2 + j
                    split_hi(act, n + (3 * j + 2), o.slot(j), (s_unit, p * 4 + (o.m0 + 2 * j + 1)))
                    act_silu(act, o, f)
                    split_hi(act, n + (3 * j + 3), o.slot(j + 1), (s_unit, p * 4 + (o.m0 + 2 * j + 2)))
                    act_hhi(act, o, f, 2 * par + j)
                    if not (last and j == 1):
                        split_hi(act, n + (3 * j + 4), o.slot(j), (s_down, p * KT + (o.a0 + 4 * j - 4)))

            pair(o.unit0 + 4, 1, 1)
            pair(o.unit0 + 10, 2, 0)
            with act.Fori(0, (PAIRS - 3) // 2) as reg:
                i = Lin(reg)
                for j in range(2):
                    pair(i * 12 + (o.unit0 + 16 + 6 * j), i * 2 + (3 + j), 1 - j)
            tail(act)

        def dve_gs(dve, o, f, src, wait):
            if wait:
                dve.wait_ge(s_h, val(f + o.f0))
            nc.vector.tensor_tensor(t_a[:], src[:], rstd_b[:], ALU.mult).then_inc(s_gs, 1)

        def dve_us(dve, o, f, src, wait):
            if wait:
                dve.wait_ge(s_hlo, val(f + o.f0))
            nc.vector.tensor_tensor(t_b[:], src[:], rstd_b[:], ALU.mult).then_inc(s_us, 1)

        def dve_h(dve, o, f):
            dve.wait_ge(s_silu, val(f + (o.f0 + 1)))
            dve.wait_ge(s_us, val(f + (o.f0 + 1)))
            nc.vector.tensor_tensor(t_b[:], t_b[:], t_a[:], ALU.mult).then_inc(s_h, 1)

        def dve_hlo(dve, o, f, hslot):
            dve.wait_ge(s_hhi, val(f + (o.f0 + 1)))
            nc.vector.tensor_tensor(o.h_lo[:, hslot, :], t_b[:], o.h_hi[:, hslot, :].bitcast(F32),
                                    ALU.subtract).then_inc(s_hlo, 1)

        def dve_xadd(dve, o, p, d):
            dve.wait_ge(s_down, val(p * KT + (o.a0 + d + 1)))
            before = p * KT + (o.a0 + d - 7) if not isinstance(p, int) or p else o.a0
            if not isinstance(before, int) or before > 0:
                dve.wait_ge(s_xadd, val(before))
            nc.vector.scalar_tensor_tensor(x[:, d, :], ps[2 + d % 2][:], 0.5, x[:, d, :],
                                           ALU.mult, ALU.add).then_inc(s_xadd, 1)

        def dve_ffn(dve, o, tail):
            if o.norm == 2:
                dve.wait_ge(s_xfin, KT)
            for n in range(4):
                split_lo(dve, o.unit0 + n + 2, o.slot(n))
                if n == 0:
                    dve_stats(dve, o.norm)
                    dve.wait_ge(s_rb, val(o.norm + 1))
                if n % 2 == 0:
                    dve_gs(dve, o, n // 2, ps[n], n > 0)
                else:
                    dve_us(dve, o, n // 2, ps[n], n > 1)
                    dve_h(dve, o, n // 2)
                    dve_hlo(dve, o, n // 2, n // 2)

            def pair(n, p, par, last=False):
                for j in range(2):
                    f = p * 2 + j
                    split_lo(dve, n + (3 * j + 2), o.slot(j))
                    dve.wait_ge(s_unit, val(p * 4 + (o.m0 + 2 * j + 1)))
                    dve_gs(dve, o, f, ps[0], True)
                    split_lo(dve, n + (3 * j + 3), o.slot(j + 1))
                    dve.wait_ge(s_unit, val(p * 4 + (o.m0 + 2 * j + 2)))
                    dve_us(dve, o, f, ps[1], True)
                    dve_xadd(dve, o, p - 1, 4 * j)
                    dve_h(dve, o, f)
                    dve_xadd(dve, o, p - 1, 4 * j + 1)
                    dve_hlo(dve, o, f, 2 * par + j)
                    for dd in range(2, 4):
                        dve_xadd(dve, o, p - 1, 4 * j + dd)
                    split_lo(dve, n + (3 * j + 4), o.slot(j))

            pair(o.unit0 + 4, 1, 1)
            pair(o.unit0 + 10, 2, 0)
            with dve.Fori(0, (PAIRS - 3) // 2) as reg:
                i = Lin(reg)
                for j in range(2):
                    pair(i * 12 + (o.unit0 + 16 + 6 * j), i * 2 + (3 + j), 1 - j)
            tail(dve)

        def dve_ffn_tail(dve, o, hi, lo):
            p = PAIRS - 1
            for d in range(KT):
                dve_xadd(dve, o, p, d)
                if hi is not None:
                    if d > 0:
                        dve_norm_tile(dve, o.norm + 1, d - 1, hi, lo)
                    if d == 3 or d == 7:
                        split_lo(dve, o.unit0 + FFN_UNITS + d // 4, o.slot(d // 4))
            if hi is not None:
                dve_norm_tile(dve, o.norm + 1, KT - 1, hi, lo)

        def act_ffn_tail(act, o, hi):
            last = o.a0 + KT * (PAIRS - 1)
            for d in range(KT):
                act_norm_tile(act, o.norm + 1, d, hi, (s_xadd, last + d + 1))
                if hi is not None and (d == 3 or d == 7):
                    split_hi(act, o.unit0 + FFN_UNITS + d // 4, o.slot(d // 4), (s_down, last + d + 1))


        def region(start, end):
            top = [start]

            def take(name, shape, dt=F32):
                size = 4
                for n in shape[1:]:
                    size *= n
                t = at(name, shape, dt, top[0])
                top[0] += (size + 31) // 32 * 32
                assert top[0] <= end, (name, top[0] - end)
                return t
            return take

        x_base = rb_base - 3 * KT * S * 4
        xr = region(x_base, x_base + KT * S * 4)
        m_rows = xr("m_rows", [MH, S])
        cb_all = xr("cb_all", [P, NB, 5, MH])
        mk0 = xr("mk0", [P, 2 * P])
        mk = xr("mk", [P, 2 * P])
        sinkc = xr("sinkc", [P, HEADS])
        sink8 = xr("sink8", [P, HEADS])
        mbig = xr("mbig", [P, P])
        selh = xr("selh", [MH, MH, P])
        sell = xr("sell", [P, P])

        pr = region(rb_base, rb_base + 2 * KT * S * 4)
        rope_c = pr("rope_c", [P, S])
        rope_s = pr("rope_s", [P, S])
        z = [pr(f"z{i}", [P, S + 4]) for i in range(2)]
        swapped = pr("swapped", [P, S])
        y = [pr(f"y{i}", [P, S]) for i in range(2)]
        rz_i = pr("rz_i", [MH, S])
        rz_f = pr("rz_f", [MH, S])
        r_t = pr("r_t", [MH, S])
        r_b = pr("r_b", [MH, S])
        r_d = pr("r_d", [MH, S])
        r_mp = pr("r_mp", [MH, NB])
        rows = pr("rows", [P, S])

        k_hi = xr("k_hi", [P, KV_HEADS, 2 * P], F32R)
        k_lo = xr("k_lo", [P, KV_HEADS, 2 * P], F32R)
        zv = xr("zv", [P, 2, P])
        vnat = xr("vnat", [P, 2, KV_HEADS, 2, HD])
        nd = xr("nd", [P, MH, NA + 1])
        cst = xr("cst", [P, MH, NA + 1])
        br = region(rb_base, rb_base + 2 * KT * S * 4)
        zq = br("zq", [P, HEADS, P])
        q_hl = br("q_hl", [P, HEADS, P], F32R)
        zk = br("zk", [P, KV_HEADS, P])
        zm = br("zm", [P, 16, P])
        ot = br("ot", [P, KT, P])
        sm = [br(f"sm{i}", [P, S]) for i in range(2)]
        ptb = [br(f"ptb{i}", [P, S]) for i in range(2)]
        vmn = br("vmn", [P, MH, NA + 1])
        dm = br("dm", [P, MH * P])
        dt_ = br("dt", [P, MH * P])
        ptm = br("ptm", [P, MH * P])
        tmp = [br(f"tmp{i}", [P, NA + 1]) for i in range(2)]
        hn, ht = sq[0], sqacc
        ka = br("ka", [P, MH * P])
        turn = br("turn", [P, 1])
        mx = br("mx", [P, HEADS])
        nm = br("nm", [P, HEADS])
        sn = br("sn", [P, HEADS])
        es = br("es", [P, HEADS])
        rs = br("rs", [P, HEADS])
        rd = br("rd", [P, HEADS])
        cb = br("cb", [P, 5, MH])
        dn = br("dn", [P, MH])
        rn = br("rn", [P, MH])
        ssq = br("ssq", [P, MH])
        var = br("var", [P, MH])
        half_var = br("half_var", [P, MH])
        three_halves = br("three_halves", [P, MH])
        lv = br("lv", [P, MH])
        y0 = br("y0", [P, MH])
        yy = br("yy", [P, MH])
        yc = br("yc", [P, MH])
        scl = br("scl", [P, MH])

        s_cs = sem("s_cs")
        s_bconst = sem("s_bconst")
        s_xs = sem("s_xs")
        s_z = sem("s_z")
        s_pad = sem("s_pad")
        s_swap = sem("s_swap")
        s_rm = sem("s_rm")
        s_cv = sem("s_cv")
        s_csilu = sem("s_csilu")
        s_y = sem("s_y")
        s_st = [sem(f"s_st{i}") for i in range(2)]
        s_row = sem("s_row")
        s_rowa = sem("s_rowa")
        s_rt = sem("s_rt")
        s_cb = sem("s_cb")
        s_so = sem("s_so")
        s_sos = sem("s_sos")

        N_BCONST = 6

        def pe_proj(pe):
            pe.wait_ge(s_wlo, U_PROJ + 1)
            products(pe, ps[0], U_PROJ % 2, ra_hi, ra_lo, k_wait=(s_alo, KT))

            def units(first, count):
                with pe.Fori(0, count // 2) as reg:
                    i = Lin(reg, 2)
                    for j in range(2):
                        ee = i + (first + j)
                        pe.wait_ge(s_wlo, val(ee + (U_PROJ + 1)))
                        if first + j >= 2:
                            pe.wait_ge(s_z, val(ee - 1))
                        products(pe, ps[(first + j) % 2], (U_PROJ + first + j) % 2, ra_hi, ra_lo)

            pe.wait_ge(s_wlo, U_PROJ + 2)
            products(pe, ps[1], (U_PROJ + 1) % 2, ra_hi, ra_lo, ks=(0, 2))
            pe_sums(pe, 1)
            products(pe, ps[1], (U_PROJ + 1) % 2, ra_hi, ra_lo, ks=(2, 5))
            pe_spread(pe, 1)
            products(pe, ps[1], (U_PROJ + 1) % 2, ra_hi, ra_lo, ks=(5, KT))
            pe.wait_ge(s_wlo, U_PROJ + 3)
            pe.wait_ge(s_z, 1)
            products(pe, ps[0], U_PROJ % 2, ra_hi, ra_lo)
            units(3, 24)
            pe.wait_ge(s_rowa, 6)
            for c in range(NB):
                mm = nc.tensor.transpose(ps[2][:, c * P:(c + 1) * P], rows[:, c * P:(c + 1) * P], ident[:])
            mm.then_inc(s_rt, 1)
            units(27, 4)
            pe.wait_ge(s_cb, 1)
            pe.wait_ge(s_bconst, 16 * N_BCONST)
            nc.tensor.matmul(ps[3][:, 0:NB * MH], sell[:], cb_all[:, :, 2, :], start=True,
                             stop=True).then_inc(s_so, 1)
            units(31, 6)

        def act_rope(act, ee, par, first=False):
            act.wait_ge(s_z, val(ee + 1))
            if not first:
                act.wait_ge(s_y, val(ee - 1))
            for q in range(4):
                o = q ^ 1
                nc.scalar.copy(swapped[32 * q:32 * q + 32, :],
                               z[par][32 * o:32 * o + 32, 3:3 + S]).then_inc(s_swap, 1)

        def act_proj(act):
            split_hi(act, U_PROJ + 2, U_PROJ % 2, (s_unit, M_PROJ + 1))
            act_stats(act, 1)
            for ee in (1, 2):
                split_hi(act, ee + U_PROJ + 2, ee % 2, (s_unit, ee + M_PROJ + 1))
                act_rope(act, ee, ee % 2, first=ee == 1)
            with act.Fori(0, N_ROPE // 2 - 1) as reg:
                for j in range(2):
                    ee = Lin(reg, 2, 3 + j)
                    split_hi(act, ee + (U_PROJ + 2), (1 + j) % 2, (s_unit, ee + (M_PROJ + 1)))
                    act_rope(act, ee, (1 + j) % 2)

            def raw(first, count):
                with act.Fori(0, count // 2) as reg:
                    for j in range(2):
                        ee = Lin(reg, 2, first + j)
                        split_hi(act, ee + (U_PROJ + 2), (first + j) % 2, (s_unit, ee + (M_PROJ + 1)))

            raw(11, 2)
            with act.Fori(0, N_CONV // 2) as reg:
                for j in range(2):
                    ee = Lin(reg, 2, 13 + j)
                    split_hi(act, ee + (U_PROJ + 2), (13 + j) % 2, (s_unit, ee + (M_PROJ + 1)))
                    act.wait_ge(s_cv, val(Lin(reg, 8, 4 * j + 4)))
                    if j == 0:
                        nc.scalar.activation(y[1][:], y[1][:], ACT.Silu).then_inc(s_y, 1)
                    else:
                        nc.scalar.activation(y[0][:], y[0][:], ACT.Silu).then_inc(s_csilu, 1)
                        act.wait_ge(s_csilu, val(Lin(reg, 1, 1)))
                        nc.scalar.activation(y[0][:], y[0][:], ACT.Copy,
                                             scale=float(DK) ** -0.5).then_inc(s_y, 1)
            raw(21, 2)
            act_rows1(act)
            raw(23, 2)
            act_rows2(act)
            raw(25, 10)
            act.wait_ge(b["init"], 5)
            act_keys(act, 0)
            raw(35, 2)

        def act_rows1(act):
            act.wait_ge(s_row, 3)
            nc.scalar.activation(r_t[:], rz_f[:], ACT.Abs).then_inc(s_rowa, 1)
            act.wait_ge(s_rowa, 1)
            nc.scalar.activation(r_t[:], r_t[:], ACT.Exp, scale=-1.0).then_inc(s_rowa, 1)
            act.wait_ge(s_rowa, 2)
            nc.scalar.activation(r_t[:], r_t[:], ACT.Ln, bias=1.0).then_inc(s_rowa, 1)

        def act_rows2(act):
            for i, (q, scale) in enumerate(((32, 1.0), (64, 1.0), (96, -1.0))):
                act.wait_ge(s_row, 17)
                nc.scalar.activation(rows[q:q + MH, :], rows[q:q + MH, :], ACT.Exp,
                                     scale=scale).then_inc(s_rowa, 1)

        def dve_rows0(dve):
            dve.wait_ge(s_unit, M_PROJ + 1)
            nc.vector.tensor_tensor(rz_f[:], ps[0][32:32 + MH, :], rstd_b[32:32 + MH, :],
                                    ALU.mult).then_inc(s_row, 1)
            dve.wait_ge(s_row, 1)
            nc.vector.tensor_tensor(rz_i[:], ps[0][0:MH, :], rstd_b[0:MH, :], ALU.mult).then_inc(s_z, 1)

        def dve_rows1(dve):
            dve.wait_ge(s_z, 1)
            nc.vector.tensor_scalar(rz_i[:], rz_i[:], col[0:MH, C_BI:C_BI + 1], None,
                                    ALU.add).then_inc(s_row, 1)
            nc.vector.tensor_scalar(rz_f[:], rz_f[:], col[0:MH, C_BF:C_BF + 1], None,
                                    ALU.add).then_inc(s_row, 1)
            nc.vector.memset(rows[:], 0.0).then_inc(s_row, 1)
            nc.vector.memset(r_d[:], 1.0).then_inc(s_row, 1)
            dve.wait_ge(s_row, 5)
            d_starts = r_d[:].rearrange("h (c l) -> h c l", l=P)
            nc.vector.memset(d_starts[:, :, 0:1], 0.0).then_inc(s_row, 1)
            nc.vector.memset(r_mp[:], 0.0).then_inc(s_row, 1)

        def dve_rows2(dve):
            chunk = lambda t: t[:].rearrange("h (c l) -> h c l", l=P)
            dve.wait_ge(s_rowa, 3)
            dve.wait_ge(s_row, 7)
            nc.vector.scalar_tensor_tensor(rz_f[:], rz_f[:], 0.0, r_t[:], ALU.min,
                                           ALU.subtract).then_inc(s_row, 1)
            dve.wait_ge(s_row, 8)
            nc.vector.tensor_tensor_scan(r_b[:], r_d[:], rz_f[:], 0.0, ALU.mult,
                                         ALU.add).then_inc(s_row, 1)
            dve.wait_ge(s_row, 9)
            nc.vector.tensor_tensor(rows[0:MH, :], rz_i[:], r_b[:], ALU.subtract).then_inc(s_row, 1)
            nc.vector.memset(r_d[:], 0.0).then_inc(s_row, 1)
            dve.wait_ge(s_row, 11)
            nc.vector.tensor_copy(chunk(r_d)[:, 1:, 0:1], chunk(r_b)[:, :-1, P - 1:P]).then_inc(s_row, 1)
            dve.wait_ge(s_row, 12)
            dve.wait_ge(s_xs, 16 * KT)
            nc.vector.tensor_tensor_scan(m_rows[:], r_d[:], rows[0:MH, :], 0.0, ALU.add,
                                         ALU.max).then_inc(s_row, 1)

        def dve_rows3(dve):
            chunk = lambda t: t.rearrange("h (c l) -> h c l", l=P)
            dve.wait_ge(s_row, 13)
            mc, bc = chunk(m_rows[:]), chunk(r_b[:])
            nc.vector.tensor_tensor(r_mp[:, 1:].unsqueeze(2), mc[:, :-1, P - 1:P], bc[:, :-1, P - 1:P],
                                    ALU.add).then_inc(s_row, 1)
            nc.vector.tensor_tensor(chunk(rows[32:32 + MH, :]), chunk(rows[0:MH, :]),
                                    mc[:, :, P - 1:P].to_broadcast([MH, NB, P]),
                                    ALU.subtract).then_inc(s_row, 1)
            nc.vector.tensor_tensor(rows[96:96 + MH, :], m_rows[:], r_b[:], ALU.add).then_inc(s_row, 1)
            dve.wait_ge(s_row, 16)
            nc.vector.tensor_tensor(chunk(rows[64:64 + MH, :]), r_mp[:].unsqueeze(2).to_broadcast([MH, NB, P]),
                                    mc, ALU.subtract).then_inc(s_row, 1)

        def dve_cols(dve):
            dve.wait_ge(s_rt, 1)
            nc.vector.tensor_copy(cb_all[:, :, 0:4, :],
                                  ps[2][:].rearrange("p (c k l) -> p c k l", c=NB, k=4)[:, :, :, 0:MH]
                                  ).then_inc(s_cb, 1)

        def dve_z(dve, ee, par):
            dve.wait_ge(s_unit, val(ee + (M_PROJ + 1)))
            nc.vector.tensor_tensor(z[par][:, 3:3 + S], ps[par][:], rstd_b[:], ALU.mult).then_inc(s_z, 1)

        def y_free(dve, ee, slot, peeled):
            if not peeled:
                dve.wait_ge(s_st[slot], val(ee * 8 + (-8 if slot else -16)))

        def dve_proj(dve):
            split_lo(dve, U_PROJ + 2, U_PROJ % 2)
            dve_stats(dve, 1)
            dve.wait_ge(s_rb, 2)
            dve_rows0(dve)
            nc.vector.memset(z[0][:, 0:3], 0.0).then_inc(s_pad, 1)
            nc.vector.memset(z[1][:, 0:3], 0.0).then_inc(s_pad, 1)
            dve.wait_ge(s_cs, 32)

            def rope(ee, par, peeled=False):
                split_lo(dve, ee + (U_PROJ + 2), par)
                if ee != 1:
                    dve.wait_ge(s_rm, val(ee * 2 - 2))
                dve_z(dve, ee, par)
                y_free(dve, ee, par, peeled)
                dve.wait_ge(s_z, val(ee + 1))
                nc.vector.tensor_tensor(y[par][:], z[par][:, 3:3 + S], rope_c[:], ALU.mult).then_inc(s_rm, 1)
                dve.wait_ge(s_swap, val(ee * 4))
                nc.vector.tensor_tensor(swapped[:], swapped[:], rope_s[:], ALU.mult).then_inc(s_rm, 1)
                dve.wait_ge(s_rm, val(ee * 2))
                nc.vector.tensor_tensor(y[par][:], y[par][:], swapped[:], ALU.add).then_inc(s_y, 1)

            def raw(ee, par):
                split_lo(dve, ee + (U_PROJ + 2), par)
                dve.wait_ge(s_unit, val(ee + (M_PROJ + 1)))
                y_free(dve, ee, par, False)
                nc.vector.tensor_tensor(y[par][:], ps[par][:], rstd_b[:], ALU.mult).then_inc(s_z, 1)

            rope(1, 1, True)
            rope(2, 0, True)
            with dve.Fori(0, N_ROPE // 2 - 1) as reg:
                for j in range(2):
                    rope(Lin(reg, 2, 3 + j), (1 + j) % 2)
            raw(11, 1)
            raw(12, 0)
            with dve.Fori(0, N_CONV // 2) as reg:
                for j in range(2):
                    ee, par = Lin(reg, 2, 13 + j), (1 + j) % 2
                    split_lo(dve, ee + (U_PROJ + 2), par)
                    dve.wait_ge(s_pad, 2)
                    dve_z(dve, ee, par)
                    y_free(dve, ee, par, False)
                    dve.wait_ge(s_z, val(ee + 1))
                    k0 = Lin(reg, 10, C_CONV + 5 * j)
                    c = lambda t: col[:, bass.ds(val(k0 + t), 1)]
                    nc.vector.tensor_scalar(y[par][:], z[par][:, 3:3 + S], c(3), c(4), ALU.mult,
                                            ALU.add).then_inc(s_cv, 1)
                    for t in (2, 1, 0):
                        dve.wait_ge(s_cv, val(Lin(reg, 8, 4 * j + 3 - t)))
                        nc.vector.scalar_tensor_tensor(y[par][:], z[par][:, t:t + S], c(t), y[par][:],
                                                       ALU.mult, ALU.add).then_inc(s_cv, 1)
            raw(21, 1)
            dve_rows1(dve)
            raw(22, 0)
            raw(23, 1)
            dve_rows2(dve)
            raw(24, 0)
            dve_rows3(dve)

            def raws(first, count):
                with dve.Fori(0, count // 2) as reg:
                    for j in range(2):
                        raw(Lin(reg, 2, first + j), (1 + j) % 2)

            raws(25, 4)
            dve_cols(dve)
            dve_block_init(dve)
            raws(29, 2)
            dve.wait_ge(s_so, 1)
            nc.vector.tensor_copy(cb_all[:, :, 4, :],
                                  ps[3][:, 0:NB * MH].rearrange("p (c h) -> p c h", c=NB)).then_inc(s_sos, 1)
            raws(31, 4)
            dve_keys(dve, 0)
            raws(35, 2)

        def sp_proj(sp):
            def store(ee, par, ready):
                sp.wait_ge(ready[0], val(ready[1]))
                sp.dma_start(zs[val(ee - 1)], y[par][:]).then_inc(s_st[par], 16)

            def tick(ee, k, ready):
                load_unit(sp, ee + (U_PROJ + 2), k % 2)
                store(ee - 1, 1 - k % 2, ready)

            sp.wait_ge(s_down, FT * KT // 2)
            sp.dma_start(rope_c[:], rope_cs[0]).then_inc(s_cs, 16)
            sp.dma_start(rope_s[:], rope_cs[1]).then_inc(s_cs, 16)
            load_unit(sp, U_PROJ + 2, U_PROJ % 2)
            load_unit(sp, U_PROJ + 3, (U_PROJ + 1) % 2)
            for d in range(KT):
                sp.wait_ge(s_xadd, PAIRS * KT - KT + d + 1)
                sp.dma_start(x_s[:, d, :], x[:, d, :]).then_inc(s_xs, 16)
            sp.wait_ge(s_xs, 16 * KT)
            for dst, src in ((mk0, masks[:, 0]), (mk, masks[:, 1]), (sinkc, sinks), (mbig, mask_big), (selh, sel_head),
                             (sell, sel_last)):
                sp.dma_start(dst[:], src).then_inc(s_bconst, 16)
            with sp.Fori(0, N_ROPE // 2) as reg:
                for j in range(2):
                    tick(Lin(reg, 2, 2 + j), j, (s_y, Lin(reg, 2, 1 + j)))
            for ee in (12, 13):
                tick(ee, ee, (s_z, ee))
            with sp.Fori(0, N_CONV // 2) as reg:
                for j in range(2):
                    tick(Lin(reg, 2, 14 + j), j, (s_y, Lin(reg, 2, N_ROPE + 1 + j)))
            for i in range(2):
                sp.wait_ge(s_st[i], 16 * 6)
            load_qk(sp, 0)
            load_v(sp, 0)
            with sp.Fori(0, N_RAW // 2 - 1) as reg:
                for j in range(2):
                    tick(Lin(reg, 2, 22 + j), j, (s_z, Lin(reg, 2, 22 + j)))


        b = {name: sem(f"b_{name}") for name in (
            "qk_landed",
            "v_landed",
            "mlstm_landed",
            "k_moved",
            "qk_hi",
            "qk_lo",
            "v_turned",
            "v_ready",
            "scores",
            "masked",
            "neg_max",
            "sink_less_max",
            "exp",
            "denominator",
            "divided",
            "probs",
            "probs_turned",
            "probs_t",
            "weighed",
            "att_out",
            "att_stored",
            "ml_scores",
            "maxima_spread",
            "decay_masked",
            "decay",
            "ml_probs",
            "mv_turned",
            "mv_ready",
            "mk_turned",
            "mk_weighed",
            "num_new",
            "num_old",
            "state_new",
            "num_scaled",
            "num",
            "state",
            "norm_steps",
            "squares",
            "root_steps",
            "h",
            "h_turned",
            "h_t",
            "h_stored",
            "gate_scaled",
            "init",
            "columns",
            "v_moved",
            "k_lo_moved",
            "newton",
        )}
        s_gst = [sem(f"s_gst{i}") for i in range(2)]
        s_ld = [sem(f"s_ld{i}") for i in range(4)]
        s_fhi = sem("s_fhi")
        s_flo = sem("s_flo")
        att_stage = [sm[0], sm[1], ptb[0], ptb[1]]

        def lin(n, k, c):
            return n * k + c

        def pcol(g):
            return (g % 2) * HALF + (g // 2) * 2 * P

        def pe_htt(pe, n):
            pe.wait_ge(b["h"], val(n))
            for t in range(KT):
                mm = nc.tensor.transpose(ps[3][:, t * P:(t + 1) * P], hn[:, t * P:(t + 1) * P], ident[:])
            mm.then_inc(b["h_turned"], 1)

        def pe_block(pe, n, first=False):
            def scores(j):
                for g in range(GROUP):
                    o = ps[1 + j % 2][:, pcol(g):pcol(g) + 2 * P]
                    nc.tensor.matmul(o, q_hl[:, GROUP * j + g, :], k_hi[:, j, :], start=True, stop=False,
                                     skip_group_check=True)
                    mm = nc.tensor.matmul(o, q_hl[0:HD, GROUP * j + g, :], k_lo[0:HD, j, :], start=False,
                                          stop=True, skip_group_check=True)
                mm.then_inc(b["scores"], 1)

            def turn_p(j):
                pe.wait_ge(b["probs"], val(lin(n, 4, j + 1)))
                for t in range(1, 2 * GROUP, 2) if first else range(2 * GROUP):
                    mm = nc.tensor.transpose(ps[1 + j % 2][:, t * P:(t + 1) * P],
                                             sm[j % 2][:, t * P:(t + 1) * P], ident[:])
                mm.then_inc(b["probs_turned"], 1)

            def weigh_v(j):
                pe.wait_ge(b["probs_t"], val(lin(n, 4, j + 1)))
                if j >= 2:
                    pe.wait_ge(b["att_out"], val(lin(n, 8, 2 * j - 2)))
                o = ps[3][:, (1 - j % 2) * HALF:(2 - j % 2) * HALF]
                p_t = ptb[j % 2][:].rearrange("p (g k q) -> p g k q", g=GROUP, k=2)
                for k in ((1,) if first else (0, 1)):
                    mm = nc.tensor.matmul(o.rearrange("p (g q) -> p g q", g=GROUP), vnat[:, k, j, :, :],
                                          p_t[:, :, k, :], start=(first or k == 0), stop=(k == 1))
                mm.then_inc(b["weighed"], 1)

            def gate(c, k0, k1):
                if k0 == 0:
                    pe.wait_ge(s_wlo, val(lin(n, 2, U_BLK + c + 1)))
                products(pe, ps[0], (U_BLK + c) % 2, ra_hi, ra_lo, ks=(k0, k1))

            pe.wait_ge(b["qk_lo"], val(lin(n, 2, 2)))
            if not first:
                pe.wait_ge(b["num"], val(lin(n, 4, 0)))
            scores(0)
            if not first:
                pe.wait_ge(b["num_scaled"], val(lin(n, 4, 0)))
            scores(1)
            if first:
                pe.wait_ge(s_z, PROJ_UNITS)
            else:
                pe.wait_ge(b["gate_scaled"], val(lin(n, 2, 0)))
            gate(0, 0, 4)
            if not first:
                pe.wait_ge(b["state"], val(lin(n, 4, 0)))
                pe_htt(pe, n)
            turn_p(0)
            if not first:
                pe.wait_ge(b["h_t"], val(n))
            pe.wait_ge(b["v_landed"], val(lin(n, 16, 16)))
            for t in range(2):
                mm = nc.tensor.transpose(ps[3][:, t * P:(t + 1) * P], zv[:, t, :], ident[:])
            mm.then_inc(b["v_turned"], 1)
            turn_p(1)
            pe.wait_ge(b["v_ready"], val(lin(n, 1, 1)))
            weigh_v(0)
            scores(2)
            weigh_v(1)
            scores(3)
            gate(0, 4, 7)
            turn_p(2)
            gate(0, 7, 8)
            turn_p(3)
            weigh_v(2)
            pe.wait_ge(b["mlstm_landed"], val(lin(n, 32, 32)))
            pe.wait_ge(b["gate_scaled"], val(lin(n, 2, 1)))
            for t in range(KT):
                mm = nc.tensor.transpose(ps[0][:, t * P:(t + 1) * P], zm[:, t, :], ident[:])
            mm.then_inc(b["mv_turned"], 1)
            for h in range(MH):
                mm = nc.tensor.matmul(ps[1][:, h * P:(h + 1) * P], selh[:, h, :],
                                      m_rows[:, bass.ds(val(lin(n, P, 0)), P)], start=True, stop=True,
                                      skip_group_check=True)
            mm.then_inc(b["maxima_spread"], 1)
            for h in range(MH):
                mm = nc.tensor.matmul(ps[1][:, HALF + h * P:HALF + (h + 1) * P], zm[:, KT + 2 * h + 1, :],
                                      zm[:, KT + 2 * h, :], start=True, stop=True, skip_group_check=True)
            mm.then_inc(b["ml_scores"], 1)
            weigh_v(3)
            for h in range(MH):
                mm = nc.tensor.transpose(ps[2][:, h * P:(h + 1) * P], zm[:, KT + 2 * h + 1, :], ident[:])
            mm.then_inc(b["mk_turned"], 1)
            pe.wait_ge(b["mv_ready"], val(lin(n, 1, 1)))
            gate(1, 0, 3)
            pe.wait_ge(b["ml_probs"], val(lin(n, 1, 1)))
            pe.wait_ge(b["att_out"], val(lin(n, 8, 8)))
            for h in range(MH):
                o = slice((h % 2) * HALF, (h % 2) * HALF + NA)
                if h == 2:
                    gate(1, 3, 5)
                if h >= 2:
                    pe.wait_ge(b["num"], val(lin(n, 4, h - 1)))
                nc.tensor.matmul(ps[1][:, o], ptm[:, h * P:(h + 1) * P], vmn[:, h, 0:NA], start=True,
                                 stop=True).then_inc(b["num_new"], 1)
                nc.tensor.matmul(ps[2][:, o], zm[:, KT + 2 * h, :], cst[:, h, 0:NA], start=True,
                                 stop=True).then_inc(b["num_old"], 1)
                if h >= 2:
                    pe.wait_ge(b["state"], val(lin(n, 4, h - 1)))
                nc.tensor.matmul(ps[3][:, o], ka[:, h * P:(h + 1) * P], vmn[:, h, 0:NA], start=True,
                                 stop=True).then_inc(b["state_new"], 1)
            gate(1, 5, 8)

        def act_keys(act, n):
            if not isinstance(n, int) or n:
                act.wait_ge(b["scores"], val(lin(n, 4, 0)))
            act.wait_ge(b["qk_landed"], val(lin(n, 128, 128)))
            nc.scalar.copy(k_hi[:, :, 0:P], k_hi[:, :, P:2 * P]).then_inc(b["k_moved"], 1)
            nc.scalar.copy(q_hl[:], zq[:]).then_inc(b["qk_hi"], 1)
            act.wait_ge(b["k_moved"], val(lin(n, 1, 1)))
            nc.scalar.copy(k_hi[:, :, P:2 * P], zk[:]).then_inc(b["qk_hi"], 1)

        def dve_keys(dve, n):
            dve.wait_ge(b["qk_hi"], val(lin(n, 2, 2)))
            nc.vector.tensor_tensor(q_hl[HD:P, :, :], zq[HD:P, :, :], q_hl[HD:P, :, :].bitcast(F32),
                                    ALU.subtract).then_inc(b["qk_lo"], 1)
            nc.vector.tensor_copy(k_lo[0:HD, :, 0:P], k_lo[0:HD, :, P:2 * P].bitcast(F32)).then_inc(b["k_lo_moved"], 1)
            dve.wait_ge(b["k_lo_moved"], val(lin(n, 1, 1)))
            nc.vector.tensor_tensor(k_lo[0:HD, :, P:2 * P], zk[0:HD], k_hi[0:HD, :, P:2 * P].bitcast(F32),
                                    ALU.subtract).then_inc(b["qk_lo"], 1)

        def pool_hn(pool, n):
            pool.wait_ge(b["root_steps"], val(lin(n, 2, 0)))
            nc.gpsimd.tensor_tensor(yy[:], y0[:], y0[:], ALU.mult).then_inc(b["newton"], 1)
            pool.wait_ge(b["newton"], val(lin(n, 5, -4)))
            pool.wait_ge(b["norm_steps"], val(lin(n, 5, 0)))
            nc.gpsimd.tensor_tensor(yy[:], yy[:], half_var[:], ALU.mult).then_inc(b["newton"], 1)
            pool.wait_ge(b["newton"], val(lin(n, 5, -3)))
            nc.gpsimd.tensor_tensor(yy[:], yy[:], three_halves[:], ALU.add).then_inc(b["newton"], 1)
            pool.wait_ge(b["newton"], val(lin(n, 5, -2)))
            nc.gpsimd.tensor_tensor(yc[:], yy[:], y0[:], ALU.mult).then_inc(b["newton"], 1)
            pool.wait_ge(b["newton"], val(lin(n, 5, -1)))
            nc.gpsimd.tensor_tensor(scl[:], yc[:], rn[:], ALU.mult).then_inc(b["newton"], 1)
            pool.wait_ge(b["newton"], val(lin(n, 5, 0)))
            nc.gpsimd.tensor_tensor(hn[:].rearrange("p (h v) -> p h v", h=MH), nd[:, :, 0:DV],
                                    scl[:].unsqueeze(2).to_broadcast([P, MH, DV]),
                                    ALU.mult).then_inc(b["h"], 1)

        def act_hte(act, n):
            act.wait_ge(b["h_turned"], val(n))
            if not isinstance(n, int) or n > 1:
                act.wait_ge(b["h_stored"], val(lin(n, 16, -16)))
            nc.scalar.copy(ht[:], ps[3][:]).then_inc(b["h_t"], 1)

        def act_att_hi(act, k):
            act.wait_ge(s_ld[k % 4], 16 * (k // 4 + 1))
            act.wait_ge(s_unit, M_MERGE)
            nc.scalar.copy(ra_hi[:, k, :], att_stage[k % 4][:]).then_inc(s_fhi, 1)

        def dve_att_lo(dve, k):
            dve.wait_ge(s_fhi, k + 1)
            nc.vector.tensor_tensor(ra_lo[:, k, :], att_stage[k % 4][:], ra_hi[:, k, :].bitcast(F32),
                                    ALU.subtract).then_inc(s_flo, 1)

        def load_att(sp, k):
            if k >= 4:
                sp.wait_ge(s_flo, k - 3)
            sp.dma_start(att_stage[k % 4][:], att_s[k, :, P:]).then_inc(s_ld[k % 4], 16)

        def act_block(act, n, first=False, last=False):
            def exps(j):
                act.wait_ge(b["neg_max"], val(lin(n, 4, j + 1)))
                for g in range(GROUP):
                    h = GROUP * j + g
                    p = sm[j % 2][:, pcol(g):pcol(g) + 2 * P]
                    nc.scalar.activation(p, p, ACT.Exp, bias=nm[:, h:h + 1], scale=HD ** -0.5,
                                         accum_out=rs[:, h:h + 1]).then_inc(b["exp"], 1)
                act.wait_ge(b["sink_less_max"], val(lin(n, 4, j + 1)))
                q = slice(GROUP * j, GROUP * (j + 1))
                nc.scalar.activation(es[:, q], sn[:, q], ACT.Exp).then_inc(b["exp"], 1)

            def take_p(j):
                act.wait_ge(b["probs_turned"], val(lin(n, 4, j + 1)))
                if j >= 2:
                    act.wait_ge(b["weighed"], val(lin(n, 4, j - 1)))
                nc.scalar.copy(ptb[j % 2][:], ps[1 + j % 2][:]).then_inc(b["probs_t"], 1)

            exps(0)
            exps(1)
            if not first:
                act_hte(act, n)
            take_p(0)
            if not first:
                split_hi(act, lin(n, 2, U_BLK + 1), (U_BLK + 1) % 2, (s_unit, lin(n, 2, M_BLK)))
            take_p(1)
            exps(2)
            exps(3)
            take_p(2)
            split_hi(act, lin(n, 2, U_BLK + 2), U_BLK % 2, (s_unit, lin(n, 2, M_BLK + 1)))
            take_p(3)
            act.wait_ge(b["mv_turned"], val(lin(n, 1, 1)))
            nc.scalar.copy(vmn[:, :, 0:DV], ps[0][:].rearrange("p (h v) -> p h v", h=MH)).then_inc(b["mv_ready"], 1)
            act.wait_ge(b["decay_masked"], val(lin(n, 1, 1)))
            for h in range(MH):
                q = slice(h * P, (h + 1) * P)
                nc.scalar.activation(dt_[:, q], dm[:, q], ACT.Exp, bias=cb[:, 0, h:h + 1],
                                     scale=-1.0).then_inc(b["decay"], 1)
            if not last:
                act_keys(act, n + 1)
            for h in range(MH):
                act.wait_ge(b["num_old"], val(lin(n, 4, h + 1)))
                if h >= 2:
                    act.wait_ge(b["num"], val(lin(n, 4, h - 1)))
                nc.scalar.activation(tmp[h % 2][:, 0:NA], ps[2][:, (h % 2) * HALF:(h % 2) * HALF + NA],
                                     ACT.Copy, scale=cb[:, 2, h:h + 1]).then_inc(b["num_scaled"], 1)
            act.wait_ge(b["norm_steps"], val(lin(n, 5, 3)))
            for h in range(MH):
                nc.scalar.activation(hn[:, h * DV:(h + 1) * DV], nd[:, h, 0:DV], ACT.Square,
                                     scale=rn[:, h:h + 1], accum_out=ssq[:, h:h + 1]).then_inc(b["squares"], 1)
            if last:
                for k in range(4):
                    act_att_hi(act, k)
            act.wait_ge(b["norm_steps"], val(lin(n, 5, 4)))
            nc.scalar.activation(lv[:], var[:], ACT.Ln).then_inc(b["root_steps"], 1)
            act.wait_ge(b["root_steps"], val(lin(n, 2, 1)))
            nc.scalar.activation(y0[:], lv[:], ACT.Exp, scale=-0.5).then_inc(b["root_steps"], 1)

        def dve_block(dve, n, first=False, last=False):
            def maxima(j):
                dve.wait_ge(b["scores"], val(lin(n, 4, j + 1)))
                nc.vector.memset(turn[:], 0.0)
                for g in range(GROUP):
                    h = GROUP * j + g
                    q = slice(pcol(g), pcol(g) + 2 * P)
                    nc.vector.tensor_tensor_reduce(sm[j % 2][:, q], ps[1 + j % 2][:, q], (mk0 if first else mk)[:],
                                                   1.0, sink8[:, h:h + 1], ALU.add, ALU.max,
                                                   mx[:, h:h + 1]).then_inc(b["masked"], 1)
                q = slice(GROUP * j, GROUP * (j + 1))
                dve.wait_ge(b["masked"], val(lin(n, 16, 4 * j + 4)))
                nc.vector.tensor_scalar(nm[:, q], mx[:, q], -HD ** -0.5, None, ALU.mult).then_inc(b["neg_max"], 1)
                dve.wait_ge(b["neg_max"], val(lin(n, 4, j + 1)))
                nc.vector.tensor_tensor(sn[:, q], sinkc[:, q], nm[:, q], ALU.add).then_inc(b["sink_less_max"], 1)

            def divisors(j):
                q = slice(GROUP * j, GROUP * (j + 1))
                dve.wait_ge(b["exp"], val(lin(n, 20, 5 * j + 5)))
                nc.vector.tensor_tensor(rd[:, q], rs[:, q], es[:, q], ALU.add).then_inc(b["denominator"], 1)
                dve.wait_ge(b["denominator"], val(lin(n, 4, j + 1)))
                nc.vector.reciprocal(rd[:, q], rd[:, q]).then_inc(b["divided"], 1)
                dve.wait_ge(b["divided"], val(lin(n, 4, j + 1)))
                p = sm[j % 2][:].rearrange("p (a b k) -> p a b k", a=2, b=2)
                nc.vector.tensor_tensor(p, p, rd[:, q].rearrange("p (b a) -> p a b", a=2).unsqueeze(3)
                                        .to_broadcast([P, 2, 2, 2 * P]), ALU.mult).then_inc(b["probs"], 1)

            def outputs(j):
                dve.wait_ge(b["weighed"], val(lin(n, 4, j + 1)))
                if j == 0:
                    if first:
                        dve.wait_ge(s_st[1], 16 * (Z_TILES // 2))
                    else:
                        dve.wait_ge(b["att_stored"], val(lin(n, 16, 0)))
                for a in range(2):
                    rows_a, c0 = slice(64 * a, 64 * a + 64), (1 - j % 2) * HALF + 2 * P * a
                    nc.vector.tensor_copy(ot[rows_a, 2 * j:2 * j + 2, :],
                                          ps[3][rows_a, c0:c0 + 2 * P].rearrange("p (t q) -> p t q", t=2)
                                          ).then_inc(b["att_out"], 1)

            maxima(0)
            maxima(1)
            divisors(0)
            divisors(1)
            nc.vector.tensor_copy(cb[:], cb_all[:, bass.ds(val(n), 1), :, :].rearrange("p c k h -> p (c k) h")
                                  ).then_inc(b["columns"], 1)
            nc.vector.tensor_copy(vnat[:, 0], vnat[:, 1]).then_inc(b["v_moved"], 1)
            dve.wait_ge(b["v_turned"], val(lin(n, 1, 1)))
            dve.wait_ge(b["v_moved"], val(lin(n, 1, 1)))
            nc.vector.tensor_copy(vnat[:, 1], ps[3][:, 0:2 * P].rearrange("p (j v) -> p j v", j=KV_HEADS)
                                  .unsqueeze(2).to_broadcast([P, KV_HEADS, 2, HD])).then_inc(b["v_ready"], 1)
            outputs(0)
            maxima(2)
            outputs(1)
            maxima(3)
            divisors(2)
            divisors(3)
            dve.wait_ge(s_unit, val(lin(n, 2, M_BLK + 1)))
            if not first:
                dve.wait_ge(s_gst[0], val(lin(n, 16, 0)))
            nc.vector.tensor_tensor(t_a[:], ps[0][:], rstd_b[:], ALU.mult).then_inc(b["gate_scaled"], 1)
            if not first:
                split_lo(dve, lin(n, 2, U_BLK + 1), (U_BLK + 1) % 2)
            split_lo(dve, lin(n, 2, U_BLK + 2), U_BLK % 2)
            outputs(2)
            dve.wait_ge(b["maxima_spread"], val(lin(n, 1, 1)))
            nc.vector.tensor_tensor(dm[:].rearrange("p (h l) -> p h l", h=MH),
                                    ps[1][:, 0:HALF].rearrange("p (h l) -> p h l", h=MH),
                                    mbig[:].unsqueeze(1).to_broadcast([P, MH, P]), ALU.add).then_inc(b["decay_masked"], 1)
            outputs(3)
            dve.wait_ge(b["mk_turned"], val(lin(n, 1, 1)))
            dve.wait_ge(b["columns"], val(lin(n, 1, 1)))
            nc.vector.tensor_tensor(ka[:].rearrange("p (h l) -> p h l", h=MH),
                                    ps[2][:, 0:HALF].rearrange("p (h l) -> p h l", h=MH),
                                    cb[:, 1, :].unsqueeze(2).to_broadcast([P, MH, P]),
                                    ALU.mult).then_inc(b["mk_weighed"], 1)
            dve.wait_ge(b["ml_scores"], val(lin(n, 1, 1)))
            dve.wait_ge(b["decay"], val(lin(n, 4, 4)))
            nc.vector.tensor_tensor(ptm[:], ps[1][:, HALF:2 * HALF], dt_[:], ALU.mult).then_inc(b["ml_probs"], 1)
            if not last:
                dve_keys(dve, n + 1)
            for h in range(MH):
                o = slice((h % 2) * HALF, (h % 2) * HALF + NA)
                dve.wait_ge(b["num_new"], val(lin(n, 4, h + 1)))
                dve.wait_ge(b["num_scaled"], val(lin(n, 4, h + 1)))
                nc.vector.tensor_tensor(nd[:, h, 0:NA], ps[1][:, o], tmp[h % 2][:, 0:NA],
                                        ALU.add).then_inc(b["num"], 1)
                dve.wait_ge(b["state_new"], val(lin(n, 4, h + 1)))
                nc.vector.scalar_tensor_tensor(cst[:, h, 0:NA], cst[:, h, 0:NA], cb[:, 4, h:h + 1],
                                               ps[3][:, o], ALU.mult, ALU.add).then_inc(b["state"], 1)
            dve.wait_ge(b["num"], val(lin(n, 4, 4)))
            if not first:
                dve.wait_ge(b["h"], val(n))
            nc.vector.tensor_tensor(dn[:], nd[:, :, DV], cb[:, 3, :], ALU.max).then_inc(b["norm_steps"], 1)
            dve.wait_ge(b["norm_steps"], val(lin(n, 5, 1)))
            nc.vector.scalar_tensor_tensor(dn[:], nd[:, :, DV], -1.0, dn[:], ALU.mult,
                                           ALU.max).then_inc(b["norm_steps"], 1)
            dve.wait_ge(b["norm_steps"], val(lin(n, 5, 2)))
            nc.vector.reciprocal(rn[:], dn[:]).then_inc(b["norm_steps"], 1)
            dve.wait_ge(b["squares"], val(lin(n, 4, 4)))
            nc.vector.tensor_scalar(var[:], ssq[:], 1.0 / DV, EPS, ALU.mult, ALU.add).then_inc(b["norm_steps"], 1)
            nc.vector.tensor_scalar(half_var[:], ssq[:], -0.5 / DV, -0.5 * EPS, ALU.mult,
                                    ALU.add).then_inc(b["norm_steps"], 1)
            dve.wait_ge(s_unit, val(lin(n, 2, M_BLK + 2)))
            if not first:
                dve.wait_ge(s_gst[1], val(lin(n, 16, 0)))
            nc.vector.tensor_tensor(t_b[:], ps[0][:], rstd_b[:], ALU.mult).then_inc(b["gate_scaled"], 1)

        def load_qk(sp, n):
            for dst, t0, t1 in ((zq, 0, 8), (zk, 8, 10)):
                for half in range(2):
                    for odd in range(2):
                        sp.dma_start(dst[HD * half:HD * (half + 1), odd::2, :],
                                     zs[t0:t1, HD * odd:HD * (odd + 1), bass.ds(val(lin(n, P, 0)), P)]
                                     .rearrange("t p c -> p t c")).then_inc(b["qk_landed"], 16)

        def load_v(sp, n):
            sp.dma_start(zv[:], zs[10:12, :, bass.ds(val(lin(n, P, 0)), P)].rearrange("t p c -> p t c")
                         ).then_inc(b["v_landed"], 16)

        def load_mlstm(sp, n):
            sp.wait_ge(s_st[0], 16 * (Z_TILES // 2))
            for i, t in enumerate((N_ROPE + 10, N_ROPE + 2)):
                sp.dma_start(zm[:, 8 * i:8 * i + 8, :],
                             zs[t:t + 8, :, bass.ds(val(lin(n, P, 0)), P)].rearrange("t p c -> p t c")
                             ).then_inc(b["mlstm_landed"], 16)

        def store_ht(sp, n):
            sp.wait_ge(b["h_t"], val(n))
            sp.dma_start(mem_s[:, :, bass.ds(val(n * P), P)].rearrange("t p c -> p t c"),
                         ht[:].rearrange("p (t l) -> p t l", t=KT)).then_inc(b["h_stored"], 16)

        def sp_block(sp, n, first=False, last=False):
            if not first:
                load_unit(sp, lin(n, 2, U_BLK + 2), U_BLK % 2)
                store_ht(sp, n)
            if not last:
                sp.wait_ge(b["qk_lo"], val(lin(n, 2, 2)))
                load_qk(sp, n + 1)
                sp.wait_ge(b["v_turned"], val(lin(n, 1, 1)))
                load_v(sp, n + 1)
            load_unit(sp, lin(n, 2, U_BLK + 3), (U_BLK + 1) % 2)
            sp.wait_ge(b["gate_scaled"], val(lin(n, 2, 1)))
            sp.dma_start(gs[val(lin(n, 2, 0))], t_a[:]).then_inc(s_gst[0], 16)
            sp.wait_ge(b["att_out"], val(lin(n, 8, 8)))
            sp.dma_start(att_s[:, :, bass.ds(val(n * P + P), P)].rearrange("t p c -> p t c"),
                         ot[:]).then_inc(b["att_stored"], 16)
            if last:
                sp.wait_ge(b["att_stored"], 16 * NB)
                for k in range(4):
                    load_att(sp, k)
            else:
                sp.wait_ge(b["num_old"], val(lin(n, 4, 4)))
                load_mlstm(sp, n + 1)
            sp.wait_ge(b["gate_scaled"], val(lin(n, 2, 2)))
            sp.dma_start(gs[val(lin(n, 2, 1))], t_b[:]).then_inc(s_gst[1], 16)

        def sp_blocks(sp):
            for i in range(2):
                sp.wait_ge(s_st[i], 16 * (Z_TILES // 2))
            load_mlstm(sp, 0)
            sp_block(sp, 0, first=True)
            with sp.Fori(1, NB - 1) as reg:
                sp_block(sp, Lin(reg))
            sp_block(sp, NB - 1, last=True)
            for k in range(4, KT):
                load_att(sp, k)

        def pe_blocks(pe):
            pe.wait_ge(s_z, PROJ_UNITS - 1)
            pe.wait_ge(s_sos, 1)
            pe_block(pe, 0, first=True)
            with pe.Fori(1, NB) as reg:
                pe_block(pe, Lin(reg))

        def act_blocks(act):
            act_block(act, 0, first=True)
            act_block(act, 1)
            with act.Fori(2, NB - 1) as reg:
                act_block(act, Lin(reg))
            act_block(act, NB - 1, last=True)

        def dve_block_init(dve):
            dve.wait_ge(s_bconst, 16 * N_BCONST)
            nc.vector.memset(k_hi[:].bitcast(F32), 0.0).then_inc(b["init"], 1)
            nc.vector.memset(k_lo[:].bitcast(F32), 0.0).then_inc(b["init"], 1)
            nc.vector.memset(vnat[:], 0.0).then_inc(b["init"], 1)
            nc.vector.memset(cst[:], 0.0).then_inc(b["init"], 1)
            nc.vector.tensor_scalar(sink8[:], sinkc[:], HD ** 0.5, None, ALU.mult).then_inc(b["init"], 1)

        def dve_blocks(dve):
            nc.vector.memset(vmn[:, :, DV:DV + 1], 1.0).then_inc(b["init"], 1)
            nc.vector.memset(three_halves[:], 1.5).then_inc(b["init"], 1)
            dve.wait_ge(b["init"], 7)
            dve.wait_ge(s_sos, 1)
            dve_block(dve, 0, first=True)
            with dve.Fori(1, NB - 1) as reg:
                dve_block(dve, Lin(reg))
            dve_block(dve, NB - 1, last=True)

        s_sg = sem("s_sg")
        s_sgo = sem("s_sgo")
        s_ym = sem("s_ym")
        s_ysum = sem("s_ysum")
        s_mem = sem("s_mem")
        s_xfin = sem("s_xfin")
        s_lg = [sem(f"s_lg{i}") for i in range(2)]
        s_lgo = [sem(f"s_lgo{i}") for i in range(2)]
        s_lm = [sem(f"s_lm{i}") for i in range(2)]
        s_lx = sem("s_lx")
        w_slot = [U_MERGE % 2, 1 - U_MERGE % 2]
        gate_stage = [[x[:, KT - 1, :], t_a], [rstd_b, sqacc]]
        o_stage = [rstd_b, sqacc]
        mem_stage = [t_b, sq[0]]

        def pe_merge(pe):
            for part, (hi, lo) in enumerate(((ra_hi, ra_lo), (rb_hi, rb_lo), (ra_hi, ra_lo))):
                def unit(c, k_wait=None, ks=(0, KT)):
                    u = c + (U_MERGE + KT * part)
                    j = (c if isinstance(c, int) else c.a) % 2
                    pe.wait_ge(s_wlo, val(u + 1))
                    if part == 0:
                        if isinstance(c, int):
                            if c == 0:
                                pe.wait_ge(b["gate_scaled"], 2 * NB)
                            else:
                                pe.wait_ge(b["num"], MH * NB)
                        else:
                            pe.wait_ge(s_ym, val(c - 1))
                    elif part == 1:
                        pe.wait_ge(s_ym, val(c + (KT - 1)))
                    elif isinstance(c, int):
                        pe.wait_ge(s_ym, 2 * KT - 1 + c)
                    else:
                        pe.wait_ge(s_xfin, val(c - 1))
                    products(pe, ps[j], w_slot[j], hi, lo, k_wait=k_wait, ks=ks)

                unit(0, k_wait=(s_flo, KT * part))
                if part == 0:
                    pe.wait_ge(b["state"], 4 * NB)
                    pe_htt(pe, NB)
                unit(1)
                with pe.Fori(0, KT // 2 - 1) as reg:
                    for j in range(2):
                        unit(Lin(reg, 2, 2 + j))

        def act_merge(act):
            for k in range(4, KT):
                act_att_hi(act, k)
            split_hi(act, U_MERGE + 1, w_slot[1], (s_unit, M_MERGE))
            act_hte(act, NB)

            def branch(part):
                with act.Fori(0, KT // 2) as reg:
                    for j in range(2):
                        c = Lin(reg, 2, j)
                        gate = gate_stage[part][j][:]
                        act.wait_ge(s_lg[j], val(Lin(reg, 16, 16 + 16 * KT // 2 * part)))
                        nc.scalar.activation(gate, gate, ACT.Sigmoid).then_inc(s_sg, 1)
                        split_hi(act, c + (U_MERGE + KT * part + 2), w_slot[j],
                                 (s_unit, c + (M_MERGE + KT * part + 1)))
                        if part == 0:
                            act.wait_ge(s_lgo[j], val(Lin(reg, 16, 16)))
                            nc.scalar.activation(o_stage[j][:], o_stage[j][:], ACT.Sigmoid).then_inc(s_sgo, 1)
                            act.wait_ge(s_mem, val(c + 1))
                            nc.scalar.copy(rb_hi[:, bass.ds(val(c), 1), :].rearrange("p o s -> p (o s)"),
                                           mem_stage[j][:]).then_inc(s_fhi, 1)
                        else:
                            act.wait_ge(s_ysum, val(c + 1))
                            nc.scalar.copy(ra_hi[:, bass.ds(val(c), 1), :].rearrange("p o s -> p (o s)"),
                                           x[:, bass.ds(val(c), 1), :].rearrange("p o s -> p (o s)")
                                           ).then_inc(s_fhi, 1)

            branch(0)
            branch(1)
            for c in range(KT):
                split_hi(act, U_MERGE + 2 * KT + c + 2, w_slot[c % 2], (s_unit, M_MERGE + 2 * KT + c + 1))
                act_norm_tile(act, 2, c, rb_hi, (s_xfin, c + 1))

        def dve_merge(dve):
            for k in range(KT):
                dve_att_lo(dve, k)
            split_lo(dve, U_MERGE + 1, w_slot[1])

            def tile_of(t, c):
                return t[:, bass.ds(val(c), 1), :].rearrange("p o s -> p (o s)")

            with dve.Fori(0, KT // 2) as reg:
                for j in range(2):
                    c = Lin(reg, 2, j)
                    split_lo(dve, c + (U_MERGE + 2), w_slot[j])
                    dve.wait_ge(s_unit, val(c + (M_MERGE + 1)))
                    dve.wait_ge(s_sg, val(c + 1))
                    nc.vector.tensor_tensor(tile_of(x, c), ps[j][:], gate_stage[0][j][:], ALU.mult).then_inc(s_ym, 1)
                    dve.wait_ge(s_lm[j], val(Lin(reg, 16, 16)))
                    dve.wait_ge(s_sgo, val(c + 1))
                    nc.vector.scalar_tensor_tensor(mem_stage[j][:], mem_stage[j][:],
                                                   col[:, bass.ds(val(c + C_HN), 1)], o_stage[j][:],
                                                   ALU.mult, ALU.mult).then_inc(s_mem, 1)
                    dve.wait_ge(s_fhi, val(c + (KT + 1)))
                    nc.vector.tensor_tensor(tile_of(rb_lo, c), mem_stage[j][:], tile_of(rb_hi, c).bitcast(F32),
                                            ALU.subtract).then_inc(s_flo, 1)
            with dve.Fori(0, KT // 2) as reg:
                for j in range(2):
                    c = Lin(reg, 2, j)
                    gate = gate_stage[1][j][:]
                    split_lo(dve, c + (U_MERGE + KT + 2), w_slot[j])
                    dve.wait_ge(s_unit, val(c + (M_MERGE + KT + 1)))
                    dve.wait_ge(s_sg, val(c + (KT + 1)))
                    nc.vector.tensor_tensor(gate, ps[j][:], gate, ALU.mult).then_inc(s_ym, 1)
                    dve.wait_ge(s_ym, val(c + (KT + 1)))
                    nc.vector.tensor_tensor(tile_of(x, c), tile_of(x, c), gate, ALU.add).then_inc(s_ysum, 1)
                    dve.wait_ge(s_fhi, val(c + (2 * KT + 1)))
                    nc.vector.tensor_tensor(tile_of(ra_lo, c), tile_of(x, c), tile_of(ra_hi, c).bitcast(F32),
                                            ALU.subtract).then_inc(s_flo, 1)
            for c in range(KT):
                split_lo(dve, U_MERGE + 2 * KT + c + 2, w_slot[c % 2])
                dve.wait_ge(s_unit, M_MERGE + 2 * KT + c + 1)
                dve.wait_ge(s_lx, 16 * (c + 1))
                nc.vector.tensor_tensor(x[:, c, :], ps[c % 2][:], t_b[:], ALU.add).then_inc(s_xfin, 1)
                dve_norm_tile(dve, 2, c, rb_hi, rb_lo)

        def sp_merge(sp):
            for i in range(2):
                sp.wait_ge(s_gst[i], 16 * NB)

            def load_gate(c, j, part):
                sp.dma_start(gate_stage[part][j][:], gs[val(c * 2 + part)]).then_inc(s_lg[j], 16)

            def load_mem(c, j):
                sp.dma_start(o_stage[j][:], zs[val(c + (N_ROPE + 18))]).then_inc(s_lgo[j], 16)
                sp.dma_start(mem_stage[j][:], mem_s[val(c), :, P:]).then_inc(s_lm[j], 16)

            for c in range(2):
                load_gate(c, c, 0)
                load_unit(sp, U_MERGE + c + 2, w_slot[c])
            store_ht(sp, NB)
            sp.wait_ge(b["h_stored"], 16 * NB)
            for c in range(2):
                load_mem(c, c)
            with sp.Fori(0, KT // 2 - 1) as reg:
                for j in range(2):
                    c = Lin(reg, 2, 2 + j)
                    sp.wait_ge(s_ym, val(c - 1))
                    load_gate(c, j, 0)
                    sp.wait_ge(s_flo, val(c + (KT - 1)))
                    load_mem(c, j)
                    load_unit(sp, c + (U_MERGE + 2), w_slot[j])
            for c in range(2):
                sp.wait_ge(s_mem, KT - 1 + c)
                load_gate(c, c, 1)
                load_unit(sp, U_MERGE + KT + c + 2, w_slot[c])
            with sp.Fori(0, KT // 2 - 1) as reg:
                for j in range(2):
                    c = Lin(reg, 2, 2 + j)
                    sp.wait_ge(s_ysum, val(c - 1))
                    load_gate(c, j, 1)
                    load_unit(sp, c + (U_MERGE + KT + 2), w_slot[j])
            sp.wait_ge(s_flo, 2 * KT)
            for c in range(KT):
                if c:
                    sp.wait_ge(s_xfin, c)
                sp.dma_start(t_b[:], x_s[:, c, :]).then_inc(s_lx, 16)
                load_unit(sp, U_MERGE + 2 * KT + c + 2, w_slot[c % 2])

        ffn1 = Ffn(0, 0, 0, 0, (ra_hi, ra_lo), (rb_hi, rb_lo))
        ffn2 = Ffn(1, U_FFN2, M_FFN2, 2, (rb_hi, rb_lo), (ra_hi, ra_lo))

        block = e(nc.Block())

        @block.sync
        def _(sp):
            sp.dma_start(x[:, 0, :], x_t[:, 0, :]).then_inc(s_x[0], 16)
            sp.dma_start(col[:], cols).then_inc(s_const, 16)
            sp.dma_start(ident[:], ident_d).then_inc(s_const, 16)
            for i in range(1, KT):
                if i in (1, 4):
                    load_unit(sp, i // 4, i // 4, first=True)
                sp.dma_start(x[:, i, :], x_t[:, i, :]).then_inc(s_x[i], 16)
            load_units(sp, 2, FFN_UNITS)
            sp_proj(sp)
            sp_blocks(sp)
            sp_merge(sp)
            load_units(sp, U_FFN2 + 2, FFN_UNITS - 2)
            for half in range(2):
                c = slice(half * HALF, (half + 1) * HALF)
                for d in (0, 1, 2, KT - 2, 3, 4, KT - 1, 5):
                    if d < KT - 2:
                        sp.wait_ge(s_fin, half * (KT - 2) + d + 1)
                    else:
                        sp.wait_ge(s_fin_pool, 2 * half + d - (KT - 3))
                    sp.dma_start(out[:, d, c], x[:, d, c]).then_inc(s_out, 16)
            sp.wait_ge(s_out, 16 * 2 * KT)

        @block.tensor
        def _(pe):
            pe.wait_ge(s_const, 32)
            pe.wait_ge(s_ones, 1)
            pe_ffn(pe, ffn1)
            pe_proj(pe)
            pe_blocks(pe)
            pe_merge(pe)
            pe_ffn(pe, ffn2)
            pe_sums(pe, 3)
            pe_spread(pe, 3)

        @block.scalar
        def _(act):
            act.wait_ge(s_const, 32)
            for d in range(KT):
                act_norm_tile(act, 0, d, ra_hi, (s_x[d], 16), unit={0: 0, 4: 1}.get(d))
            act_ffn(act, ffn1, lambda act: act_ffn_tail(act, ffn1, ra_hi))
            act_proj(act)
            act_blocks(act)
            act_merge(act)
            act_ffn(act, ffn2, lambda act: act_ffn_tail(act, ffn2, None))
            act_root(act, 3)
            for d in range(KT - 2, KT):
                g = C_GAIN + 3 * KT + d
                nc.scalar.activation(x[:, d, :], x[:, d, :], ACT.Copy, scale=col[:, g:g + 1]).then_inc(s_gain, 1)
            for half in range(2):
                c = slice(half * HALF, (half + 1) * HALF)
                act.wait_ge(s_rbc, 4 + half)
                nc.scalar.copy(rstd_b[:, c], ps[3][:, c]).then_inc(s_rb, 1)

        @block.vector
        def _(dve):
            nc.vector.memset(ones[:], 1.0).then_inc(s_ones, 1)
            dve.wait_ge(s_const, 32)
            for d in range(KT):
                dve_norm_tile(dve, 0, d, ra_hi, ra_lo)
                if d in (0, 4):
                    split_lo(dve, d // 4, d // 4)
            dve_ffn(dve, ffn1, lambda dve: dve_ffn_tail(dve, ffn1, ra_hi, ra_lo))
            dve_proj(dve)
            dve_blocks(dve)
            dve_merge(dve)
            dve_ffn(dve, ffn2, lambda dve: dve_ffn_tail(dve, ffn2, None, None))
            dve_stats(dve, 3)
            for half in range(2):
                dve.wait_ge(s_rb, 4 + half)
                c = slice(half * HALF, (half + 1) * HALF)
                for d in range(KT - 2):
                    g = C_GAIN + 3 * KT + d
                    nc.vector.scalar_tensor_tensor(x[:, d, c], x[:, d, c], col[:, g:g + 1], rstd_b[:, c],
                                                   ALU.mult, ALU.mult).then_inc(s_fin, 1)

        @block.gpsimd
        def _(pool):
            pool_norm(pool, 0)
            pool_norm(pool, 1)
            pool.wait_ge(b["init"], 7)
            with pool.Fori(1, NB + 1) as reg:
                pool_hn(pool, Lin(reg))
            pool_norm(pool, 2)
            pool_norm(pool, 3)
            for half in range(2):
                c = slice(half * HALF, (half + 1) * HALF)
                for d in range(KT - 2, KT):
                    pool.wait_ge(s_rb, 4 + half)
                    pool.wait_ge(s_gain, d - (KT - 3))
                    nc.gpsimd.tensor_tensor(x[:, d, c], x[:, d, c], rstd_b[:, c], ALU.mult).then_inc(s_fin_pool, 1)


def tile_weights(w):
    return w.reshape(KT, P, w.shape[1] // P, P).transpose(2, 1, 0, 3).reshape(-1, P, D)


def tile_down(w):
    return w.reshape(PAIRS, 2, P, 2, HALF).transpose(0, 3, 2, 1, 4).reshape(-1, P, D)


def ffn_stream(gate, up, down):
    g, u, d = tile_weights(gate), tile_weights(up), tile_down(down)
    parts = [g[0:1], u[0:1], g[1:2], u[1:2]]
    for p in range(1, PAIRS):
        for j in range(2):
            f, h = 2 * p + j, 2 * (p - 1) + j
            parts += [g[f:f + 1], u[f:f + 1], d[h:h + 1]]
    return parts + [d[-2:]]


def projection_columns(a):
    w = a["w_in"][0]
    at = np.cumsum([0, D, 256, 256, 512, 512, D, D, MH, MH, D, D])
    q, k, v, qm, km, vm, om, i, f, ga, gm = [w[:, at[n]:at[n + 1]] for n in range(11)]
    gates = np.zeros((D, P), w.dtype)
    gates[:, 0:MH], gates[:, 32:32 + MH] = i, f
    turns = [t[:, c * P:(c + 1) * P] for c in range(MH) for t in (qm, km)]
    ends = [t[:, c * P:(c + 1) * P] for c in range(KT) for t in (ga, gm)]
    return np.concatenate([gates, q, k, v] + turns + [vm, om] + ends, axis=1)


def kernel(**inputs):
    import concourse.bacc as bacc
    from concourse.bass_utils import run_bass_kernel_spmd

    a = {k: np.asarray(v) for k, v in inputs.items()}
    w_stream = np.concatenate(
        ffn_stream(a["ffn1_w_gate"][0], a["ffn1_w_up"][0], a["ffn1_w_down"][0])
        + [tile_weights(projection_columns(a))]
        + [tile_weights(a[k][0]) for k in ("w_att", "w_mlstm", "w_out")]
        + ffn_stream(a["ffn2_w_gate"][0], a["ffn2_w_up"][0], a["ffn2_w_down"][0]))
    x_t = np.ascontiguousarray(a["x"][0].T.reshape(KT, P, S).transpose(1, 0, 2))

    def by_tile(v):
        return v.reshape(KT, P).T

    def on_heads(v):
        return np.concatenate([v, np.zeros(P - MH, v.dtype)])[:, None]

    conv = np.concatenate([a["conv_w"][0], a["conv_b"]], axis=0).reshape(5, 2, MH, P)
    cols = np.concatenate([by_tile(a["ffn1_norm"][0]), by_tile(a["mix_norm"][0]), by_tile(a["ffn2_norm"][0]),
                           by_tile(a["final_norm"]), np.full((P, 1), EPS, np.float32),
                           by_tile(a["head_norm"][0]), on_heads(a["b_i"][0]), on_heads(a["b_f"][0]),
                           conv.transpose(3, 2, 1, 0).reshape(P, 40)], axis=1)
    pos = np.arange(S, dtype=np.float32)
    freq = np.float32(10000.0) ** (-np.arange(HD // 2, dtype=np.float32) / np.float32(HD // 2))
    angle = (pos[None, :] * freq[:, None]).astype(np.float32)
    sin, cos = np.sin(angle), np.cos(angle)
    rope_cs = np.stack([np.tile(cos, (4, 1)), np.tile(np.concatenate([-sin, sin]), (2, 1))]).astype(np.float32)
    l, m = np.arange(P)[:, None], np.arange(P)[None, :]
    prev = np.where(m > l, 0.0, -BIG)
    cur = np.where(m <= l, 0.0, -BIG)
    masks = np.stack([np.concatenate([before, cur], axis=1)
                      for before in (np.full((P, P), -BIG), prev)], axis=1).astype(np.float32)
    mask_big = np.where(l > m, BIG, 0.0).astype(np.float32)
    sel_head = np.zeros((MH, MH, P), np.float32)
    for h in range(MH):
        sel_head[h, h] = 1.0
    sel_last = np.zeros((P, P), np.float32)
    sel_last[P - 1] = 1.0
    arrays = {"w_stream": w_stream, "x_t": x_t, "cols": np.ascontiguousarray(cols),
              "ident_d": np.eye(P, dtype=np.float32),
              "sinks": np.ascontiguousarray(np.broadcast_to(a["attn_sinks"], (P, HEADS))),
              "rope_cs": rope_cs, "masks": masks, "mask_big": mask_big, "sel_head": sel_head,
              "sel_last": sel_last}
    nc = bacc.Bacc("TRN2", target_bir_lowering=False, num_devices=1)
    args = [nc.dram_tensor(k, v.shape, F32, kind="ExternalInput").ap() for k, v in arrays.items()]
    args.append(nc.dram_tensor("out_t", (P, KT, S), F32, kind="ExternalOutput").ap())
    for name, shape in (("zs", (Z_TILES, P, S)), ("gs", (2 * KT, P, S)), ("att_s", (KT, P, P + S)),
                        ("mem_s", (KT, P, P + S)), ("x_s", (P, KT, S))):
        args.append(nc.dram_tensor(name, shape, F32, kind="Internal").ap())
    hybrid_layer(nc, *args)
    r = run_bass_kernel_spmd(nc, [arrays], core_ids=[0])
    out_t = r.results[0]["out_t"]
    return np.ascontiguousarray(out_t.transpose(1, 0, 2).reshape(D, S).T)[None]
```
